# Optimizing a Trainium2 kernel written in Bass

```python
import jax
import jax.numpy as jnp
from jax import lax
import numpy as np

D_MODEL = 2048
BATCH = 1
SEQ = 256
DEPTH = 1

HEAD_DIM = 64
MIX_WIDTH = D_MODEL
ATTN_WIDTH = MIX_WIDTH // 2
RWKV_WIDTH = MIX_WIDTH - ATTN_WIDTH
ATTN_HEADS = ATTN_WIDTH // HEAD_DIM
RWKV_HEADS = RWKV_WIDTH // HEAD_DIM
WINDOWS = (128, 512, 2048)
DILATIONS = (1, 4, 16)
ROT_DIM = HEAD_DIM // 4
ROPE_THETA = 500000.0
DECAY_LORA = 64
ICLR_LORA = 64
GATE_LORA = 160
RWKV_COLS = 3 * RWKV_WIDTH + DECAY_LORA + ICLR_LORA + GATE_LORA
IN_COLS = 3 * ATTN_WIDTH + RWKV_COLS
FFN_DIM = -(-(8 * D_MODEL) // (3 * 256)) * 256
RMS_EPS = 1e-6
GN_EPS = HEAD_DIM * 1e-5

kernel_name = 'hymba_dilated_rwkv7_adaln_layer'

def _rmsnorm(x, g):
    xf = x.astype(jnp.float32)
    y = xf * lax.rsqrt(jnp.mean(xf * xf, axis=-1, keepdims=True) + RMS_EPS)
    return (y * g.astype(jnp.float32)).astype(x.dtype)

def _partial_rope(t, positions):
    inv = ROPE_THETA ** (-jnp.arange(0, ROT_DIM, 2, dtype=jnp.float32) / ROT_DIM)
    ang = positions.astype(jnp.float32)[..., None] * inv
    cos = jnp.cos(ang)[:, :, None, :]
    sin = jnp.sin(ang)[:, :, None, :]
    half = ROT_DIM // 2
    r1 = t[..., :half].astype(jnp.float32)
    r2 = t[..., half:ROT_DIM].astype(jnp.float32)
    rot = jnp.concatenate([r1 * cos - r2 * sin, r2 * cos + r1 * sin], axis=-1).astype(t.dtype)
    return jnp.concatenate([rot, t[..., ROT_DIM:]], axis=-1)

def _dilated_branch(q, k, v, window, dilation):
    b, s, h, dh = q.shape
    blk = window // dilation
    unit = blk * dilation
    s_pad = -(-s // unit) * unit
    n_sub = s_pad // dilation
    nb = n_sub // blk

    def to_blocks(t):
        t = jnp.pad(t, ((0, 0), (0, s_pad - s), (0, 0), (0, 0)))
        t = t.reshape(b, n_sub, dilation, h, dh).transpose(0, 3, 2, 1, 4)
        return t.reshape(b, h, dilation, nb, blk, dh)

    def with_prev(t):
        prev = jnp.pad(t, ((0, 0), (0, 0), (0, 0), (1, 0), (0, 0), (0, 0)))[:, :, :, :-1]
        return jnp.concatenate([prev, t], axis=4)

    qb = to_blocks(q)
    kw = with_prev(to_blocks(k))
    vw = with_prev(to_blocks(v))
    scores = jnp.einsum('bhrnqd,bhrnkd->bhrnqk', qb, kw,
                        preferred_element_type=jnp.float32) * (dh ** -0.5)
    qi = jnp.arange(blk)[:, None]
    kj = jnp.arange(2 * blk)[None, :]
    steps = blk + qi - kj
    band = (steps >= 0) & (steps <= blk)
    valid = band[None] & ((jnp.arange(nb)[:, None, None] > 0) | (kj[None] >= blk))
    scores = jnp.where(valid, scores, -jnp.inf)
    m = jnp.max(scores, axis=-1, keepdims=True)
    p = jnp.exp(scores - m)
    l = jnp.sum(p, axis=-1, keepdims=True)
    o = jnp.einsum('bhrnqk,bhrnkd->bhrnqd', p, vw.astype(jnp.float32)) / l
    lse = (m + jnp.log(l))[..., 0]
    o = o.reshape(b, h, dilation, n_sub, dh).transpose(0, 3, 2, 1, 4).reshape(b, s_pad, h, dh)[:, :s]
    lse = lse.reshape(b, h, dilation, n_sub).transpose(0, 3, 2, 1).reshape(b, s_pad, h)[:, :s]
    return o, lse

def _dilated_mixture(q, k, v):
    outs, lses = zip(*[_dilated_branch(q, k, v, w, d) for w, d in zip(WINDOWS, DILATIONS)])
    wts = jax.nn.softmax(jnp.stack(lses, axis=0), axis=0)
    o = jnp.sum(wts[..., None] * jnp.stack(outs, axis=0), axis=0)
    return o.astype(q.dtype)

def _rwkv7(y, mu_shift, w0, w_decay_up, a0, w_iclr_up, w_gate_up, k_k, k_a, r_k, gn_g, gn_b):
    dt = y.dtype
    b, s, _ = y.shape
    yf = y.astype(jnp.float32)
    prev = jnp.pad(yf, ((0, 0), (1, 0), (0, 0)))[:, :-1]
    yf = yf + (prev - yf) * mu_shift
    c0 = RWKV_WIDTH
    r = yf[..., :c0]
    k = yf[..., c0:2 * c0]
    v = yf[..., 2 * c0:3 * c0]
    wl = yf[..., 3 * c0:3 * c0 + DECAY_LORA]
    al = yf[..., 3 * c0 + DECAY_LORA:3 * c0 + DECAY_LORA + ICLR_LORA]
    gl = yf[..., 3 * c0 + DECAY_LORA + ICLR_LORA:]
    w = -jax.nn.softplus(-(w0 + jnp.tanh(wl) @ w_decay_up)) - 0.5
    decay = jnp.exp(-jnp.exp(w))
    a = jax.nn.sigmoid(a0 + al @ w_iclr_up)
    g = jax.nn.sigmoid(gl) @ w_gate_up
    hd = lambda t: t.reshape(b, s, RWKV_HEADS, HEAD_DIM)
    kk = hd(k * k_k)
    kk = kk / jnp.maximum(jnp.sqrt(jnp.sum(kk * kk, axis=-1, keepdims=True)), 1e-12)
    k = k * (1.0 + (a - 1.0) * k_a)
    r_h, w_h, k_h, v_h, a_h = hd(r), hd(decay), hd(k), hd(v), hd(a)

    def step(state, inp):
        r_t, w_t, k_t, v_t, kk_t, a_t = inp
        sa = jnp.einsum('bhvk,bhk->bhv', state, -kk_t)
        state = (state * w_t[..., None, :]
                 + sa[..., :, None] * (kk_t * a_t)[..., None, :]
                 + v_t[..., :, None] * k_t[..., None, :])
        return state, jnp.einsum('bhvk,bhk->bhv', state, r_t)

    xs = tuple(jnp.moveaxis(t, 1, 0) for t in (r_h, w_h, k_h, v_h, kk, a_h))
    state0 = jnp.zeros((b, RWKV_HEADS, HEAD_DIM, HEAD_DIM), jnp.float32)
    _, outs = lax.scan(step, state0, xs)
    o = jnp.moveaxis(outs, 0, 1)
    mean = jnp.mean(o, axis=-1, keepdims=True)
    var = jnp.mean(jnp.square(o - mean), axis=-1, keepdims=True)
    o = ((o - mean) * lax.rsqrt(var + GN_EPS)).reshape(b, s, RWKV_WIDTH) * gn_g + gn_b
    bonus = jnp.sum(r_h * k_h * r_k, axis=-1, keepdims=True) * v_h
    o = (o + bonus.reshape(b, s, RWKV_WIDTH)) * g
    return o.astype(dt)

def _swiglu(h, w_gate, w_up, w_down):
    return (jax.nn.silu(h @ w_gate) * (h @ w_up)) @ w_down

def setup_inputs(seed: int = 0) -> dict:
    key = jax.random.key(seed)
    ks = jax.random.split(key, 26)
    f32 = jnp.float32
    L = DEPTH

    def nrm(k, shape, scale):
        return jax.random.normal(k, shape, f32) * scale

    return {
        'x': nrm(ks[0], (BATCH, SEQ, D_MODEL), 1.0),
        'c': nrm(ks[1], (BATCH, D_MODEL), 1.0),
        'positions': jnp.broadcast_to(jnp.arange(SEQ, dtype=jnp.int32), (BATCH, SEQ)),
        'w_ada': nrm(ks[2], (L, D_MODEL, 6 * D_MODEL), 0.5 * D_MODEL ** -0.5),
        'b_ada': nrm(ks[3], (L, 6 * D_MODEL), 0.01),
        'norm1_g': 1.0 + nrm(ks[4], (L, D_MODEL), 0.05),
        'norm2_g': 1.0 + nrm(ks[5], (L, D_MODEL), 0.05),
        'normf_g': 1.0 + nrm(ks[6], (D_MODEL,), 0.05),
        'w_in': nrm(ks[7], (L, D_MODEL, IN_COLS), D_MODEL ** -0.5),
        'w_out': nrm(ks[8], (L, MIX_WIDTH, D_MODEL), MIX_WIDTH ** -0.5),
        'mu_shift': jax.random.uniform(ks[9], (L, RWKV_COLS), f32, 0.0, 1.0),
        'w0': jax.random.uniform(ks[10], (L, RWKV_WIDTH), f32, -6.0, 1.0),
        'w_decay_up': nrm(ks[11], (L, DECAY_LORA, RWKV_WIDTH), 0.5 * DECAY_LORA ** -0.5),
        'a0': nrm(ks[12], (L, RWKV_WIDTH), 0.1),
        'w_iclr_up': nrm(ks[13], (L, ICLR_LORA, RWKV_WIDTH), 0.5 * ICLR_LORA ** -0.5),
        'w_gate_up': nrm(ks[14], (L, GATE_LORA, RWKV_WIDTH), GATE_LORA ** -0.5),
        'k_k': 0.85 + nrm(ks[15], (L, RWKV_WIDTH), 0.05),
        'k_a': 1.0 + nrm(ks[16], (L, RWKV_WIDTH), 0.05),
        'r_k': nrm(ks[17], (L, RWKV_HEADS, HEAD_DIM), 0.1),
        'gn_g': 1.0 + nrm(ks[18], (L, RWKV_WIDTH), 0.05),
        'gn_b': nrm(ks[19], (L, RWKV_WIDTH), 0.01),
        'w_ffn_gate': nrm(ks[20], (L, D_MODEL, FFN_DIM), D_MODEL ** -0.5),
        'w_ffn_up': nrm(ks[21], (L, D_MODEL, FFN_DIM), D_MODEL ** -0.5),
        'w_ffn_down': nrm(ks[22], (L, FFN_DIM, D_MODEL), FFN_DIM ** -0.5),
    }

def reference(x, c, positions, w_ada, b_ada, norm1_g, norm2_g, normf_g, w_in, w_out,
              mu_shift, w0, w_decay_up, a0, w_iclr_up, w_gate_up, k_k, k_a, r_k,
              gn_g, gn_b, w_ffn_gate, w_ffn_up, w_ffn_down):
    b, s, _ = x.shape
    for i in range(DEPTH):
        ada = (jax.nn.silu(c) @ w_ada[i] + b_ada[i])[:, None, :]
        sh1, sc1, gt1, sh2, sc2, gt2 = jnp.split(ada, 6, axis=-1)
        h = _rmsnorm(x, norm1_g[i]) * (1.0 + sc1) + sh1
        proj = h @ w_in[i]
        q = proj[..., :ATTN_WIDTH].reshape(b, s, ATTN_HEADS, HEAD_DIM)
        k = proj[..., ATTN_WIDTH:2 * ATTN_WIDTH].reshape(b, s, ATTN_HEADS, HEAD_DIM)
        v = proj[..., 2 * ATTN_WIDTH:3 * ATTN_WIDTH].reshape(b, s, ATTN_HEADS, HEAD_DIM)
        q = _partial_rope(q, positions)
        k = _partial_rope(k, positions)
        attn = _dilated_mixture(q, k, v).reshape(b, s, ATTN_WIDTH)
        rwkv = _rwkv7(proj[..., 3 * ATTN_WIDTH:], mu_shift[i], w0[i], w_decay_up[i], a0[i],
                      w_iclr_up[i], w_gate_up[i], k_k[i], k_a[i], r_k[i], gn_g[i], gn_b[i])
        mix = jnp.concatenate([attn, rwkv], axis=-1) @ w_out[i]
        x = x + gt1 * mix
        h2 = _rmsnorm(x, norm2_g[i]) * (1.0 + sc2) + sh2
        x = x + gt2 * _swiglu(h2, w_ffn_gate[i], w_ffn_up[i], w_ffn_down[i])
    return _rmsnorm(x, normf_g)


_drawn_inputs = setup_inputs


def setup_inputs(seed=0):
    import zlib

    import numpy as np

    out = dict(_drawn_inputs(seed))
    spreads = {}
    factors = {'b_ada': 5.32,
     'norm1_g': 4.994,
     'norm2_g': 21.949,
     'w_decay_up': 30.073,
     'a0': 8.0,
     'k_k': 62.312,
     'k_a': 6.989,
     'gn_g': 64.0,
     'gn_b': 64.0,
     'w0': 3.114}
    for name, (base, spread) in spreads.items():
        noise = np.random.default_rng([zlib.crc32(name.encode()), seed]).standard_normal(out[name].shape)
        drawn = base * np.exp(spread * noise) if base else spread * noise
        out[name] = jnp.asarray(drawn.astype(out[name].dtype))
    for name, factor in factors.items():
        out[name] = (out[name] * factor).astype(out[name].dtype)
    return out
```

```python
import math
from contextlib import ExitStack

import numpy as np

import concourse.bass as bass
from concourse import mybir

F32 = mybir.dt.float32
F32R = mybir.dt.float32r
I32 = mybir.dt.int32
ALU = mybir.AluOpType
ACT = mybir.ActivationFunctionType
AX = mybir.AxisListType.X

P = 128
T = 256
NT = T // P
D = 2048
KT = D // P
HD = 64
HEADS = 16
PAIRS = HEADS // 2
AW = 1024
IN_COLS = 3 * AW + 3 * AW + 288
FFN = 5632
FK = FFN // P
CW = 512
UK = 2
RING = 4
LAG = 3
UPG = KT // UK
WIN_G = 13
N_OUT0 = WIN_G * UPG
OUT_G = D // CW
N_GU0 = N_OUT0 + OUT_G * UPG
GU_G = FFN // CW
N_DOWN0 = N_GU0 + 2 * GU_G * UPG
DOWN_U = FK // UK
N_UNITS = N_DOWN0 + OUT_G * DOWN_U
LORA_W = 288
RMS_EPS = 1e-6
GN_EPS = HD * 1e-5
LEVELS = 6
SQ = math.exp(-0.5)

V_C, V_N1, V_N2, V_W0, V_A0, V_KK, V_KA, V_RK, V_GG, V_GB = 0, 16, 32, 48, 56, 64, 72, 80, 88, 96
V_B = 104
V_MU = 200
NVEC = 227

C_ID, C_ONE, C_BLK, C_PERM, C_LC, C_LEV, C_SI, C_M0, C_M0T, C_RES, C_INV = (
    0, 128, 256, 384, 512, 896, 896 + 768, 1920, 2048, 2176, 2432)
NCONST = 2433


def constants():
    c = np.zeros((P, NCONST), np.float32)
    i = np.arange(P)
    c[:, C_ID:C_ID + P] = np.eye(P)
    c[:, C_ONE:C_ONE + P] = 1.0
    c[:, C_BLK:C_BLK + P] = (i[:, None] // HD == i[None, :] // HD)
    for h in (0, HD):
        for d in range(8):
            c[h + d + 8, C_PERM + h + d] = -1.0
            c[h + d, C_PERM + h + d + 8] = 1.0
    t = np.arange(T)[:, None]
    j = np.arange(T)[None, :]
    count = (((t - j) >= 0) & ((t - j) <= 128)).astype(np.float64)
    for dil in (4, 16):
        count += (j <= t) & ((t - j) % dil == 0) & ((t - j) <= 128 * dil)
    lc = np.where(count > 0, np.log(np.maximum(count, 1)), -1e30).astype(np.float32)
    c[:, C_LC:C_LC + P] = lc[:P, :P]
    c[:, C_LC + P:C_LC + 3 * P] = lc[P:, :]
    s, u = i[:, None], i[None, :]
    for lev in range(1, LEVELS + 1):
        b = 2 ** lev
        c[:, C_LEV + P * (lev - 1):C_LEV + P * lev] = (u // b == s // b + 1) & (s // b % 2 == 0)
    c[:, C_SI:C_SI + P] = s < u
    c[:, C_SI + P:C_SI + 2 * P] = s <= u
    c[:, C_M0:C_M0 + P] = (s == u + 1) & (u % 2 == 0)
    c[:, C_M0T:C_M0T + P] = (u == s + 1) & (s % 2 == 0)
    c[:, C_RES:C_RES + T] = (np.arange(T) % 64 != 0)
    rot = 16
    inv = (np.float32(500000.0) ** (-np.arange(0, rot, 2, dtype=np.float32) / np.float32(rot))).astype(np.float32)
    for h in (0, HD):
        for d in range(rot):
            c[h + d, C_INV] = inv[d % 8]
    return c


def slot_of(n):
    return n % RING


def build(nc, a):
    ctx = ExitStack()
    with ctx:
        def sem(name):
            return ctx.enter_context(nc.semaphore(name))

        top = [nc.sbuf_base + 31 - (nc.sbuf_base + 31) % 32]

        def fixed(name, shape, dt=F32):
            size = 4 * int(np.prod(shape[1:]))
            t = nc.alloc_sbuf_tensor_at(name, shape, dt, offset=top[0])
            top[0] += -(-size // 32) * 32
            return t

        raw = fixed("raw", [P, RING, UK, CW])
        w_hi = fixed("w_hi", [P, RING, UK, CW], F32R)
        w_lo = fixed("w_lo", [P, RING, UK, CW], F32R)
        idone = fixed("idone", [P, 2 * P])
        vec = fixed("vec", [P, NVEC])
        ada_t = fixed("ada_t", [P, 96])
        scale1 = fixed("scale1", [P, KT])
        scale2 = fixed("scale2", [P, KT])
        silu_c = fixed("silu_c", [P, KT])
        sig_c = fixed("sig_c", [P, KT])
        acc = fixed("acc", [P, 2, CW])
        stat = fixed("stat", [P, 32])
        base = top[0]
        end = nc.sbuf_usable_end

        def at(name, offset, shape, dt=F32):
            size = 4 * int(np.prod(shape[1:]))
            assert base + offset + size <= end, (name, base, offset, size, end)
            return nc.alloc_sbuf_tensor_at(name, shape, dt, offset=base + offset)

        ident = idone[:, 0:P]
        ones = idone[:, P:2 * P]

        KB = 1024
        h_hi = at("h_hi", 0, [P, KT, T], F32R)
        h_lo = at("h_lo", 16 * KB, [P, KT, T], F32R)
        o = 32 * KB
        cst = at("cst", o, [P, NCONST - 256]); o += 4 * NCONST - 1024 + 28
        o = -(-o // 32) * 32
        cosT = at("cosT", o, [P, T]); o += KB
        sinT = at("sinT", o, [P, T]); o += KB
        ada_raw = at("ada_raw", o, [P, RING, UK, CW]); o += 16 * KB
        w_di = at("w_di", o, [P, AW]); o += 4 * KB
        w_g = at("w_g", o, [P, AW]); o += 4 * KB
        w_g2 = at("w_g2", o, [P, AW]); o += 4 * KB
        rkv_off = o
        rkv = at("rkv", o, [P, 24, T]); o += 24 * KB
        lora = at("lora", o, [P, 3, T]); o += 3 * KB
        mixa_hi = at("mixa_hi", o, [P, 8, T], F32R); o += 8 * KB
        mixa_lo = at("mixa_lo", o, [P, 8, T], F32R); o += 8 * KB
        qkv_off = o
        qk = at("qk", o, [P, 16, T]); o += 16 * KB
        v_tok = at("v_tok", o, [P, NT, AW]); o += 8 * KB
        tmp_off = o
        ybuf = at("ybuf", o, [P, 4, T + 1]); o += 4 * 4 * (T + 1)
        o = -(-o // 32) * 32
        qraw = at("qraw", o, [P, 4, T])
        t1 = at("t1", o + 4 * KB, [P, 2, T])
        prob = at("prob", o, [P, 3, P]); o += 1536
        prob_t = at("prob_t", o, [P, 3, P]); o += 1536
        x_in = at("x_in", rkv_off, [P, NT, D])
        xn_t = at("xn_t", qkv_off, [P, KT, T])
        vrows = at("vrows", tmp_off, [P, 3, P])
        pos_i = at("pos_i", rkv_off + 16 * KB, [P, T], I32)
        ang = at("ang", rkv_off + 17 * KB, [P, T])
        turns = at("turns", rkv_off + 18 * KB, [P, T])

        o = 0
        op = at("op", o, [P, 4, T]); o += 4 * KB
        br = at("br", o, [P, 4, 2 * P]); o += 4 * KB
        kr = at("kr", o, [P, 4, 2 * P]); o += 4 * KB
        xm = at("xm", o, [P, 4, P]); o += 2 * KB
        xt = at("xt", o, [P, 4, P]); o += 2 * KB
        y1 = at("y1", o, [P, 4, P]); o += 2 * KB
        nt = at("nt", o, [P, 2, 4, P]); o += 4 * KB
        tv = at("tv", o, [P, 4, P]); o += 2 * KB
        us = at("us", o, [P, 2, HD]); o += 512
        sa = at("sa", o, [P, 2, 2, HD]); o += KB
        s0 = at("s0", o, [P, HD]); o += 256
        o_t = at("o_t", o, [P, T]); o += KB
        e3 = at("e3", o, [P, 3, T]); o += 3 * KB
        assert o <= 32 * KB
        rn = at("rn", 0, [P, PAIRS, T])
        lw = at("lw", qkv_off, [P, PAIRS, T])
        ab = at("ab", qkv_off + 8 * KB, [P, PAIRS, T])
        kk = at("kk", qkv_off + 16 * KB, [P, PAIRS, T])
        cen = at("cen", qkv_off + 24 * KB, [P, 2, T])
        sq = at("sq", qkv_off + 26 * KB, [P, T])
        refc = at("refc", qkv_off + 27 * KB, [P, 4])
        mixr_hi = at("mixr_hi", 0, [P, 8, T], F32R)
        mixr_lo = at("mixr_lo", 8 * KB, [P, 8, T], F32R)

        act_hi = at("act_hi", 32 * KB, [P, FK, T], F32R)
        act_lo = at("act_lo", 32 * KB + 44 * KB, [P, FK, T], F32R)
        x1 = at("x1", 120 * KB, [P, NT, D])
        sg = at("sg", 136 * KB, [P, 2, 4, T])
        xn2 = at("xn2", rkv_off, [P, NT, D])
        gtb = at("gtb", 136 * KB, [P, CW])
        diag = at("diag", 138 * KB, [P, CW])
        upd = at("upd", 140 * KB, [P, CW])
        h2f = at("h2f", 136 * KB, [P, 2, 4, T])
        ada_raw2 = at("ada_raw2", 0, [P, RING, UK, CW])
        nf_b = at("nf_b", 16 * KB, [P, D])
        gtb2 = at("gtb2", 24 * KB, [P, CW])
        diag2 = at("diag2", 26 * KB, [P, CW])
        upd2 = at("upd2", 28 * KB, [P, CW])
        sqj = at("sqj", 30 * KB, [P, CW])
        sqj1 = at("sqj1", 142 * KB, [P, CW])

        ps = [ctx.enter_context(nc.psum_tensor(f"bank{b}", [P, 512], F32)) for b in range(8)]
        FIN = 5

        def ck(col, n=P):
            return cst[:, col - 256:col - 256 + n]

        def v1(col):
            return vec[:, col:col + 1]

        def over4(x):
            return x.unsqueeze(1).broadcast_to([P, 4, x.shape[1]])

        s_cst, s_rows, s_x, s_pos, s_small, s_v0 = map(sem, ("s_cst", "s_rows", "s_x", "s_pos", "s_small", "s_v0"))
        s_raw = [sem(f"s_raw{i}") for i in range(RING)]
        s_hi, s_lo, s_used = sem("s_hi"), sem("s_lo"), sem("s_used")
        s_ada = [sem(f"s_ada{i}") for i in range(RING)]
        s_adaused, s_fin, s_col = map(sem, ("s_adaused", "s_fin", "s_col"))
        s_vt, s_vec, s_sigc, s_siluc = map(sem, ("s_vt", "s_vec", "s_sigc", "s_siluc"))
        s_ss, s_ms, s_rt, s_xn, s_xt, s_xnt = map(sem, ("s_ss", "s_ms", "s_rt", "s_xn", "s_xt", "s_xnt"))
        s_hf, s_hhi, s_hlo = map(sem, ("s_hf", "s_hhi", "s_hlo"))
        s_trig, s_sin = sem("s_trig"), sem("s_sin")
        s_evac, s_perm, s_rope = sem("s_evac"), sem("s_perm"), sem("s_rope")
        s_shift, s_lora = sem("s_shift"), sem("s_lora")
        s_score, s_masked, s_exp, s_prob, s_pt, s_ptc, s_o, s_ohi, s_mixa = map(
            sem, ("s_score", "s_masked", "s_exp", "s_prob", "s_pt", "s_ptc", "s_o", "s_ohi", "s_mixa"))
        s_zw, s_sigs, s_kkr, s_sqk, s_ssq, s_rnr, s_rns, s_pre, s_lwr = map(
            sem, ("s_zw", "s_sigs", "s_kkr", "s_sqk", "s_ssq", "s_rnr", "s_rns", "s_pre", "s_lwr"))
        s_cen, s_e3, s_op, s_gram, s_tvc, s_gramc, s_tv, s_nt, s_y, s_y1, s_xx, s_xc = map(
            sem, ("s_cen", "s_e3", "s_op", "s_gram", "s_tvc", "s_gramc", "s_tv", "s_nt", "s_y", "s_y1",
                  "s_xx", "s_xc"))
        s_u, s_uc, s_sa, s_sac, s_st, s_stc, s_ot, s_otc = map(
            sem, ("s_u", "s_uc", "s_sa", "s_sac", "s_st", "s_stc", "s_ot", "s_otc"))
        s_mean, s_dev, s_dsq, s_bon, s_var, s_bonus, s_vrt, s_g, s_mixf, s_mrhi, s_mixr = map(
            sem, ("s_mean", "s_dev", "s_dsq", "s_bon", "s_var", "s_bonus", "s_vrt", "s_g", "s_mixf",
                  "s_mrhi", "s_mixr"))
        s_x1in, s_diag, s_gt, s_gtb, s_x1, s_ssp, s_ms2, s_rt2, s_xn2, s_x2t, s_h2f, s_h2hi, s_h2lo = map(
            sem, ("s_x1in", "s_diag", "s_gt", "s_gtb", "s_x1", "s_ssp", "s_ms2", "s_rt2", "s_xn2", "s_x2t",
                  "s_h2f", "s_h2hi", "s_h2lo"))
        s_silu, s_prod, s_ahi, s_alo, s_nf, s_fs, s_out = map(
            sem, ("s_silu", "s_prod", "s_ahi", "s_alo", "s_nf", "s_fs", "s_out"))
        s_dch = sem("s_dch")

        w_in = a["w_in"].rearrange("l (k p) n -> p (l k) n", p=P)
        w_out = a["w_out"].rearrange("l (k p) n -> p (l k) n", p=P)
        w_gate = a["w_ffn_gate"].rearrange("l (k p) n -> p (l k) n", p=P)
        w_up = a["w_ffn_up"].rearrange("l (k p) n -> p (l k) n", p=P)
        w_down = a["w_ffn_down"].rearrange("l (k p) n -> p (l k) n", p=P)
        w_ada = a["w_ada"].rearrange("l (k p) n -> p (l k) n", p=P)
        x_dram = a["x"].rearrange("b (t p) d -> p (b t) d", p=P)
        out_dram = a["out"].rearrange("b (t p) d -> p (b t) d", p=P)

        ada_order = [g for j in range(4) for g in (j, 4 + j)] + list(range(8, 24))
        INIT_ADA = 8 * UPG
        END_ADA1 = 20 * UPG

        block = ctx.enter_context(nc.Block())

        @block.sync
        def _(sp):
            sp.dma_start(idone[:], a["const"][:, 0:256]).then_inc(s_cst, 16)
            rows = 0
            for name, n in (("c", 16), ("norm1_g", 16), ("norm2_g", 16), ("w0", 8), ("a0", 8), ("k_k", 8),
                            ("k_a", 8), ("r_k", 8), ("gn_g", 8), ("gn_b", 8)):
                flat = a[name].rearrange("a b c -> (a b c)") if name == "r_k" else a[name].rearrange("a b -> (a b)")
                sp.dma_start(vrows[rows:rows + n, 0, :], flat.rearrange("(r q) -> r q", q=P)).then_inc(s_rows, 16)
                rows += n
            sp.dma_start(vrows[0:96, 1, :], a["b_ada"].rearrange("l (r q) -> (l r) q", q=P)).then_inc(s_rows, 16)
            mu = a["mu_shift"].rearrange("a b -> (a b)")
            sp.dma_start(vrows[0:26, 2, :], mu[0:26 * P].rearrange("(r q) -> r q", q=P)).then_inc(s_rows, 16)
            sp.dma_start(vrows[26:27, 2, :], mu[3232:3360].rearrange("(r q) -> r q", q=P)).then_inc(s_rows, 16)
            for t in range(NT):
                sp.dma_start(x_in[:, t, :], x_dram[:, t, :]).then_inc(s_x, 16)
            sp.dma_start(pos_i[:], a["positions"].partition_broadcast(P).rearrange("p a b -> p (a b)")).then_inc(s_pos, 16)
            sp.dma_start(cst[:], a["const"][:, 256:NCONST]).then_inc(s_small, 16)
            sp.dma_start(w_di[0:64, :], a["w_decay_up"][0]).then_inc(s_small, 16)
            sp.dma_start(w_di[64:128, :], a["w_iclr_up"][0]).then_inc(s_small, 16)
            sp.dma_start(w_g[:], a["w_gate_up"][0, 0:128, :]).then_inc(s_small, 16)
            sp.dma_start(w_g2[96:128, :], a["w_gate_up"][0, 128:160, :]).then_inc(s_small, 16)

            for ku in range(UPG):
                if ku >= RING:
                    sp.wait_ge(s_lo, ku - RING + 1)
                sp.dma_start(raw[:, slot_of(ku)], w_in[:, UK * ku:UK * ku + UK, 0:CW]).then_inc(s_raw[slot_of(ku)], 16)
            with sp.Fori(1, WIN_G - 1) as g:
                for ku in range(UPG):
                    sp.wait_ge(s_lo, g * UPG + (ku - RING + 1))
                    sp.dma_start(raw[:, slot_of(ku)],
                                 w_in[:, UK * ku:UK * ku + UK, bass.ts(g, CW)]).then_inc(s_raw[slot_of(ku)], 16)
            for ku in range(UPG):
                sp.wait_ge(s_lo, (WIN_G - 1) * UPG + ku - RING + 1)
                sp.dma_start(raw[:, slot_of(ku), :, 0:LORA_W],
                             w_in[:, UK * ku:UK * ku + UK, 6 * AW:6 * AW + LORA_W]).then_inc(s_raw[slot_of(ku)], 16)
            with sp.Fori(0, OUT_G) as g:
                for ku in range(UPG):
                    sp.wait_ge(s_lo, g * UPG + (N_OUT0 + ku - RING + 1))
                    sp.dma_start(raw[:, slot_of(ku)],
                                 w_out[:, UK * ku:UK * ku + UK, bass.ts(g, CW)]).then_inc(s_raw[slot_of(ku)], 16)
            with sp.Fori(0, GU_G) as g:
                for m, w in enumerate((w_gate, w_up)):
                    for ku in range(UPG):
                        sp.wait_ge(s_lo, g * (2 * UPG) + (N_GU0 + m * UPG + ku - RING + 1))
                        sp.dma_start(raw[:, slot_of(ku)],
                                     w[:, UK * ku:UK * ku + UK, bass.ts(g, CW)]).then_inc(s_raw[slot_of(ku)], 16)
            with sp.Fori(0, OUT_G // 2) as g:
                for m in range(2):
                    for ku in range(DOWN_U):
                        j = m * DOWN_U + ku
                        sp.wait_ge(s_lo, g * (2 * DOWN_U) + (N_DOWN0 + j - RING + 1))
                        sp.dma_start(raw[:, slot_of(j)],
                                     w_down[:, UK * ku:UK * ku + UK, bass.ds(g * (2 * CW) + m * CW, CW)]
                                     ).then_inc(s_raw[slot_of(j)], 16)
            for t in range(NT):
                sp.wait_ge(s_fs, t + 1)
                sp.dma_start(out_dram[:, t, :], x1[:, t, :]).then_inc(s_out, 16)
            sp.wait_ge(s_out, 16 * NT)

        @block.gpsimd
        def _(pool):
            for u in range(INIT_ADA):
                g, ku = ada_order[u // UPG], u % UPG
                if u >= RING:
                    pool.wait_ge(s_adaused, u - RING + 1)
                pool.dma_start(ada_raw[:, u % RING],
                               w_ada[:, UK * ku:UK * ku + UK, g * CW:(g + 1) * CW]).then_inc(s_ada[u % RING], 16)
            def ada_group(g):
                for ku in range(UPG):
                    pool.wait_ge(s_adaused, g * UPG + (ku - RING + 1))
                    pool.dma_start(ada_raw[:, ku % RING],
                                   w_ada[:, UK * ku:UK * ku + UK, bass.ds(g * CW, CW)]
                                   ).then_inc(s_ada[ku % RING], 16)

            with pool.Fori(8, 15) as g:
                ada_group(g)

            def level_mask(hp, lev):
                i = hp * LEVELS + lev
                if i >= 2:
                    pool.wait_ge(s_y, i - 1)
                nc.gpsimd.tensor_tensor(nt[:, i % 2], br[:, :, 0:P], over4(ck(C_LEV + P * lev)),
                                        ALU.mult).then_inc(s_nt, 1)

            pool.wait_ge(s_small, 80)
            for hp in range(PAIRS):
                pool.wait_ge(s_gramc, 3 * hp + 2)
                for lev in range(LEVELS):
                    level_mask(hp, lev)

            with pool.Fori(15, 20) as g:
                ada_group(g)
            pool.wait_ge(s_used, N_DOWN0)
            with pool.Fori(0, 4) as g:
                for ku in range(UPG):
                    pool.wait_ge(s_adaused, g * UPG + (END_ADA1 + ku - RING + 1))
                    pool.dma_start(ada_raw2[:, ku % RING],
                                   w_ada[:, UK * ku:UK * ku + UK, bass.ds(g * CW + 20 * CW, CW)]
                                   ).then_inc(s_ada[ku % RING], 16)
            pool.dma_start(nf_b[:], a["normf_g"].partition_broadcast(P)).then_inc(s_nf, 16)

        @block.scalar
        def _(act):
            def round_unit(n, width=CW):
                act.wait_ge(s_raw[slot_of(n)], 16 * (n // RING + 1))
                if n >= RING:
                    act.wait_ge(s_used, n - RING + 1)
                nc.scalar.activation(w_hi[:, slot_of(n), :, 0:width], raw[:, slot_of(n), :, 0:width],
                                     ACT.Copy).then_inc(s_hi, 1)

            act.wait_ge(s_vt, 1)
            nc.scalar.activation(vec[:], ps[4][:, 0:NVEC], ACT.Copy).then_inc(s_vec, 1)
            act.wait_ge(s_vec, 1)
            nc.scalar.activation(sig_c[:], vec[:, V_C:V_C + KT], ACT.Sigmoid).then_inc(s_sigc, 1)
            for t in range(NT):
                act.wait_ge(s_x, 16 * NT)
                nc.scalar.activation(xn_t[:, 8 * t:8 * t + 8, :].rearrange("p k t -> p (k t)"), x_in[:, t, :], ACT.Square,
                                     accum_out=stat[:, t:t + 1]).then_inc(s_ss, 1)
            act.wait_ge(s_ms, 1)
            nc.scalar.activation(stat[:, 4:6], stat[:, 2:4], ACT.Sqrt).then_inc(s_rt, 1)
            for b in range(8):
                act.wait_ge(s_xt, b + 1)
                nc.scalar.activation(xn_t[:, 2 * b:2 * b + 2, :], ps[b][:, :].rearrange("p (k t) -> p k t", k=2),
                                     ACT.Copy).then_inc(s_xnt, 1)
            act.wait_ge(s_trig, 1)
            nc.scalar.activation(sinT[:], ang[:], ACT.Sin)
            nc.scalar.activation(cosT[:], turns[:], ACT.Sin).then_inc(s_sin, 1)
            for n in range(RING):
                round_unit(n)
            for j in range(4):
                act.wait_ge(s_hf, j + 1)
                nc.scalar.activation(h_hi[:, 4 * j:4 * j + 4, :], xn_t[:, 4 * j:4 * j + 4, :], ACT.Copy).then_inc(s_hhi, 1)

            def win_epilogue(gi):
                pb = 2 * (gi % 2)
                act.wait_ge(s_used, UPG * (gi + 1))
                if gi < 4:
                    if gi:
                        act.wait_ge(s_rope, 2 * gi)
                    for b in range(2):
                        last = nc.scalar.activation(qraw[:, 2 * b:2 * b + 2, :],
                                                    ps[pb + b][:, :].rearrange("p (k t) -> p k t", k=2), ACT.Copy)
                elif gi < 6:
                    for t in range(NT):
                        last = nc.scalar.activation(v_tok[:, t, CW * (gi - 4):CW * (gi - 3)], ps[pb + t][:, :], ACT.Copy)
                else:
                    if gi == 6:
                        act.wait_ge(s_v0, 1)
                    else:
                        act.wait_ge(s_shift, gi - 6)
                    for b in range(2 if gi < 12 else 1):
                        last = nc.scalar.activation(ybuf[:, 2 * b:2 * b + 2, 1:T + 1],
                                                    ps[pb + b][:, :].rearrange("p (k t) -> p k t", k=2), ACT.Copy)
                    if gi == 12:
                        last = nc.scalar.activation(ybuf[:, 2, 1:T + 1], ps[pb + 1][:, 0:T], ACT.Copy)
                last.then_inc(s_evac, 1)

            def attn_exp(h):
                act.wait_ge(s_masked, h + 1)
                nc.scalar.activation(prob[:, 0, :], prob[:, 0, :], ACT.Exp, bias=stat[:, 6:7],
                                     accum_out=stat[:, 8:9])
                nc.scalar.activation(prob[:, 1:3, :], prob[:, 1:3, :], ACT.Exp, bias=stat[:, 7:8],
                                     accum_out=stat[:, 9:10]).then_inc(s_exp, 1)

            def attn_copy_pt(h):
                act.wait_ge(s_pt, h + 1)
                if h:
                    act.wait_ge(s_o, h)
                nc.scalar.activation(prob_t[:], ps[6][:, 0:3 * P].rearrange("p (k t) -> p k t", k=3),
                                     ACT.Copy).then_inc(s_ptc, 1)

            def attn_out(hp):
                act.wait_ge(s_o, 2 * hp + 2)
                nc.scalar.activation(mixa_hi[:, hp, :], ps[7][:, 0:T], ACT.Copy).then_inc(s_ohi, 1)

            def attn_slot(i):
                if 2 <= i < HEADS + 2 and i % 2 == 1:
                    attn_out((i - 3) // 2)
                if 1 <= i < HEADS + 1:
                    attn_copy_pt(i - 1)
                if i < HEADS:
                    attn_exp(i)

            for gi in range(WIN_G):
                for ku in range(UPG):
                    n = gi * UPG + ku
                    if n >= RING:
                        round_unit(n, LORA_W if gi == WIN_G - 1 else CW)
                    if gi and ku == 2:
                        win_epilogue(gi - 1)
                    u = n - 6 * UPG - 4 - LAG
                    if u >= 0 and u % 2 == 0 and u // 2 < HEADS + 2:
                        attn_slot(u // 2)
            win_epilogue(WIN_G - 1)

            act.wait_ge(s_lora, 1)
            nc.scalar.activation(lora[0:64, 0, :], lora[0:64, 0, :], ACT.Tanh)
            nc.scalar.activation(lora[:, 1, :], lora[:, 1, :], ACT.Sigmoid)
            nc.scalar.activation(lora[96:128, 2, :], lora[96:128, 2, :], ACT.Sigmoid).then_inc(s_lora, 1)
            for hp in range(PAIRS):
                act.wait_ge(s_kkr, hp + 1)
                if hp:
                    act.wait_ge(s_ssq, hp)
                nc.scalar.activation(sq[:], kk[:, hp, :], ACT.Square).then_inc(s_sqk, 1)
                act.wait_ge(s_zw, hp + 1)
                nc.scalar.activation(lw[:, hp, :], ps[4][:, 0:T], ACT.Sigmoid, bias=v1(V_W0 + hp))
                nc.scalar.activation(ab[:, hp, :], ps[6][:, 0:T], ACT.Sigmoid, bias=v1(V_A0 + hp)).then_inc(s_sigs, 1)
            act.wait_ge(s_rnr, PAIRS)
            nc.scalar.activation(rn[:], rn[:], ACT.Sqrt).then_inc(s_rns, 1)

            def pair_exps(hp):
                act.wait_ge(s_cen, hp + 1)
                if hp:
                    act.wait_ge(s_op, hp)
                nc.scalar.activation(e3[:, 0, :], cen[:, 0, :], ACT.Exp)
                nc.scalar.activation(e3[:, 1, :], cen[:, 0, :], ACT.Exp, scale=-1.0)
                nc.scalar.activation(e3[:, 2, :], cen[:, 1, :], ACT.Exp)
                nc.scalar.activation(refc[:, 3:4], refc[:, 2:3], ACT.Exp).then_inc(s_e3, 1)

            for hp in range(PAIRS):
                pair_exps(hp)
                act.wait_ge(s_tv, hp + 1)
                nc.scalar.activation(tv[:], ps[0][:, :].rearrange("p (k t) -> p k t", k=4), ACT.Copy).then_inc(s_tvc, 1)
                for lev in range(LEVELS):
                    i = hp * LEVELS + lev
                    act.wait_ge(s_xx, i + 1)
                    if lev < LEVELS - 1:
                        nc.scalar.activation(xm[:], ps[1][:, :].rearrange("p (k t) -> p k t", k=4), ACT.Copy)
                    nc.scalar.activation(xt[:], ps[2][:, :].rearrange("p (k t) -> p k t", k=4), ACT.Copy).then_inc(s_xc, 1)
                for c in range(2):
                    act.wait_ge(s_u, 2 * hp + c + 1)
                    nc.scalar.activation(us[:, 0, :], ps[6][:, 0:HD], ACT.Copy)
                    nc.scalar.activation(us[:, 1, :], ps[7][:, 0:HD], ACT.Copy).then_inc(s_uc, 1)
                    act.wait_ge(s_sa, 2 * hp + c + 1)
                    nc.scalar.activation(sa[:, c], ps[3][:, 0:2 * HD].rearrange("p (e d) -> p e d", e=2),
                                         ACT.Copy).then_inc(s_sac, 1)
                    if c == 0:
                        act.wait_ge(s_st, hp + 1)
                        nc.scalar.activation(s0[:], ps[0][:, 0:HD], ACT.Copy, scale=refc[:, 3:4]).then_inc(s_stc, 1)
                act.wait_ge(s_ot, hp + 1)
                nc.scalar.activation(o_t[0:64, :], ps[1][0:64, 0:T], ACT.Copy)
                nc.scalar.activation(o_t[64:128, :], ps[2][64:128, 0:T], ACT.Copy).then_inc(s_otc, 1)
                act.wait_ge(s_dev, hp + 1)
                nc.scalar.activation(sq[:], lw[:, hp, :], ACT.Square).then_inc(s_dsq, 1)
            act.wait_ge(s_bonus, PAIRS)
            nc.scalar.activation(kk[:], kk[:], ACT.Sqrt).then_inc(s_vrt, 1)
            for hp in range(PAIRS):
                act.wait_ge(s_mixf, hp + 1)
                nc.scalar.activation(mixr_hi[:, hp, :], lw[:, hp, :], ACT.Copy).then_inc(s_mrhi, 1)

            act.wait_ge(s_mixr, PAIRS)
            act.dma_start(x1[:], x_dram).then_inc(s_x1in, 16)

            def gate_copy(i, dst):
                act.wait_ge(s_gt, i + 1)
                if i:
                    act.wait_ge(s_x1, 2 * i)
                nc.scalar.activation(dst[:], ps[4][:, :], ACT.Copy).then_inc(s_gtb, 1)

            def square_sums(i, junk):
                ct = i % 4
                for t in range(NT):
                    act.wait_ge(s_x1, 2 * i + t + 1)
                    if i or t:
                        act.wait_ge(s_ssp, 2 * i + t)
                    ins = nc.scalar.activation(junk[:], x1[:, t, ct * CW:(ct + 1) * CW], ACT.Square,
                                               accum_out=stat[:, 10 + 4 * t + ct:11 + 4 * t + ct])
                    ins.then_inc(s_ssp, 1)

            for g in range(OUT_G):
                for ku in range(UPG):
                    round_unit(N_OUT0 + g * UPG + ku)
                    if g and ku == 2:
                        gate_copy(g - 1, gtb)
                    if g and ku == 4:
                        square_sums(g - 1, sqj1)
            gate_copy(OUT_G - 1, gtb)
            square_sums(OUT_G - 1, sqj1)
            act.wait_ge(s_ms2, 1)
            nc.scalar.activation(stat[:, 4:6], stat[:, 2:4], ACT.Sqrt).then_inc(s_rt2, 1)
            for n in range(RING):
                round_unit(N_GU0 + n)
            for j in range(4):
                act.wait_ge(s_h2f, j + 1)
                nc.scalar.activation(h_hi[:, 4 * j:4 * j + 4, :], h2f[:, j % 2], ACT.Copy).then_inc(s_h2hi, 1)

            def ffn_silu(gn, parity):
                act.wait_ge(s_used, gn * (2 * UPG) + (N_GU0 + 2 * UPG))
                for b in range(2):
                    last = nc.scalar.activation(sg[:, parity, 2 * b:2 * b + 2, :],
                                                ps[4 * parity + b][:, :].rearrange("p (k t) -> p k t", k=2), ACT.Silu)
                last.then_inc(s_silu, 1)

            def ffn_hi(gn, parity):
                act.wait_ge(s_prod, gn + 1)
                nc.scalar.activation(act_hi[:, bass.ds(gn * 4, 4), :], sg[:, parity], ACT.Copy).then_inc(s_ahi, 1)

            def round_gu(it, j):
                act.wait_ge(s_raw[j % RING], it * (2 * UPG // RING * 16) + 16 * ((N_GU0 + j) // RING + 1))
                act.wait_ge(s_used, it * (2 * UPG) + (N_GU0 + j - RING + 1))
                nc.scalar.activation(w_hi[:, j % RING], raw[:, j % RING], ACT.Copy).then_inc(s_hi, 1)

            for j in range(RING, 2 * UPG):
                round_gu(0, j)
            with act.Fori(0, (GU_G - 1) // 2) as it:
                for half in range(2):
                    for j in range(2 * UPG):
                        round_gu(it * 2, 2 * UPG * (1 + half) + j)
                        if j == 2:
                            ffn_silu(it * 2 + half, half)
                        if j == 5:
                            ffn_hi(it * 2 + half, half)
            ffn_silu(GU_G - 1, 0)
            for n in range(N_DOWN0, N_DOWN0 + 2):
                round_unit(n)
            ffn_hi(GU_G - 1, 0)
            for g in range(OUT_G):
                for ku in range(DOWN_U):
                    n = N_DOWN0 + g * DOWN_U + ku
                    if n >= N_DOWN0 + 2:
                        round_unit(n)
                    if g and ku == 2:
                        gate_copy(OUT_G + g - 1, gtb2)
                    if g and ku == 4:
                        square_sums(OUT_G + g - 1, sqj)
            gate_copy(2 * OUT_G - 1, gtb2)
            square_sums(2 * OUT_G - 1, sqj)
            act.wait_ge(s_ms2, 2)
            nc.scalar.activation(stat[:, 4:6], stat[:, 2:4], ACT.Sqrt).then_inc(s_rt2, 1)

        @block.vector
        def _(dve):
            links = [0]

            def link(ins):
                links[0] += 1
                ins.then_inc(s_dch, 1)
                dve.wait_ge(s_dch, links[0])

            def rest_unit(n, width=CW):
                dve.wait_ge(s_hi, n + 1)
                nc.vector.tensor_tensor(w_lo[:, slot_of(n), :, 0:width], raw[:, slot_of(n), :, 0:width],
                                        w_hi[:, slot_of(n), :, 0:width].bitcast(F32), ALU.subtract).then_inc(s_lo, 1)

            def ada_unit(u):
                g, ku = u // UPG, u % UPG
                buf = ada_raw2 if u >= END_ADA1 else ada_raw
                dve.wait_ge(s_ada[u % RING], 16 * (u // RING + 1))
                if ku == 0 and g >= 2:
                    dve.wait_ge(s_fin, g - 1)
                dst = acc[:, g % 2, :]
                for kx in range(UK):
                    k = UK * ku + kx
                    if k == 0:
                        link(nc.vector.tensor_scalar(dst, buf[:, u % RING, kx, :], silu_c[:, k:k + 1], None, ALU.mult))
                    elif kx == 0:
                        link(nc.vector.scalar_tensor_tensor(dst, buf[:, u % RING, kx, :], silu_c[:, k:k + 1], dst,
                                                            ALU.mult, ALU.add))
                    else:
                        nc.vector.scalar_tensor_tensor(dst, buf[:, u % RING, kx, :], silu_c[:, k:k + 1], dst,
                                                       ALU.mult, ALU.add).then_inc(s_adaused, 1)
                dve.wait_ge(s_adaused, u + 1)

            def ada_cols(g):
                c = 4 * ada_order[g]
                dve.wait_ge(s_fin, g + 1)
                nc.vector.tensor_tensor(ada_t[:, c:c + 4], ps[FIN][:, 0:4], vec[:, V_B + c:V_B + c + 4],
                                        ALU.add).then_inc(s_col, 1)
                dve.wait_ge(s_col, g + 1)

            def first_h(j):
                if j == 0:
                    dve.wait_ge(s_xnt, 8)
                link(nc.vector.scalar_tensor_tensor(scale1[:, 4 * j:4 * j + 4], ada_t[:, 16 + 4 * j:20 + 4 * j], 1.0,
                                                    vec[:, V_N1 + 4 * j:V_N1 + 4 * j + 4], ALU.add, ALU.mult))
                for k in range(4 * j, 4 * j + 4):
                    last = nc.vector.tensor_scalar(xn_t[:, k, :], xn_t[:, k, :], scale1[:, k:k + 1], ada_t[:, k:k + 1],
                                                   ALU.mult, ALU.add)
                last.then_inc(s_hf, 1)
                dve.wait_ge(s_hhi, j + 1)
                nc.vector.tensor_tensor(h_lo[:, 4 * j:4 * j + 4, :], xn_t[:, 4 * j:4 * j + 4, :],
                                        h_hi[:, 4 * j:4 * j + 4, :].bitcast(F32), ALU.subtract).then_inc(s_hlo, 1)

            dve.wait_ge(s_sigc, 1)
            nc.vector.tensor_tensor(silu_c[:], vec[:, V_C:V_C + KT], sig_c[:], ALU.mult).then_inc(s_siluc, 1)
            dve.wait_ge(s_siluc, 1)
            dve.wait_ge(s_pos, 16)
            dve.wait_ge(s_small, 80)
            link(nc.vector.tensor_copy(ang[:], pos_i[:]))
            link(nc.vector.tensor_scalar(ang[:], ang[:], ck(C_INV, 1), None, ALU.mult))
            magic = 12582912.0
            link(nc.vector.tensor_scalar(turns[:], ang[:], 1.0 / (2 * math.pi), magic, ALU.mult, ALU.add))
            link(nc.vector.tensor_scalar(turns[:], turns[:], magic, None, ALU.subtract))
            for part in (6.28125, 0.0019340515136718750, 1.2556659146019e-06):
                link(nc.vector.scalar_tensor_tensor(ang[:], turns[:], -part, ang[:], ALU.mult, ALU.add))
            link(nc.vector.tensor_scalar(ang[:], ang[:], 3.1415925, -3.1415925, ALU.min, ALU.max))
            link(nc.vector.tensor_scalar(turns[:], ang[:], -1.0, None, ALU.mult))
            link(nc.vector.tensor_tensor(turns[:], turns[:], ang[:], ALU.max))
            nc.vector.tensor_scalar(turns[:], turns[:], -1.0, math.pi / 2, ALU.mult, ALU.add).then_inc(s_trig, 1)
            dve.wait_ge(s_ss, NT)
            nc.vector.tensor_scalar(stat[:, 2:4], stat[:, 0:2], 1.0 / D, RMS_EPS, ALU.mult, ALU.add).then_inc(s_ms, 1)
            for u in range(2):
                ada_unit(u)
            dve.wait_ge(s_rt, 1)
            link(nc.vector.reciprocal(stat[:, 4:6], stat[:, 4:6]))
            for t in range(NT):
                nc.vector.tensor_scalar(x_in[:, t, :], x_in[:, t, :], stat[:, 4 + t:5 + t], None, ALU.mult).then_inc(s_xn, 1)
            for u in range(2, INIT_ADA):
                ada_unit(u)
                g = u // UPG
                if u % UPG == 3 and g >= 1:
                    ada_cols(g - 1)
                if u % (2 * UPG) == 4 and g >= 2:
                    first_h(g // 2 - 1)
                if u % UPG == 6 and g >= 6:
                    rest_unit(2 * (g - 6))
                    rest_unit(2 * (g - 6) + 1)
            ada_cols(7)
            first_h(3)
            nc.vector.memset(ybuf[:, :, 0:1], 0.0).then_inc(s_v0, 1)

            def win_epilogue(gi):
                if gi < 4:
                    for b in range(2):
                        i = 2 * gi + b
                        dve.wait_ge(s_perm, i + 1)
                        dst = qk[:, 4 * gi + 2 * b:4 * gi + 2 * b + 2, :]
                        cos2 = cosT[:].unsqueeze(1).broadcast_to([P, 2, T])
                        sin2 = sinT[:].unsqueeze(1).broadcast_to([P, 2, T])
                        if i:
                            dve.wait_ge(s_rope, i)
                        nc.vector.tensor_tensor(t1[:], ps[6 + b][:, :].rearrange("p (k t) -> p k t", k=2), sin2, ALU.mult)
                        link(nc.vector.tensor_tensor(dst, qraw[:, 2 * b:2 * b + 2, :], cos2, ALU.mult))
                        nc.vector.tensor_tensor(dst, dst, t1[:], ALU.add).then_inc(s_rope, 1)
                elif gi >= 6:
                    dve.wait_ge(s_evac, gi + 1)
                    if gi == 6:
                        dve.wait_ge(s_v0, 1)
                    n = 4 if gi < 12 else 3
                    dst = rkv[:, 4 * (gi - 6):4 * (gi - 6) + 4, :] if gi < 12 else lora[:, :, :]
                    link(nc.vector.tensor_tensor(dst, ybuf[:, 0:n, 0:T], ybuf[:, 0:n, 1:T + 1], ALU.subtract))
                    for i in range(n):
                        last = nc.vector.scalar_tensor_tensor(dst[:, i, :], dst[:, i, :], v1(V_MU + 4 * (gi - 6) + i),
                                                              ybuf[:, i, 1:T + 1], ALU.mult, ALU.add)
                    last.then_inc(s_shift if gi < 12 else s_lora, 1)

            def attn_mask(h):
                dve.wait_ge(s_score, h + 1)
                if h:
                    dve.wait_ge(s_pt, h)
                link(nc.vector.scalar_tensor_tensor(prob[:], ps[4][:, 0:3 * P].rearrange("p (k t) -> p k t", k=3),
                                                    HD ** -0.5, ck(C_LC, 3 * P).rearrange("p (k t) -> p k t", k=3),
                                                    ALU.mult, ALU.add))
                nc.vector.tensor_reduce(stat[:, 6:7], prob[:, 0, :], axis=AX, op=ALU.max, negate=True)
                nc.vector.tensor_reduce(stat[:, 7:8], prob[:, 1:3, :].rearrange("p k t -> p (k t)"), axis=AX,
                                        op=ALU.max, negate=True).then_inc(s_masked, 1)

            def attn_norm(h):
                dve.wait_ge(s_exp, h + 1)
                link(nc.vector.reciprocal(stat[:, 8:10], stat[:, 8:10]))
                nc.vector.tensor_scalar(prob[:, 0, :], prob[:, 0, :], stat[:, 8:9], None, ALU.mult)
                nc.vector.tensor_scalar(prob[:, 1:3, :], prob[:, 1:3, :], stat[:, 9:10], None, ALU.mult).then_inc(s_prob, 1)

            def attn_rest(hp):
                dve.wait_ge(s_ohi, hp + 1)
                nc.vector.tensor_tensor(mixa_lo[:, hp, :], ps[7][:, 0:T], mixa_hi[:, hp, :].bitcast(F32),
                                        ALU.subtract).then_inc(s_mixa, 1)

            def attn_slot(i):
                if 2 <= i < HEADS + 2 and i % 2 == 1:
                    attn_rest((i - 3) // 2)
                if i < HEADS:
                    attn_mask(i)

            ada_next = [INIT_ADA]

            def ada_step(limit):
                if ada_next[0] < limit:
                    u = ada_next[0]
                    ada_unit(u)
                    ada_next[0] += 1

            for gi in range(WIN_G):
                for ku in range(UPG):
                    n = gi * UPG + ku
                    if n >= RING:
                        rest_unit(n, LORA_W if gi == WIN_G - 1 else CW)
                    if gi and ku == 4:
                        win_epilogue(gi - 1)
                    u = n - 6 * UPG - 4 - LAG
                    if u >= 0 and u % 2 == 0 and u // 2 < HEADS + 2:
                        attn_slot(u // 2)
                    if u >= 0 and u % 2 == 1 and u // 2 < HEADS:
                        attn_norm(u // 2)
                    if n % 2 == 1:
                        ada_step(END_ADA1)
                        if ada_next[0] % UPG == 2 and n > 2 * UPG:
                            ada_cols(ada_next[0] // UPG - 1)
            win_epilogue(WIN_G - 1)

            for hp in range(PAIRS):
                nc.vector.tensor_scalar(kk[:, hp, :], rkv[:, 8 + hp, :], v1(V_KK + hp), None, ALU.mult).then_inc(s_kkr, 1)
            for hp in range(PAIRS):
                dve.wait_ge(s_ssq, hp + 1)
                nc.vector.tensor_copy(rn[:, hp, :], ps[7][:, 0:T]).then_inc(s_rnr, 1)
            dve.wait_ge(s_sigs, PAIRS)
            nc.vector.tensor_scalar(lw[:], lw[:], -SQ, None, ALU.mult).then_inc(s_lwr, 1)
            for hp in range(PAIRS):
                link(nc.vector.tensor_scalar(cen[:, 0, :], ab[:, hp, :], 1.0, v1(V_KA + hp), ALU.subtract, ALU.mult))
                link(nc.vector.scalar_tensor_tensor(rkv[:, 8 + hp, :], cen[:, 0, :], 1.0, rkv[:, 8 + hp, :], ALU.add,
                                                    ALU.mult))
            dve.wait_ge(s_rns, 1)
            link(nc.vector.tensor_scalar(rn[:], rn[:], 1e-12, None, ALU.max))
            link(nc.vector.reciprocal(rn[:], rn[:]))
            link(nc.vector.tensor_tensor(kk[:], kk[:], rn[:], ALU.mult))
            nc.vector.tensor_tensor(ab[:], ab[:], kk[:], ALU.mult).then_inc(s_pre, 1)
            dve.wait_ge(s_pre, 1)

            def pair_head(hp):
                link(nc.vector.tensor_tensor_scan(cen[:, 0, :], ck(C_RES, T), lw[:, hp, :], 0.0, ALU.mult, ALU.add))
                c4 = cen[:, 0, :].rearrange("p (c b t) -> p c b t", c=2, b=2)
                link(nc.vector.tensor_copy(refc[:, 0:2], c4[:, :, 0, 63]))
                for c in range(2):
                    x = cen[:, 0, 128 * c:128 * c + 64]
                    ins = nc.vector.tensor_scalar(x, x, refc[:, c:c + 1], None, ALU.subtract)
                link(ins)
                nc.vector.tensor_tensor(refc[:, 2:3], refc[:, 1:2], cen[:, 0, 127:128], ALU.add)
                nc.vector.tensor_tensor(cen[:, 1, :], cen[:, 0, :], lw[:, hp, :], ALU.subtract).then_inc(s_cen, 1)
                dve.wait_ge(s_e3, hp + 1)
                if hp:
                    dve.wait_ge(s_ot, hp)
                nc.vector.scalar_tensor_tensor(op[:, 0, :], kk[:, hp, :], -1.0, e3[:, 2, :], ALU.mult, ALU.mult)
                nc.vector.tensor_tensor(op[:, 1, :], rkv[:, hp, :], e3[:, 0, :], ALU.mult)
                nc.vector.tensor_tensor(op[:, 2, :], ab[:, hp, :], e3[:, 1, :], ALU.mult)
                nc.vector.tensor_tensor(op[:, 3, :], rkv[:, 8 + hp, :], e3[:, 1, :], ALU.mult).then_inc(s_op, 1)

            strict_incl = ck(C_SI, T).bitcast(I32).unsqueeze(1).broadcast_to([P, 2, T])
            link(nc.vector.memset(br[:], 0.0))
            link(nc.vector.memset(kr[:], 0.0))
            for hp in range(PAIRS):
                pair_head(hp)
                dve.wait_ge(s_gram, 2 * hp + 1)
                m0 = ck(C_M0).unsqueeze(1).broadcast_to([P, 2, P])
                for e in range(2):
                    nc.vector.tensor_tensor(xm[:, 2 * e:2 * e + 2, :],
                                            ps[4 + 2 * e][:, 0:2 * P].rearrange("p (c s) -> p c s", c=2), m0, ALU.mult)
                    ins = nc.vector.copy_predicated(br[:, 2 * e:2 * e + 2, :], strict_incl,
                                                    ps[1 + e][:, :].rearrange("p (c s) -> p c s", c=2))
                link(ins)
                nc.vector.tensor_tensor(xm[:], xm[:], over4(ident), ALU.add).then_inc(s_gramc, 1)
                link(nc.vector.tensor_tensor(xt[:], br[:, :, 0:P], over4(ck(C_M0T)), ALU.mult))
                nc.vector.tensor_tensor(xt[:], xt[:], over4(ident), ALU.add).then_inc(s_gramc, 1)
                dve.wait_ge(s_gram, 2 * hp + 2)
                for e in range(2):
                    ins = nc.vector.copy_predicated(kr[:, 2 * e:2 * e + 2, :], strict_incl,
                                                    ps[4 + 3 * e][:, :].rearrange("p (c s) -> p c s", c=2))
                ins.then_inc(s_gramc, 1)
                for lev in range(LEVELS):
                    i = hp * LEVELS + lev
                    dve.wait_ge(s_y, i + 1)
                    nc.vector.tensor_tensor(y1[:], ps[3][:, :].rearrange("p (k t) -> p k t", k=4), over4(ident),
                                            ALU.add).then_inc(s_y1, 1)
                nc.vector.scalar_tensor_tensor(rkv[:, hp, :], rkv[:, hp, :], v1(V_RK + hp), rkv[:, 8 + hp, :],
                                               ALU.mult, ALU.mult).then_inc(s_bon, 1)
                dve.wait_ge(s_mean, hp + 1)
                nc.vector.scalar_tensor_tensor(lw[:, hp, :], ps[6][:, 0:T], -1.0 / HD, o_t[:], ALU.mult,
                                               ALU.add).then_inc(s_dev, 1)
                dve.wait_ge(s_var, hp + 1)
                nc.vector.tensor_scalar(kk[:, hp, :], ps[7][:, 0:T], 1.0 / HD, GN_EPS, ALU.mult, ALU.add)
                nc.vector.tensor_tensor(rkv[:, hp, :], ps[3][:, 0:T], rkv[:, 16 + hp, :], ALU.mult).then_inc(s_bonus, 1)
            dve.wait_ge(s_bonus, PAIRS)
            dve.wait_ge(s_vrt, 1)
            link(nc.vector.reciprocal(kk[:], kk[:]))
            link(nc.vector.tensor_tensor(lw[:], lw[:], kk[:], ALU.mult))
            for hp in range(PAIRS):
                ins = nc.vector.tensor_scalar(lw[:, hp, :], lw[:, hp, :], v1(V_GG + hp), v1(V_GB + hp), ALU.mult, ALU.add)
            link(ins)
            link(nc.vector.tensor_tensor(lw[:], lw[:], rkv[:, 0:8, :], ALU.add))
            for hp in range(PAIRS):
                dve.wait_ge(s_g, hp + 1)
                nc.vector.tensor_tensor(lw[:, hp, :], lw[:, hp, :], ps[4 if hp % 2 == 0 else 6][:, 0:T],
                                        ALU.mult).then_inc(s_mixf, 1)
            for hp in range(PAIRS):
                dve.wait_ge(s_mrhi, hp + 1)
                nc.vector.tensor_tensor(mixr_lo[:, hp, :], lw[:, hp, :], mixr_hi[:, hp, :].bitcast(F32),
                                        ALU.subtract).then_inc(s_mixr, 1)

            def gate_diag(i, dst):
                c = (8 if i < 4 else 20) * 4 + 4 * (i % 4)
                if i:
                    dve.wait_ge(s_gt, i)
                nc.vector.tensor_tensor(dst[:].rearrange("p (k t) -> p k t", k=4), over4(ident),
                                        ada_t[:, c:c + 4].unsqueeze(2).broadcast_to([P, 4, P]), ALU.mult).then_inc(s_diag, 1)

            def residual(i, gate, tmp, banks):
                ct = i % 4
                dve.wait_ge(s_gtb, i + 1)
                dve.wait_ge(s_used, N_OUT0 + UPG * (i + 1) if i < 4 else N_DOWN0 + DOWN_U * (i - 3))
                for t in range(NT):
                    if i or t:
                        dve.wait_ge(s_x1, 2 * i + t)
                    link(nc.vector.tensor_tensor(tmp[:], ps[banks + t][:, :], gate[:], ALU.mult))
                    x = x1[:, t, ct * CW:(ct + 1) * CW]
                    nc.vector.tensor_tensor(x, x, tmp[:], ALU.add).then_inc(s_x1, 1)

            def row_rms(i):
                dve.wait_ge(s_ssp, 8 * (i + 1))
                link(nc.vector.tensor_reduce(stat[:, 2:4], stat[:, 10:18].rearrange("p (t c) -> p t c", t=2), axis=AX, op=ALU.add))
                nc.vector.tensor_scalar(stat[:, 2:4], stat[:, 2:4], 1.0 / D, RMS_EPS, ALU.mult, ALU.add).then_inc(s_ms2, 1)
                dve.wait_ge(s_rt2, i + 1)
                link(nc.vector.reciprocal(stat[:, 4:6], stat[:, 4:6]))

            dve.wait_ge(s_x1in, 16)
            done_cols = [ada_next[0] // UPG]
            for g in range(OUT_G):
                for ku in range(UPG):
                    n_out = g * UPG + ku
                    rest_unit(N_OUT0 + n_out)
                    ada_step(END_ADA1)
                    ada_step(END_ADA1)
                    if ku == 1:
                        gate_diag(g, diag)
                    if g and ku == 4:
                        residual(g - 1, gtb, upd, 2 * ((g - 1) % 2))
                    if ku in (2, 6):
                        summed = (ada_next[0] - 2) // UPG
                    if ku in (5, 1) and n_out > 2:
                        while done_cols[0] < summed:
                            ada_cols(done_cols[0])
                            done_cols[0] += 1
            while ada_next[0] < END_ADA1:
                ada_step(END_ADA1)
            while done_cols[0] < END_ADA1 // UPG:
                ada_cols(done_cols[0])
                done_cols[0] += 1
            link(nc.vector.scalar_tensor_tensor(scale2[:], ada_t[:, 64:80], 1.0, vec[:, V_N2:V_N2 + KT], ALU.add, ALU.mult))
            residual(OUT_G - 1, gtb, upd, 2)
            row_rms(0)
            for t in range(NT):
                nc.vector.tensor_scalar(xn2[:, t, :], x1[:, t, :], stat[:, 4 + t:5 + t], None, ALU.mult).then_inc(s_xn2, 1)
            for n in range(RING):
                rest_unit(N_GU0 + n)
            for j in range(4):
                if j >= 2:
                    dve.wait_ge(s_h2lo, j - 1)
                for b in range(2):
                    dve.wait_ge(s_x2t, 2 * j + b + 1)
                    for kx in range(2):
                        k = 4 * j + 2 * b + kx
                        last = nc.vector.tensor_scalar(h2f[:, j % 2, 2 * b + kx, :], ps[(2 * j + b) % 4][:, kx * T:(kx + 1) * T],
                                                       scale2[:, k:k + 1], ada_t[:, 48 + k:49 + k], ALU.mult, ALU.add)
                last.then_inc(s_h2f, 1)
                dve.wait_ge(s_h2hi, j + 1)
                nc.vector.tensor_tensor(h_lo[:, 4 * j:4 * j + 4, :], h2f[:, j % 2], h_hi[:, 4 * j:4 * j + 4, :].bitcast(F32),
                                        ALU.subtract).then_inc(s_h2lo, 1)

            def ffn_product(gn, parity):
                dve.wait_ge(s_silu, gn + 1)
                for b in range(2):
                    x = sg[:, parity, 2 * b:2 * b + 2, :]
                    last = nc.vector.tensor_tensor(x, x, ps[4 * parity + 2 + b][:, :].rearrange("p (k t) -> p k t", k=2), ALU.mult)
                last.then_inc(s_prod, 1)

            def ffn_lo(gn, parity):
                dve.wait_ge(s_ahi, gn + 1)
                nc.vector.tensor_tensor(act_lo[:, bass.ds(gn * 4, 4), :], sg[:, parity],
                                        act_hi[:, bass.ds(gn * 4, 4), :].bitcast(F32), ALU.subtract).then_inc(s_alo, 1)

            def rest_gu(it, j):
                dve.wait_ge(s_hi, it * (2 * UPG) + (N_GU0 + j + 1))
                nc.vector.tensor_tensor(w_lo[:, j % RING], raw[:, j % RING], w_hi[:, j % RING].bitcast(F32),
                                        ALU.subtract).then_inc(s_lo, 1)

            for j in range(RING, 2 * UPG):
                rest_gu(0, j)
            with dve.Fori(0, (GU_G - 1) // 2) as it:
                for half in range(2):
                    for j in range(2 * UPG):
                        rest_gu(it * 2, 2 * UPG * (1 + half) + j)
                        if j == 3:
                            ffn_product(it * 2 + half, half)
                        if j == 7:
                            ffn_lo(it * 2 + half, half)
            ffn_product(GU_G - 1, 0)
            for n in range(N_DOWN0, N_DOWN0 + 2):
                rest_unit(n)
            ffn_lo(GU_G - 1, 0)
            for g in range(OUT_G):
                for ku in range(DOWN_U):
                    n = N_DOWN0 + g * DOWN_U + ku
                    if n >= N_DOWN0 + 2:
                        rest_unit(n)
                    if ku % 2 == 0 and ku < 2 * UPG:
                        ada_unit(END_ADA1 + g * UPG + ku // 2)
                    if ku == DOWN_U - 3:
                        ada_cols(20 + g)
                        gate_diag(OUT_G + g, diag2)
                    if g and ku == 4:
                        residual(OUT_G + g - 1, gtb2, upd2, 2 * ((g - 1) % 2))
            residual(2 * OUT_G - 1, gtb2, upd2, 2)
            row_rms(1)
            dve.wait_ge(s_nf, 16)
            for t in range(NT):
                nc.vector.scalar_tensor_tensor(x1[:, t, :], x1[:, t, :], stat[:, 4 + t:5 + t], nf_b[:], ALU.mult,
                                               ALU.mult).then_inc(s_fs, 1)

        @block.tensor
        def _(pe):
            mm = nc.tensor.matmul

            def three_pass(out, sh, sl, mh, ml, first, last, shared=False):
                mm(out, sh, mh, start=first, stop=False, skip_group_check=shared)
                mm(out, sh, ml, start=False, stop=False, skip_group_check=shared)
                return mm(out, sl, mh, start=False, stop=last, skip_group_check=shared)

            def unit_channels(n, ku, pb, hi, lo, blocks):
                pe.wait_ge(s_lo, n + 1)
                for i, c0 in enumerate(blocks):
                    for kx in range(UK):
                        k = UK * ku + kx
                        out = ps[pb + i // 2][:, (i % 2) * T:(i % 2 + 1) * T]
                        w = slice(c0, c0 + P)
                        last = three_pass(out, w_hi[:, n % RING, kx, w] if isinstance(n, int) else None,
                                          w_lo[:, n % RING, kx, w], hi[:, k, :], lo[:, k, :],
                                          first=(k == 0 and i % 2 == 0), last=(k == KT - 1), shared=True)
                last.then_inc(s_used, 1)

            def unit_tokens(n, k0, kmax, pb, hi, lo):
                pe.wait_ge(s_lo, n + 1)
                for t in range(NT):
                    for kx in range(UK):
                        k = k0 + kx
                        hk, lk, kk_ = (hi, lo, k) if not isinstance(hi, tuple) else (hi[k // 8], lo[k // 8], k % 8)
                        tok = slice(t * P, (t + 1) * P)
                        last = three_pass(ps[pb + t][:, :], hk[:, kk_, tok], lk[:, kk_, tok], w_hi[:, slot_of(n), kx, :],
                                          w_lo[:, slot_of(n), kx, :], first=(k == 0), last=(k == kmax - 1))
                last.then_inc(s_used, 1)

            def ada_fin(g):
                pe.wait_ge(s_adaused, UPG * (g + 1))
                if g:
                    pe.wait_ge(s_col, g)
                for j in range(4):
                    last = mm(ps[FIN][:, j:j + 1], acc[:, g % 2, j * P:(j + 1) * P], ones[:, 0:1], start=True, stop=True)
                last.then_inc(s_fin, 1)

            pe.wait_ge(s_cst, 16)
            pe.wait_ge(s_rows, 16 * 13)
            for i, (rows, col) in enumerate(((104, 0), (96, V_B), (27, V_MU))):
                last = nc.tensor.transpose(ps[4][:, col:col + rows], vrows[0:rows, i, :], ident[0:rows, 0:rows])
            last.then_inc(s_vt, 1)
            pe.wait_ge(s_xn, NT)
            pe.wait_ge(s_vec, 1)
            for b in range(8):
                for kx in range(2):
                    for t in range(NT):
                        k = 2 * b + kx
                        last = nc.tensor.transpose(ps[b][:, kx * T + t * P:kx * T + (t + 1) * P],
                                                   x_in[:, t, k * P:(k + 1) * P], ident)
                last.then_inc(s_xt, 1)
            pe.wait_ge(s_xnt, FIN + 1)
            for g in range(8):
                ada_fin(g)

            def rope_perm(gi):
                pe.wait_ge(s_evac, gi + 1)
                if gi == 0:
                    pe.wait_ge(s_small, 80)
                    pe.wait_ge(s_xnt, 8)
                else:
                    pe.wait_ge(s_rope, 2 * gi)
                for b in range(2):
                    mm(ps[6 + b][:, :], ck(C_PERM), qraw[:, 2 * b:2 * b + 2, :].rearrange("p k t -> p (k t)"),
                       start=True, stop=True).then_inc(s_perm, 1)

            def attn_slot(i):
                if 2 <= i < HEADS + 2:
                    h = i - 2
                    hp, e = h // 2, h % 2
                    pe.wait_ge(s_ptc, h + 1)
                    if e == 0 and hp:
                        pe.wait_ge(s_mixa, hp)
                    rows = slice(64 * e, 64 * e + 64)
                    vs = slice(HD * h, HD * h + HD)
                    mm(ps[7][rows, 0:P], v_tok[:, 0, vs], prob_t[:, 0, :], start=True, stop=True)
                    mm(ps[7][rows, P:T], v_tok[:, 0, vs], prob_t[:, 1, :], start=True, stop=False)
                    mm(ps[7][rows, P:T], v_tok[:, 1, vs], prob_t[:, 2, :], start=False, stop=True).then_inc(s_o, 1)
                if 1 <= i < HEADS + 1:
                    h = i - 1
                    pe.wait_ge(s_prob, h + 1)
                    if h:
                        pe.wait_ge(s_ptc, h)
                    for j in range(3):
                        last = nc.tensor.transpose(ps[6][:, j * P:(j + 1) * P], prob[:, j, :], ident)
                    last.then_inc(s_pt, 1)
                if i < HEADS:
                    h = i
                    if h == 0:
                        pe.wait_ge(s_rope, 8)
                        pe.wait_ge(s_evac, 6)
                    else:
                        pe.wait_ge(s_masked, h)
                    rows = slice(64 * (h % 2), 64 * (h % 2) + 64)
                    q, k = qk[rows, h // 2, :], qk[rows, 8 + h // 2, :]
                    mm(ps[4][:, 0:P], q[:, 0:P], k[:, 0:P], start=True, stop=True)
                    mm(ps[4][:, P:3 * P], q[:, P:T], k, start=True, stop=True).then_inc(s_score, 1)

            full = (0, P, 2 * P, 3 * P)
            fins = [8]
            pe.wait_ge(s_xnt, 8)
            for gi in range(WIN_G):
                for ku in range(UPG):
                    n = gi * UPG + ku
                    if gi == 0 and ku % 2 == 0:
                        pe.wait_ge(s_hlo, ku // 2 + 1)
                    if gi >= 2 and ku == 0:
                        pe.wait_ge(s_evac, gi - 1)
                    pb = 2 * (gi % 2)
                    if gi in (4, 5):
                        unit_tokens(n, UK * ku, KT, pb, h_hi, h_lo)
                    else:
                        unit_channels(n, ku, pb, h_hi, h_lo, full if gi < WIN_G - 1 else (0, P, LORA_W - P))
                    if 1 <= gi <= 4 and ku == 1:
                        rope_perm(gi - 1)
                    u = n - 6 * UPG - 4
                    if u >= 0 and u % 2 == 0 and u // 2 < HEADS + 2:
                        attn_slot(u // 2)
                    if n % 2 == 1 and (INIT_ADA + n // 2 + 1) % UPG == 1 and n > 2 * UPG:
                        ada_fin(fins[0])
                        fins[0] += 1

            pe.wait_ge(s_lora, 2)
            pe.wait_ge(s_mixa, PAIRS)
            for hp in range(PAIRS):
                cols = slice(hp * P, (hp + 1) * P)
                if hp:
                    pe.wait_ge(s_sigs, hp)
                mm(ps[4][:, 0:T], w_di[0:64, cols], lora[0:64, 0, :], start=True, stop=True)
                mm(ps[6][:, 0:T], w_di[64:128, cols], lora[64:128, 0, :], start=True, stop=True).then_inc(s_zw, 1)
                pe.wait_ge(s_sqk, hp + 1)
                if hp:
                    pe.wait_ge(s_rnr, hp)
                mm(ps[7][:, 0:T], ck(C_BLK), sq[:], start=True, stop=True).then_inc(s_ssq, 1)
            pe.wait_ge(s_rnr, PAIRS)

            for hp in range(PAIRS):
                pe.wait_ge(s_op, hp + 1)
                if hp:
                    pe.wait_ge(s_bonus, hp)
                half = [slice(0, 64), slice(64, 128)]
                chunk = [slice(0, P), slice(P, T)]
                for e in range(2):
                    for c in range(2):
                        mm(ps[4 + 2 * e][:, c * P:(c + 1) * P], op[half[e], 0, chunk[c]], op[half[e], 2, chunk[c]],
                           start=True, stop=True)
                for e in range(2):
                    for c in range(2):
                        last = mm(ps[1 + e][:, 2 * c * P:2 * (c + 1) * P], op[half[e], 2, chunk[c]],
                                  op[half[e], 0:2, chunk[c]], start=True, stop=True)
                last.then_inc(s_gram, 1)
                for j, src in enumerate((op[:, 2, 0:P], op[:, 3, 0:P], rkv[:, 16 + hp, 0:P], rkv[:, 16 + hp, P:T])):
                    last = nc.tensor.transpose(ps[0][:, j * P:(j + 1) * P], src, ident)
                last.then_inc(s_tv, 1)
                pe.wait_ge(s_gramc, 3 * hp + 1)
                for e in range(2):
                    for c in range(2):
                        last = mm(ps[4 + 3 * e][:, 2 * c * P:2 * (c + 1) * P], op[half[e], 3, chunk[c]],
                                  op[half[e], 0:2, chunk[c]], start=True, stop=True)
                last.then_inc(s_gram, 1)
                pe.wait_ge(s_gramc, 3 * hp + 2)
                for lev in range(LEVELS):
                    i = hp * LEVELS + lev
                    pe.wait_ge(s_nt, i + 1)
                    if lev:
                        pe.wait_ge(s_xc, i)
                    for m in range(4):
                        last = mm(ps[3][:, m * P:(m + 1) * P], nt[:, i % 2, m, :], xm[:, m, :], start=True, stop=True)
                    last.then_inc(s_y, 1)
                    pe.wait_ge(s_y1, i + 1)
                    if lev < LEVELS - 1:
                        for m in range(4):
                            mm(ps[1][:, m * P:(m + 1) * P], xt[:, m, :], y1[:, m, :], start=True, stop=True)
                    for m in range(4):
                        last = mm(ps[2][:, m * P:(m + 1) * P], y1[:, m, :], xt[:, m, :], start=True, stop=True)
                    last.then_inc(s_xx, 1)
                pe.wait_ge(s_xc, (hp + 1) * LEVELS)
                pe.wait_ge(s_gramc, 3 * hp + 3)
                pe.wait_ge(s_tvc, hp + 1)
                for c in range(2):
                    if c:
                        pe.wait_ge(s_uc, 2 * hp + 1)
                        pe.wait_ge(s_stc, hp + 1)
                    for e in range(2):
                        m = 2 * e + c
                        hd = slice(HD * e, HD * (e + 1))
                        last = mm(ps[6 + e][:, 0:HD], kr[:, m, 0:P], tv[:, 2 + c, hd], start=True, stop=(c == 0))
                        if c:
                            last = mm(ps[6 + e][:, 0:HD], op[half[e], 0, chunk[1]], s0[half[e], :], start=False, stop=True)
                    last.then_inc(s_u, 1)
                    pe.wait_ge(s_uc, 2 * hp + c + 1)
                    if c:
                        pe.wait_ge(s_sac, 2 * hp + 1)
                    for e in range(2):
                        last = mm(ps[3][:, e * HD:(e + 1) * HD], xt[:, 2 * e + c, :], us[:, e, :], start=True, stop=True)
                    last.then_inc(s_sa, 1)
                    pe.wait_ge(s_sac, 2 * hp + c + 1)
                    if c == 0:
                        for e in range(2):
                            hd = slice(HD * e, HD * (e + 1))
                            mm(ps[0][half[e], 0:HD], tv[:, 0, hd], sa[:, 0, e, :], start=True, stop=False)
                            last = mm(ps[0][half[e], 0:HD], tv[:, 1, hd], tv[:, 2, hd], start=False, stop=True)
                        last.then_inc(s_st, 1)
                for e in range(2):
                    hd = slice(HD * e, HD * (e + 1))
                    for c in range(2):
                        m = 2 * e + c
                        out = ps[1 + e][half[e], c * P:(c + 1) * P]
                        mm(out, sa[:, c, e, :], br[:, m, P:2 * P], start=True, stop=False)
                        last = mm(out, tv[:, 2 + c, hd], kr[:, m, P:2 * P], start=False, stop=(c == 0))
                        if c:
                            last = mm(out, s0[half[e], :], op[half[e], 1, chunk[1]], start=False, stop=True)
                last.then_inc(s_ot, 1)
                pe.wait_ge(s_otc, hp + 1)
                mm(ps[6][:, 0:T], ck(C_BLK), o_t[:], start=True, stop=True).then_inc(s_mean, 1)
                pe.wait_ge(s_dsq, hp + 1)
                pe.wait_ge(s_bon, hp + 1)
                mm(ps[7][:, 0:T], ck(C_BLK), sq[:], start=True, stop=True)
                mm(ps[3][:, 0:T], ck(C_BLK), rkv[:, hp, :], start=True, stop=True).then_inc(s_var, 1)
            pe.wait_ge(s_bonus, PAIRS)
            for hp in range(PAIRS):
                cols = slice(hp * P, (hp + 1) * P)
                b = 4 if hp % 2 == 0 else 6
                if hp >= 2:
                    pe.wait_ge(s_mixf, hp - 1)
                mm(ps[b][:, 0:T], w_g[:, cols], lora[:, 1, :], start=True, stop=False)
                mm(ps[b][:, 0:T], w_g2[96:128, cols], lora[96:128, 2, :], start=False, stop=True).then_inc(s_g, 1)

            def gate_rows(i, src):
                pe.wait_ge(s_diag, i + 1)
                if i:
                    pe.wait_ge(s_gtb, i)
                mm(ps[4][:, :], ones, src[:], start=True, stop=True).then_inc(s_gt, 1)

            pe.wait_ge(s_mixr, PAIRS)
            next_ada = [INIT_ADA + WIN_G * UPG // 2]
            cols_at = [next_ada[0] // UPG]
            for g in range(OUT_G):
                for ku in range(UPG):
                    n = N_OUT0 + g * UPG + ku
                    if g >= 2 and ku == 0:
                        pe.wait_ge(s_x1, 2 * (g - 1))
                    unit_tokens(n, UK * ku, KT, 2 * (g % 2), (mixa_hi, mixr_hi), (mixa_lo, mixr_lo))
                    next_ada[0] = min(END_ADA1, next_ada[0] + 2)
                    if ku == 3:
                        gate_rows(g, diag)
                    if ku in (2, 6):
                        while cols_at[0] < (next_ada[0] - 2) // UPG:
                            ada_fin(cols_at[0])
                            cols_at[0] += 1
            while cols_at[0] < END_ADA1 // UPG:
                ada_fin(cols_at[0])
                cols_at[0] += 1
            pe.wait_ge(s_xn2, NT)
            for b in range(8):
                if b >= 4:
                    pe.wait_ge(s_h2f, (b - 4) // 2 + 1)
                for kx in range(2):
                    for t in range(NT):
                        k = 2 * b + kx
                        last = nc.tensor.transpose(ps[b % 4][:, kx * T + t * P:kx * T + (t + 1) * P],
                                                   xn2[:, t, k * P:(k + 1) * P], ident)
                last.then_inc(s_x2t, 1)

            def gu_group(g, parity, j0, first):
                if not first:
                    pe.wait_ge(s_prod, g - 1)
                for m in range(2):
                    for ku in range(UPG):
                        pe.wait_ge(s_lo, g * (2 * UPG) + (N_GU0 + m * UPG + ku + 1))
                        for i in range(4):
                            for kx in range(UK):
                                k = UK * ku + kx
                                out = ps[4 * parity + 2 * m + i // 2][:, (i % 2) * T:(i % 2 + 1) * T]
                                w = slice(i * P, (i + 1) * P)
                                last = three_pass(out, w_hi[:, ku % RING, kx, w], w_lo[:, ku % RING, kx, w],
                                                  h_hi[:, k, :], h_lo[:, k, :], first=(k == 0 and i % 2 == 0),
                                                  last=(k == KT - 1), shared=True)
                        last.then_inc(s_used, 1)

            pe.wait_ge(s_h2lo, 4)
            pe.wait_ge(s_gtb, OUT_G)
            pe.wait_ge(s_col, END_ADA1 // UPG)
            gu_group(0, 0, 0, True)
            gu_group(1, 1, 0, True)
            gu_group(2, 0, 0, False)
            with pe.Fori(1, (GU_G - 1) // 2) as it:
                gu_group(it * 2 + 1, 1, 0, False)
                gu_group(it * 2 + 2, 0, 0, False)

            pe.wait_ge(s_prod, GU_G)
            for g in range(OUT_G):
                for ku in range(DOWN_U):
                    n = N_DOWN0 + g * DOWN_U + ku
                    if g >= 2 and ku == 0:
                        pe.wait_ge(s_x1, 2 * OUT_G + 2 * (g - 1))
                    if g == 0 and ku % 2 == 0:
                        pe.wait_ge(s_alo, ku // 2 + 1)
                    unit_tokens(n, UK * ku, FK, 2 * (g % 2), act_hi, act_lo)
                    if ku == DOWN_U - 5:
                        ada_fin(20 + g)
                    if ku == DOWN_U - 1:
                        gate_rows(OUT_G + g, diag2)


_INS = ["x", "c", "positions", "w_ada", "b_ada", "norm1_g", "norm2_g", "normf_g", "w_in", "w_out", "mu_shift", "w0",
        "w_decay_up", "a0", "w_iclr_up", "w_gate_up", "k_k", "k_a", "r_k", "gn_g", "gn_b", "w_ffn_gate", "w_ffn_up",
        "w_ffn_down"]


def kernel(**inputs):
    import concourse.bacc as bacc
    from concourse.bass_utils import run_bass_kernel_spmd as run

    nc = bacc.Bacc("TRN2", target_bir_lowering=False, num_devices=1)
    arrays, aps = {}, {}
    for name in _INS:
        x = np.ascontiguousarray(inputs[name])
        arrays[f"in_{name}"] = x
        aps[name] = nc.dram_tensor(f"in_{name}", x.shape, mybir.dt.from_np(x.dtype), kind="ExternalInput").ap()
    arrays["in_const"] = constants()
    aps["const"] = nc.dram_tensor("in_const", (P, NCONST), F32, kind="ExternalInput").ap()
    aps["out"] = nc.dram_tensor("out_0", (1, T, D), F32, kind="ExternalOutput").ap()
    build(nc, aps)
    r = run(nc, [arrays], core_ids=[0])
    return r.results[0]["out_0"]
```

```python
import math
from contextlib import ExitStack

import numpy as np

import concourse.bass as bass
from concourse import mybir

F32 = mybir.dt.float32
F32R = mybir.dt.float32r
I32 = mybir.dt.int32
ALU = mybir.AluOpType
ACT = mybir.ActivationFunctionType
AX = mybir.AxisListType.X

P = 128
T = 256
NT = T // P
D = 2048
KT = D // P
HD = 64
HEADS = 16
PAIRS = HEADS // 2
AW = 1024
IN_COLS = 3 * AW + 3 * AW + 288
FFN = 5632
FK = FFN // P
CW = 512
UK = 2
RING = 4
LAG = 3
UPG = KT // UK
WIN_G = 13
N_OUT0 = WIN_G * UPG
OUT_G = D // CW
N_GU0 = N_OUT0 + OUT_G * UPG
GU_G = FFN // CW
N_DOWN0 = N_GU0 + 2 * GU_G * UPG
DOWN_U = FK // UK
N_UNITS = N_DOWN0 + OUT_G * DOWN_U
LORA_W = 288
RMS_EPS = 1e-6
GN_EPS = HD * 1e-5
WAVES = PAIRS // 2
LEVELS = 6
SQ = math.exp(-0.5)

V_C, V_N1, V_N2, V_W0, V_A0, V_KK, V_KA, V_RK, V_GG, V_GB = 0, 16, 32, 48, 56, 64, 72, 80, 88, 96
V_B = 104
V_MU = 200
NVEC = 227

C_ID, C_ONE, C_BLK, C_PERM, C_LC, C_LEV, C_SI, C_M0, C_M0T, C_RES, C_INV = (
    0, 128, 256, 384, 512, 896, 896 + 768, 1920, 2048, 2176, 2432)
NCONST = 2433


def constants():
    c = np.zeros((P, NCONST), np.float32)
    i = np.arange(P)
    c[:, C_ID:C_ID + P] = np.eye(P)
    c[:, C_ONE:C_ONE + P] = 1.0
    c[:, C_BLK:C_BLK + P] = (i[:, None] // HD == i[None, :] // HD)
    for h in (0, HD):
        for d in range(8):
            c[h + d + 8, C_PERM + h + d] = -1.0
            c[h + d, C_PERM + h + d + 8] = 1.0
    t = np.arange(T)[:, None]
    j = np.arange(T)[None, :]
    count = (((t - j) >= 0) & ((t - j) <= 128)).astype(np.float64)
    for dil in (4, 16):
        count += (j <= t) & ((t - j) % dil == 0) & ((t - j) <= 128 * dil)
    lc = np.where(count > 0, np.log(np.maximum(count, 1)), -1e30).astype(np.float32)
    c[:, C_LC:C_LC + P] = lc[:P, :P]
    c[:, C_LC + P:C_LC + 3 * P] = lc[P:, :]
    s, u = i[:, None], i[None, :]
    for lev in range(1, LEVELS + 1):
        b = 2 ** lev
        c[:, C_LEV + P * (lev - 1):C_LEV + P * lev] = (s // b == u // b + 1) & (u // b % 2 == 0)
    c[:, C_SI:C_SI + P] = s < u
    c[:, C_SI + P:C_SI + 2 * P] = s <= u
    c[:, C_M0:C_M0 + P] = (s == u + 1) & (u % 2 == 0)
    c[:, C_M0T:C_M0T + P] = (u == s + 1) & (s % 2 == 0)
    c[:, C_RES:C_RES + T] = (np.arange(T) % 64 != 0)
    rot = 16
    inv = (np.float32(500000.0) ** (-np.arange(0, rot, 2, dtype=np.float32) / np.float32(rot))).astype(np.float32)
    for h in (0, HD):
        for d in range(rot):
            c[h + d, C_INV] = inv[d % 8]
    return c


def slot_of(n):
    return n % RING


def build(nc, a):
    ctx = ExitStack()
    with ctx:
        def sem(name):
            return ctx.enter_context(nc.semaphore(name))

        top = [nc.sbuf_base + 31 - (nc.sbuf_base + 31) % 32]

        def fixed(name, shape, dt=F32):
            size = 4 * int(np.prod(shape[1:]))
            t = nc.alloc_sbuf_tensor_at(name, shape, dt, offset=top[0])
            top[0] += -(-size // 32) * 32
            return t

        raw = fixed("raw", [P, RING, UK, CW])
        split_off = top[0]
        w_hi = fixed("w_hi", [P, RING, UK, CW], F32R)
        w_lo = fixed("w_lo", [P, RING, UK, CW], F32R)
        idone = fixed("idone", [P, 2 * P])
        vec = fixed("vec", [P, NVEC])
        ada_t = fixed("ada_t", [P, 96])
        scale1 = fixed("scale1", [P, KT])
        scale2 = fixed("scale2", [P, KT])
        silu_c = fixed("silu_c", [P, KT])
        sig_c = fixed("sig_c", [P, KT])
        acc = fixed("acc", [P, 2, CW])
        stat = fixed("stat", [P, 32])
        rnc = fixed("rnc", [P, 4 * PAIRS])
        varc = fixed("varc", [P, 4 * PAIRS])
        base = top[0]
        end = nc.sbuf_usable_end

        def at(name, offset, shape, dt=F32):
            size = 4 * int(np.prod(shape[1:]))
            assert base + offset + size <= end, (name, base, offset, size, end)
            return nc.alloc_sbuf_tensor_at(name, shape, dt, offset=base + offset)

        ident = idone[:, 0:P]
        ones = idone[:, P:2 * P]

        KB = 1024
        h_hi = at("h_hi", 0, [P, KT, T], F32R)
        h_lo = at("h_lo", 16 * KB, [P, KT, T], F32R)
        o = 32 * KB
        cst = at("cst", o, [P, NCONST - 256]); o += 4 * NCONST - 1024 + 28
        o = -(-o // 32) * 32
        cosT = at("cosT", o, [P, T]); o += KB
        sinT = at("sinT", o, [P, T]); o += KB
        ada_raw = at("ada_raw", o, [P, RING, UK, CW]); o += 16 * KB
        w_di = at("w_di", o, [P, AW]); o += 4 * KB
        w_g = at("w_g", o, [P, AW]); o += 4 * KB
        w_g2 = at("w_g2", o, [P, AW]); o += 4 * KB
        rkv_off = o
        rkv = at("rkv", o, [P, 24, T]); o += 24 * KB
        lora = at("lora", o, [P, 3, T]); o += 3 * KB
        mixa_hi = at("mixa_hi", o, [P, 8, T], F32R); o += 8 * KB
        mixa_lo = at("mixa_lo", o, [P, 8, T], F32R); o += 8 * KB
        qkv_off = o
        qk = at("qk", o, [P, 16, T]); o += 16 * KB
        v_tok = at("v_tok", o, [P, NT, AW]); o += 8 * KB
        tmp_off = o
        ybuf = at("ybuf", o, [P, 4, T + 1]); o += 4 * 4 * (T + 1)
        o = -(-o // 32) * 32
        qraw = at("qraw", o, [P, 4, T])
        t1 = at("t1", o + 4 * KB, [P, 2, T])
        prob = at("prob", o, [P, 3, P]); o += 1536
        prob_t = at("prob_t", o, [P, 3, P]); o += 1536
        x_in = at("x_in", rkv_off, [P, NT, D])
        xn_t = at("xn_t", qkv_off, [P, KT, T])
        vrows = at("vrows", tmp_off, [P, 3, P])
        pos_i = at("pos_i", rkv_off + 16 * KB, [P, T], I32)
        ang = at("ang", rkv_off + 17 * KB, [P, T])
        turns = at("turns", rkv_off + 18 * KB, [P, T])

        class Side:
            pass

        sides = []
        for i, start in enumerate((base, split_off)):
            sd = Side()
            put = [start]

            def room(name, shape):
                t = nc.alloc_sbuf_tensor_at(f"{name}_{i}", shape, F32, offset=put[0])
                put[0] += 4 * int(np.prod(shape[1:]))
                return t

            sd.op = room("op", [P, 4, T])
            sd.br = room("br", [P, 4, 2 * P])
            sd.kr = room("kr", [P, 4, 2 * P])
            sd.xm = room("xm", [P, 4, P])
            sd.xt = room("xt", [P, 4, P])
            sd.y1 = room("y1", [P, LEVELS, 4, P])
            sd.tv = room("tv", [P, 4, P])
            sd.us = room("us", [P, 2, HD])
            sd.s0 = room("s0", [P, HD])
            sd.sa = room("sa", [P, 2, 2, HD])
            sd.refc = room("refc", [P, 2, 4])
            assert put[0] <= start + 32 * KB
            put[0] = base + qkv_off + (24 + 7 * i) * KB
            sd.e3 = room("e3", [P, 3, T])
            sd.cen = room("cen", [P, 2, T])
            sd.o_t = room("o_t", [P, T])
            sd.sq = room("sq", [P, T])
            assert put[0] <= end
            sd.bank = (0, 1, 2) if i == 0 else (3, 4, 6)
            sides.append(sd)
        lw = at("lw", qkv_off, [P, PAIRS, T])
        ab = at("ab", qkv_off + 8 * KB, [P, PAIRS, T])
        kk = at("kk", qkv_off + 16 * KB, [P, PAIRS, T])
        mixr_hi = at("mixr_hi", 0, [P, 8, T], F32R)
        mixr_lo = at("mixr_lo", 8 * KB, [P, 8, T], F32R)

        act_hi = at("act_hi", 32 * KB, [P, FK, T], F32R)
        act_lo = at("act_lo", 32 * KB + 44 * KB, [P, FK, T], F32R)
        x1 = at("x1", 120 * KB, [P, NT, D])
        sg = at("sg", 136 * KB, [P, 2, 4, T])
        xn2 = at("xn2", rkv_off, [P, NT, D])
        gtb = at("gtb", 136 * KB, [P, CW])
        diag = at("diag", 138 * KB, [P, CW])
        upd = at("upd", 140 * KB, [P, CW])
        h2f = at("h2f", 136 * KB, [P, 2, 4, T])
        ada_raw2 = at("ada_raw2", 0, [P, RING, UK, CW])
        nf_b = at("nf_b", 16 * KB, [P, D])
        gtb2 = at("gtb2", 24 * KB, [P, CW])
        diag2 = at("diag2", 26 * KB, [P, CW])
        upd2 = at("upd2", 28 * KB, [P, CW])
        sqj = at("sqj", 30 * KB, [P, CW])
        sqj1 = at("sqj1", 142 * KB, [P, CW])

        ps = [ctx.enter_context(nc.psum_tensor(f"bank{b}", [P, 512], F32)) for b in range(8)]
        FIN = 5

        def ck(col, n=P):
            return cst[:, col - 256:col - 256 + n]

        def v1(col):
            return vec[:, col:col + 1]

        def four(bank):
            return ps[bank][:, :].rearrange("p (m t) -> p m t", m=4)

        def blocks(x, b, odd):
            return x.rearrange("p m (n two b) -> p m n two b", two=2, b=b)[:, :, :, odd, :]

        def over4(x):
            return x.unsqueeze(1).broadcast_to([P, 4, x.shape[1]])

        s_cst, s_rows, s_x, s_pos, s_small, s_v0 = map(sem, ("s_cst", "s_rows", "s_x", "s_pos", "s_small", "s_v0"))
        s_raw = [sem(f"s_raw{i}") for i in range(RING)]
        s_hi, s_lo, s_used = sem("s_hi"), sem("s_lo"), sem("s_used")
        s_ada = [sem(f"s_ada{i}") for i in range(RING)]
        s_adaused, s_fin, s_col = map(sem, ("s_adaused", "s_fin", "s_col"))
        s_vt, s_vec, s_sigc, s_siluc = map(sem, ("s_vt", "s_vec", "s_sigc", "s_siluc"))
        s_ss, s_ms, s_rt, s_xn, s_xt, s_xnt = map(sem, ("s_ss", "s_ms", "s_rt", "s_xn", "s_xt", "s_xnt"))
        s_hf, s_hhi, s_hlo = map(sem, ("s_hf", "s_hhi", "s_hlo"))
        s_trig, s_sin = sem("s_trig"), sem("s_sin")
        s_evac, s_perm, s_rope = sem("s_evac"), sem("s_perm"), sem("s_rope")
        s_shift, s_lora = sem("s_shift"), sem("s_lora")
        s_score, s_masked, s_exp, s_prob, s_pt, s_ptc, s_o, s_ohi, s_mixa = map(
            sem, ("s_score", "s_masked", "s_exp", "s_prob", "s_pt", "s_ptc", "s_o", "s_ohi", "s_mixa"))
        s_zw, s_sigs, s_kkr, s_sqk, s_ssq, s_rnr, s_rns, s_rnc, s_rnb, s_pre, s_lwr = map(
            sem, ("s_zw", "s_sigs", "s_kkr", "s_sqk", "s_ssq", "s_rnr", "s_rns", "s_rnc", "s_rnb", "s_pre", "s_lwr"))
        for i, sd in enumerate(sides):
            (sd.s_cen, sd.s_e3, sd.s_op, sd.s_gram, sd.s_gramc, sd.s_krg, sd.s_krc, sd.s_y, sd.s_y1, sd.s_xx, sd.s_xm,
             sd.s_xt, sd.s_tv, sd.s_tvc, sd.s_eye, sd.s_u, sd.s_uc, sd.s_sa, sd.s_sac, sd.s_st, sd.s_stc, sd.s_ot,
             sd.s_otc, sd.s_mean, sd.s_dev, sd.s_dsq, sd.s_bon, sd.s_var, sd.s_bonus) = [sem(f"s_{name}_{i}") for name in (
                 "cen", "e3", "op", "gram", "gramc", "krg", "krc", "y", "y1", "xx", "xm", "xt", "tv", "tvc", "eye", "u",
                 "uc", "sa", "sac", "st", "stc", "ot", "otc", "mean", "dev", "dsq", "bon", "var", "bonus")]
        s_sd, s_rstd, s_g, s_mixf, s_mrhi, s_mixr = map(
            sem, ("s_sd", "s_rstd", "s_g", "s_mixf", "s_mrhi", "s_mixr"))
        s_x1in, s_diag, s_gt, s_gtb, s_x1, s_ssp, s_ms2, s_rt2, s_xn2, s_x2t, s_h2f, s_h2hi, s_h2lo = map(
            sem, ("s_x1in", "s_diag", "s_gt", "s_gtb", "s_x1", "s_ssp", "s_ms2", "s_rt2", "s_xn2", "s_x2t",
                  "s_h2f", "s_h2hi", "s_h2lo"))
        s_silu, s_prod, s_ahi, s_alo, s_nf, s_fs, s_out = map(
            sem, ("s_silu", "s_prod", "s_ahi", "s_alo", "s_nf", "s_fs", "s_out"))
        s_dch = sem("s_dch")

        w_in = a["w_in"].rearrange("l (k p) n -> p (l k) n", p=P)
        w_out = a["w_out"].rearrange("l (k p) n -> p (l k) n", p=P)
        w_gate = a["w_ffn_gate"].rearrange("l (k p) n -> p (l k) n", p=P)
        w_up = a["w_ffn_up"].rearrange("l (k p) n -> p (l k) n", p=P)
        w_down = a["w_ffn_down"].rearrange("l (k p) n -> p (l k) n", p=P)
        w_ada = a["w_ada"].rearrange("l (k p) n -> p (l k) n", p=P)
        x_dram = a["x"].rearrange("b (t p) d -> p (b t) d", p=P)
        out_dram = a["out"].rearrange("b (t p) d -> p (b t) d", p=P)

        INIT_ADA = 8 * UPG
        END_ADA1 = 20 * UPG

        STEPS = (["gram", "keys", "y", "x", "tokens"] + ["y", "x"] * (LEVELS - 1)
                 + ["u", "solve", "state", "u", "solve", "out", "mean", "var"])
        turns_of = []
        BEHIND = 12
        for slot in range(WAVES * len(STEPS) + BEHIND):
            for i in range(2):
                at_step = slot - BEHIND * i
                if 0 <= at_step < WAVES * len(STEPS):
                    w, j = divmod(at_step, len(STEPS))
                    turns_of.append((slot, w, i, STEPS[j], STEPS[:j].count(STEPS[j])))
        FIN_SLOT = [15 + len(STEPS) * w for w in range(WAVES)]
        RWKV_ADA_END = INIT_ADA + WIN_G * UPG // 2 + 8 * WAVES

        ada_order = [g for j in range(4) for g in (j, 4 + j)] + list(range(8, 24))

        block = ctx.enter_context(nc.Block())

        @block.sync
        def _(sp):
            sp.dma_start(idone[:], a["const"][:, 0:256]).then_inc(s_cst, 16)
            rows = 0
            for name, n in (("c", 16), ("norm1_g", 16), ("norm2_g", 16), ("w0", 8), ("a0", 8), ("k_k", 8),
                            ("k_a", 8), ("r_k", 8), ("gn_g", 8), ("gn_b", 8)):
                flat = a[name].rearrange("a b c -> (a b c)") if name == "r_k" else a[name].rearrange("a b -> (a b)")
                sp.dma_start(vrows[rows:rows + n, 0, :], flat.rearrange("(r q) -> r q", q=P)).then_inc(s_rows, 16)
                rows += n
            sp.dma_start(vrows[0:96, 1, :], a["b_ada"].rearrange("l (r q) -> (l r) q", q=P)).then_inc(s_rows, 16)
            mu = a["mu_shift"].rearrange("a b -> (a b)")
            sp.dma_start(vrows[0:26, 2, :], mu[0:26 * P].rearrange("(r q) -> r q", q=P)).then_inc(s_rows, 16)
            sp.dma_start(vrows[26:27, 2, :], mu[3232:3360].rearrange("(r q) -> r q", q=P)).then_inc(s_rows, 16)
            for t in range(NT):
                sp.dma_start(x_in[:, t, :], x_dram[:, t, :]).then_inc(s_x, 16)
            sp.dma_start(pos_i[:], a["positions"].partition_broadcast(P).rearrange("p a b -> p (a b)")).then_inc(s_pos, 16)
            sp.dma_start(cst[:], a["const"][:, 256:NCONST]).then_inc(s_small, 16)
            sp.dma_start(w_di[0:64, :], a["w_decay_up"][0]).then_inc(s_small, 16)
            sp.dma_start(w_di[64:128, :], a["w_iclr_up"][0]).then_inc(s_small, 16)
            sp.dma_start(w_g[:], a["w_gate_up"][0, 0:128, :]).then_inc(s_small, 16)
            sp.dma_start(w_g2[96:128, :], a["w_gate_up"][0, 128:160, :]).then_inc(s_small, 16)

            for ku in range(UPG):
                if ku >= RING:
                    sp.wait_ge(s_lo, ku - RING + 1)
                sp.dma_start(raw[:, slot_of(ku)], w_in[:, UK * ku:UK * ku + UK, 0:CW]).then_inc(s_raw[slot_of(ku)], 16)
            with sp.Fori(1, WIN_G - 1) as g:
                for ku in range(UPG):
                    sp.wait_ge(s_lo, g * UPG + (ku - RING + 1))
                    sp.dma_start(raw[:, slot_of(ku)],
                                 w_in[:, UK * ku:UK * ku + UK, bass.ts(g, CW)]).then_inc(s_raw[slot_of(ku)], 16)
            for ku in range(UPG):
                sp.wait_ge(s_lo, (WIN_G - 1) * UPG + ku - RING + 1)
                sp.dma_start(raw[:, slot_of(ku), :, 0:LORA_W],
                             w_in[:, UK * ku:UK * ku + UK, 6 * AW:6 * AW + LORA_W]).then_inc(s_raw[slot_of(ku)], 16)
            with sp.Fori(0, OUT_G) as g:
                for ku in range(UPG):
                    sp.wait_ge(s_lo, g * UPG + (N_OUT0 + ku - RING + 1))
                    sp.dma_start(raw[:, slot_of(ku)],
                                 w_out[:, UK * ku:UK * ku + UK, bass.ts(g, CW)]).then_inc(s_raw[slot_of(ku)], 16)
            with sp.Fori(0, GU_G) as g:
                for m, w in enumerate((w_gate, w_up)):
                    for ku in range(UPG):
                        sp.wait_ge(s_lo, g * (2 * UPG) + (N_GU0 + m * UPG + ku - RING + 1))
                        sp.dma_start(raw[:, slot_of(ku)],
                                     w[:, UK * ku:UK * ku + UK, bass.ts(g, CW)]).then_inc(s_raw[slot_of(ku)], 16)
            with sp.Fori(0, OUT_G // 2) as g:
                for m in range(2):
                    for ku in range(DOWN_U):
                        j = m * DOWN_U + ku
                        sp.wait_ge(s_lo, g * (2 * DOWN_U) + (N_DOWN0 + j - RING + 1))
                        sp.dma_start(raw[:, slot_of(j)],
                                     w_down[:, UK * ku:UK * ku + UK, bass.ds(g * (2 * CW) + m * CW, CW)]
                                     ).then_inc(s_raw[slot_of(j)], 16)
            for t in range(NT):
                sp.wait_ge(s_fs, t + 1)
                sp.dma_start(out_dram[:, t, :], x1[:, t, :]).then_inc(s_out, 16)
            sp.wait_ge(s_out, 16 * NT)

        @block.gpsimd
        def _(pool):
            for u in range(INIT_ADA):
                g, ku = ada_order[u // UPG], u % UPG
                if u >= RING:
                    pool.wait_ge(s_adaused, u - RING + 1)
                pool.dma_start(ada_raw[:, u % RING],
                               w_ada[:, UK * ku:UK * ku + UK, g * CW:(g + 1) * CW]).then_inc(s_ada[u % RING], 16)
            def ada_group(g):
                for ku in range(UPG):
                    pool.wait_ge(s_adaused, g * UPG + (ku - RING + 1))
                    pool.dma_start(ada_raw[:, ku % RING],
                                   w_ada[:, UK * ku:UK * ku + UK, bass.ds(g * CW, CW)]
                                   ).then_inc(s_ada[ku % RING], 16)

            with pool.Fori(8, 20) as g:
                ada_group(g)
            pool.wait_ge(s_used, N_DOWN0)
            with pool.Fori(0, 4) as g:
                for ku in range(UPG):
                    pool.wait_ge(s_adaused, g * UPG + (END_ADA1 + ku - RING + 1))
                    pool.dma_start(ada_raw2[:, ku % RING],
                                   w_ada[:, UK * ku:UK * ku + UK, bass.ds(g * CW + 20 * CW, CW)]
                                   ).then_inc(s_ada[ku % RING], 16)
            pool.dma_start(nf_b[:], a["normf_g"].partition_broadcast(P)).then_inc(s_nf, 16)

        @block.scalar
        def _(act):
            def round_unit(n, width=CW):
                act.wait_ge(s_raw[slot_of(n)], 16 * (n // RING + 1))
                if n >= RING:
                    act.wait_ge(s_used, n - RING + 1)
                nc.scalar.activation(w_hi[:, slot_of(n), :, 0:width], raw[:, slot_of(n), :, 0:width],
                                     ACT.Copy).then_inc(s_hi, 1)

            act.wait_ge(s_vt, 1)
            nc.scalar.activation(vec[:], ps[4][:, 0:NVEC], ACT.Copy).then_inc(s_vec, 1)
            act.wait_ge(s_vec, 1)
            nc.scalar.activation(sig_c[:], vec[:, V_C:V_C + KT], ACT.Sigmoid).then_inc(s_sigc, 1)
            for t in range(NT):
                act.wait_ge(s_x, 16 * NT)
                nc.scalar.activation(xn_t[:, 8 * t:8 * t + 8, :].rearrange("p k t -> p (k t)"), x_in[:, t, :], ACT.Square,
                                     accum_out=stat[:, t:t + 1]).then_inc(s_ss, 1)
            act.wait_ge(s_ms, 1)
            nc.scalar.activation(stat[:, 4:6], stat[:, 2:4], ACT.Sqrt).then_inc(s_rt, 1)
            for b in range(8):
                act.wait_ge(s_xt, b + 1)
                nc.scalar.activation(xn_t[:, 2 * b:2 * b + 2, :], ps[b][:, :].rearrange("p (k t) -> p k t", k=2),
                                     ACT.Copy).then_inc(s_xnt, 1)
            act.wait_ge(s_trig, 1)
            nc.scalar.activation(sinT[:], ang[:], ACT.Sin)
            nc.scalar.activation(cosT[:], turns[:], ACT.Sin).then_inc(s_sin, 1)
            for n in range(RING):
                round_unit(n)
            for j in range(4):
                act.wait_ge(s_hf, j + 1)
                nc.scalar.activation(h_hi[:, 4 * j:4 * j + 4, :], xn_t[:, 4 * j:4 * j + 4, :], ACT.Copy).then_inc(s_hhi, 1)

            def win_epilogue(gi):
                pb = 2 * (gi % 2)
                act.wait_ge(s_used, UPG * (gi + 1))
                if gi < 4:
                    if gi:
                        act.wait_ge(s_rope, 2 * gi)
                    for b in range(2):
                        last = nc.scalar.activation(qraw[:, 2 * b:2 * b + 2, :],
                                                    ps[pb + b][:, :].rearrange("p (k t) -> p k t", k=2), ACT.Copy)
                elif gi < 6:
                    for t in range(NT):
                        last = nc.scalar.activation(v_tok[:, t, CW * (gi - 4):CW * (gi - 3)], ps[pb + t][:, :], ACT.Copy)
                else:
                    if gi == 6:
                        act.wait_ge(s_v0, 1)
                    else:
                        act.wait_ge(s_shift, gi - 6)
                    for b in range(2 if gi < 12 else 1):
                        last = nc.scalar.activation(ybuf[:, 2 * b:2 * b + 2, 1:T + 1],
                                                    ps[pb + b][:, :].rearrange("p (k t) -> p k t", k=2), ACT.Copy)
                    if gi == 12:
                        last = nc.scalar.activation(ybuf[:, 2, 1:T + 1], ps[pb + 1][:, 0:T], ACT.Copy)
                last.then_inc(s_evac, 1)

            def attn_exp(h):
                act.wait_ge(s_masked, h + 1)
                nc.scalar.activation(prob[:, 0, :], prob[:, 0, :], ACT.Exp, bias=stat[:, 6:7],
                                     accum_out=stat[:, 8:9])
                nc.scalar.activation(prob[:, 1:3, :], prob[:, 1:3, :], ACT.Exp, bias=stat[:, 7:8],
                                     accum_out=stat[:, 9:10]).then_inc(s_exp, 1)

            def attn_copy_pt(h):
                act.wait_ge(s_pt, h + 1)
                if h:
                    act.wait_ge(s_o, h)
                nc.scalar.activation(prob_t[:], ps[6][:, 0:3 * P].rearrange("p (k t) -> p k t", k=3),
                                     ACT.Copy).then_inc(s_ptc, 1)

            def attn_out(hp):
                act.wait_ge(s_o, 2 * hp + 2)
                nc.scalar.activation(mixa_hi[:, hp, :], ps[7][:, 0:T], ACT.Copy).then_inc(s_ohi, 1)

            def attn_slot(i):
                if 2 <= i < HEADS + 2 and i % 2 == 1:
                    attn_out((i - 3) // 2)
                if 1 <= i < HEADS + 1:
                    attn_copy_pt(i - 1)
                if i < HEADS:
                    attn_exp(i)

            for gi in range(WIN_G):
                for ku in range(UPG):
                    n = gi * UPG + ku
                    if n >= RING:
                        round_unit(n, LORA_W if gi == WIN_G - 1 else CW)
                    if gi and ku == 2:
                        win_epilogue(gi - 1)
                    u = n - 6 * UPG - 4 - LAG
                    if u >= 0 and u % 2 == 0 and u // 2 < HEADS + 2:
                        attn_slot(u // 2)
            win_epilogue(WIN_G - 1)

            act.wait_ge(s_lora, 1)
            nc.scalar.activation(lora[0:64, 0, :], lora[0:64, 0, :], ACT.Tanh)
            nc.scalar.activation(lora[:, 1, :], lora[:, 1, :], ACT.Sigmoid)
            nc.scalar.activation(lora[96:128, 2, :], lora[96:128, 2, :], ACT.Sigmoid).then_inc(s_lora, 1)
            for hp in range(PAIRS):
                sq = sides[hp % 2].sq
                act.wait_ge(s_kkr, hp + 1)
                if hp >= 2:
                    act.wait_ge(s_ssq, hp - 1)
                nc.scalar.activation(sq[:], kk[:, hp, :], ACT.Square).then_inc(s_sqk, 1)
                act.wait_ge(s_zw, hp + 1)
                zb, ab_b = (4, 6) if hp % 2 == 0 else (2, 3)
                nc.scalar.activation(lw[:, hp, :], ps[zb][:, 0:T], ACT.Sigmoid, bias=v1(V_W0 + hp))
                nc.scalar.activation(ab[:, hp, :], ps[ab_b][:, 0:T], ACT.Sigmoid, bias=v1(V_A0 + hp)).then_inc(s_sigs, 1)
            act.wait_ge(s_ssq, PAIRS)
            nc.scalar.activation(rnc[:], ps[7][:, 0:4 * PAIRS], ACT.Sqrt).then_inc(s_rns, 1)

            def pair_exps(w, sd):
                act.wait_ge(sd.s_cen, w + 1)
                if w:
                    act.wait_ge(sd.s_op, w)
                nc.scalar.activation(sd.e3[:, 0, :], sd.cen[:, 0, :], ACT.Exp)
                nc.scalar.activation(sd.e3[:, 1, :], sd.cen[:, 0, :], ACT.Exp, scale=-1.0)
                nc.scalar.activation(sd.e3[:, 2, :], sd.cen[:, 1, :], ACT.Exp)
                nc.scalar.activation(sd.refc[:, w % 2, 3:4], sd.refc[:, w % 2, 2:3], ACT.Exp).then_inc(sd.s_e3, 1)

            def set_identity(sd):
                nc.scalar.activation(sd.xm[:], over4(ident), ACT.Copy)
                nc.scalar.activation(sd.xt[:], over4(ident), ACT.Copy).then_inc(sd.s_eye, 1)

            for sd in sides:
                pair_exps(0, sd)
                set_identity(sd)

            for slot, w, i, step, nth in turns_of:
                sd, hp = sides[i], 2 * w + i
                if step == "x":
                    lev, b = nth, 2 << nth
                    act.wait_ge(sd.s_xx, w * LEVELS + lev + 1)
                    if lev < LEVELS - 1:
                        nc.scalar.activation(blocks(sd.xm[:], b, 0), blocks(four(sd.bank[1]), b, 0), ACT.Copy).then_inc(sd.s_xm, 1)
                    nc.scalar.activation(blocks(sd.xt[:], b, 1), blocks(four(sd.bank[2]), b, 1), ACT.Copy).then_inc(sd.s_xt, 1)
                elif step == "tokens":
                    act.wait_ge(sd.s_tv, w + 1)
                    nc.scalar.activation(sd.tv[:], four(7), ACT.Copy).then_inc(sd.s_tvc, 1)
                elif step == "u":
                    act.wait_ge(sd.s_u, 2 * w + nth + 1)
                    nc.scalar.activation(sd.us[:, 0, :], ps[sd.bank[0]][:, 0:HD], ACT.Copy)
                    nc.scalar.activation(sd.us[:, 1, :], ps[sd.bank[1]][:, 0:HD], ACT.Copy).then_inc(sd.s_uc, 1)
                elif step == "solve":
                    act.wait_ge(sd.s_sa, 2 * w + nth + 1)
                    nc.scalar.activation(sd.sa[:, nth], ps[sd.bank[2]][:, 0:2 * HD].rearrange("p (e d) -> p e d", e=2),
                                         ACT.Copy).then_inc(sd.s_sac, 1)
                elif step == "state":
                    act.wait_ge(sd.s_st, w + 1)
                    nc.scalar.activation(sd.s0[:], ps[sd.bank[2]][:, 2 * HD:3 * HD], ACT.Copy,
                                         scale=sd.refc[:, w % 2, 3:4]).then_inc(sd.s_stc, 1)
                    if w + 1 < WAVES:
                        pair_exps(w + 1, sd)
                elif step == "out":
                    act.wait_ge(sd.s_ot, w + 1)
                    nc.scalar.activation(sd.o_t[0:64, :], ps[sd.bank[0]][0:64, 0:T], ACT.Copy)
                    nc.scalar.activation(sd.o_t[64:128, :], ps[sd.bank[1]][64:128, 0:T], ACT.Copy).then_inc(sd.s_otc, 1)
                    if w + 1 < WAVES:
                        set_identity(sd)
                elif step == "mean":
                    act.wait_ge(sd.s_dev, w + 1)
                    nc.scalar.activation(sd.sq[:], lw[:, hp, :], ACT.Square).then_inc(sd.s_dsq, 1)
            for sd in sides:
                act.wait_ge(sd.s_bonus, WAVES)
            nc.scalar.activation(varc[:], varc[:], ACT.Sqrt).then_inc(s_sd, 1)
            for hp in range(PAIRS):
                act.wait_ge(s_mixf, hp + 1)
                nc.scalar.activation(mixr_hi[:, hp, :], lw[:, hp, :], ACT.Copy).then_inc(s_mrhi, 1)

            act.wait_ge(s_mixr, PAIRS)
            act.dma_start(x1[:], x_dram).then_inc(s_x1in, 16)

            def gate_copy(i, dst):
                act.wait_ge(s_gt, i + 1)
                if i:
                    act.wait_ge(s_x1, 2 * i)
                nc.scalar.activation(dst[:], ps[4][:, :], ACT.Copy).then_inc(s_gtb, 1)

            def square_sums(i, junk):
                ct = i % 4
                for t in range(NT):
                    act.wait_ge(s_x1, 2 * i + t + 1)
                    if i or t:
                        act.wait_ge(s_ssp, 2 * i + t)
                    ins = nc.scalar.activation(junk[:], x1[:, t, ct * CW:(ct + 1) * CW], ACT.Square,
                                               accum_out=stat[:, 10 + 4 * t + ct:11 + 4 * t + ct])
                    ins.then_inc(s_ssp, 1)

            for g in range(OUT_G):
                for ku in range(UPG):
                    round_unit(N_OUT0 + g * UPG + ku)
                    if g and ku == 2:
                        gate_copy(g - 1, gtb)
                    if g and ku == 4:
                        square_sums(g - 1, sqj1)
            gate_copy(OUT_G - 1, gtb)
            square_sums(OUT_G - 1, sqj1)
            act.wait_ge(s_ms2, 1)
            nc.scalar.activation(stat[:, 4:6], stat[:, 2:4], ACT.Sqrt).then_inc(s_rt2, 1)
            for n in range(RING):
                round_unit(N_GU0 + n)
            for j in range(4):
                act.wait_ge(s_h2f, j + 1)
                nc.scalar.activation(h_hi[:, 4 * j:4 * j + 4, :], h2f[:, j % 2], ACT.Copy).then_inc(s_h2hi, 1)

            def ffn_silu(gn, parity):
                act.wait_ge(s_used, gn * (2 * UPG) + (N_GU0 + 2 * UPG))
                for b in range(2):
                    last = nc.scalar.activation(sg[:, parity, 2 * b:2 * b + 2, :],
                                                ps[4 * parity + b][:, :].rearrange("p (k t) -> p k t", k=2), ACT.Silu)
                last.then_inc(s_silu, 1)

            def ffn_hi(gn, parity):
                act.wait_ge(s_prod, gn + 1)
                nc.scalar.activation(act_hi[:, bass.ds(gn * 4, 4), :], sg[:, parity], ACT.Copy).then_inc(s_ahi, 1)

            def round_gu(it, j):
                act.wait_ge(s_raw[j % RING], it * (2 * UPG // RING * 16) + 16 * ((N_GU0 + j) // RING + 1))
                act.wait_ge(s_used, it * (2 * UPG) + (N_GU0 + j - RING + 1))
                nc.scalar.activation(w_hi[:, j % RING], raw[:, j % RING], ACT.Copy).then_inc(s_hi, 1)

            for j in range(RING, 2 * UPG):
                round_gu(0, j)
            with act.Fori(0, (GU_G - 1) // 2) as it:
                for half in range(2):
                    for j in range(2 * UPG):
                        round_gu(it * 2, 2 * UPG * (1 + half) + j)
                        if j == 2:
                            ffn_silu(it * 2 + half, half)
                        if j == 5:
                            ffn_hi(it * 2 + half, half)
            ffn_silu(GU_G - 1, 0)
            for n in range(N_DOWN0, N_DOWN0 + 2):
                round_unit(n)
            ffn_hi(GU_G - 1, 0)
            for g in range(OUT_G):
                for ku in range(DOWN_U):
                    n = N_DOWN0 + g * DOWN_U + ku
                    if n >= N_DOWN0 + 2:
                        round_unit(n)
                    if g and ku == 2:
                        gate_copy(OUT_G + g - 1, gtb2)
                    if g and ku == 4:
                        square_sums(OUT_G + g - 1, sqj)
            gate_copy(2 * OUT_G - 1, gtb2)
            square_sums(2 * OUT_G - 1, sqj)
            act.wait_ge(s_ms2, 2)
            nc.scalar.activation(stat[:, 4:6], stat[:, 2:4], ACT.Sqrt).then_inc(s_rt2, 1)

        @block.vector
        def _(dve):
            links = [0]

            def link(ins):
                links[0] += 1
                ins.then_inc(s_dch, 1)
                dve.wait_ge(s_dch, links[0])

            def rest_unit(n, width=CW):
                dve.wait_ge(s_hi, n + 1)
                nc.vector.tensor_tensor(w_lo[:, slot_of(n), :, 0:width], raw[:, slot_of(n), :, 0:width],
                                        w_hi[:, slot_of(n), :, 0:width].bitcast(F32), ALU.subtract).then_inc(s_lo, 1)

            def ada_unit(u):
                g, ku = u // UPG, u % UPG
                buf = ada_raw2 if u >= END_ADA1 else ada_raw
                dve.wait_ge(s_ada[u % RING], 16 * (u // RING + 1))
                if ku == 0 and g >= 2:
                    dve.wait_ge(s_fin, g - 1)
                dst = acc[:, g % 2, :]
                for kx in range(UK):
                    k = UK * ku + kx
                    if k == 0:
                        link(nc.vector.tensor_scalar(dst, buf[:, u % RING, kx, :], silu_c[:, k:k + 1], None, ALU.mult))
                    elif kx == 0:
                        link(nc.vector.scalar_tensor_tensor(dst, buf[:, u % RING, kx, :], silu_c[:, k:k + 1], dst,
                                                            ALU.mult, ALU.add))
                    else:
                        nc.vector.scalar_tensor_tensor(dst, buf[:, u % RING, kx, :], silu_c[:, k:k + 1], dst,
                                                       ALU.mult, ALU.add).then_inc(s_adaused, 1)
                dve.wait_ge(s_adaused, u + 1)

            def ada_cols(g):
                c = 4 * ada_order[g]
                dve.wait_ge(s_fin, g + 1)
                nc.vector.tensor_tensor(ada_t[:, c:c + 4], ps[FIN][:, 0:4], vec[:, V_B + c:V_B + c + 4],
                                        ALU.add).then_inc(s_col, 1)
                dve.wait_ge(s_col, g + 1)

            def first_h(j):
                if j == 0:
                    dve.wait_ge(s_xnt, 8)
                link(nc.vector.scalar_tensor_tensor(scale1[:, 4 * j:4 * j + 4], ada_t[:, 16 + 4 * j:20 + 4 * j], 1.0,
                                                    vec[:, V_N1 + 4 * j:V_N1 + 4 * j + 4], ALU.add, ALU.mult))
                for k in range(4 * j, 4 * j + 4):
                    last = nc.vector.tensor_scalar(xn_t[:, k, :], xn_t[:, k, :], scale1[:, k:k + 1], ada_t[:, k:k + 1],
                                                   ALU.mult, ALU.add)
                last.then_inc(s_hf, 1)
                dve.wait_ge(s_hhi, j + 1)
                nc.vector.tensor_tensor(h_lo[:, 4 * j:4 * j + 4, :], xn_t[:, 4 * j:4 * j + 4, :],
                                        h_hi[:, 4 * j:4 * j + 4, :].bitcast(F32), ALU.subtract).then_inc(s_hlo, 1)

            dve.wait_ge(s_sigc, 1)
            nc.vector.tensor_tensor(silu_c[:], vec[:, V_C:V_C + KT], sig_c[:], ALU.mult).then_inc(s_siluc, 1)
            dve.wait_ge(s_siluc, 1)
            dve.wait_ge(s_pos, 16)
            dve.wait_ge(s_small, 80)
            link(nc.vector.tensor_copy(ang[:], pos_i[:]))
            link(nc.vector.tensor_scalar(ang[:], ang[:], ck(C_INV, 1), None, ALU.mult))
            magic = 12582912.0
            link(nc.vector.tensor_scalar(turns[:], ang[:], 1.0 / (2 * math.pi), magic, ALU.mult, ALU.add))
            link(nc.vector.tensor_scalar(turns[:], turns[:], magic, None, ALU.subtract))
            for part in (6.28125, 0.0019340515136718750, 1.2556659146019e-06):
                link(nc.vector.scalar_tensor_tensor(ang[:], turns[:], -part, ang[:], ALU.mult, ALU.add))
            link(nc.vector.tensor_scalar(ang[:], ang[:], 3.1415925, -3.1415925, ALU.min, ALU.max))
            link(nc.vector.tensor_scalar(turns[:], ang[:], -1.0, None, ALU.mult))
            link(nc.vector.tensor_tensor(turns[:], turns[:], ang[:], ALU.max))
            nc.vector.tensor_scalar(turns[:], turns[:], -1.0, math.pi / 2, ALU.mult, ALU.add).then_inc(s_trig, 1)
            dve.wait_ge(s_ss, NT)
            nc.vector.tensor_scalar(stat[:, 2:4], stat[:, 0:2], 1.0 / D, RMS_EPS, ALU.mult, ALU.add).then_inc(s_ms, 1)
            for u in range(2):
                ada_unit(u)
            dve.wait_ge(s_rt, 1)
            link(nc.vector.reciprocal(stat[:, 4:6], stat[:, 4:6]))
            for t in range(NT):
                nc.vector.tensor_scalar(x_in[:, t, :], x_in[:, t, :], stat[:, 4 + t:5 + t], None, ALU.mult).then_inc(s_xn, 1)
            for u in range(2, INIT_ADA):
                ada_unit(u)
                g = u // UPG
                if u % UPG == 3 and g >= 1:
                    ada_cols(g - 1)
                if u % (2 * UPG) == 4 and g >= 2:
                    first_h(g // 2 - 1)
                if u % UPG == 6 and g >= 6:
                    rest_unit(2 * (g - 6))
                    rest_unit(2 * (g - 6) + 1)
            ada_cols(7)
            first_h(3)
            nc.vector.memset(ybuf[:, :, 0:1], 0.0).then_inc(s_v0, 1)

            def win_epilogue(gi):
                if gi < 4:
                    for b in range(2):
                        i = 2 * gi + b
                        dve.wait_ge(s_perm, i + 1)
                        dst = qk[:, 4 * gi + 2 * b:4 * gi + 2 * b + 2, :]
                        cos2 = cosT[:].unsqueeze(1).broadcast_to([P, 2, T])
                        sin2 = sinT[:].unsqueeze(1).broadcast_to([P, 2, T])
                        if i:
                            dve.wait_ge(s_rope, i)
                        nc.vector.tensor_tensor(t1[:], ps[6 + b][:, :].rearrange("p (k t) -> p k t", k=2), sin2, ALU.mult)
                        link(nc.vector.tensor_tensor(dst, qraw[:, 2 * b:2 * b + 2, :], cos2, ALU.mult))
                        nc.vector.tensor_tensor(dst, dst, t1[:], ALU.add).then_inc(s_rope, 1)
                elif gi >= 6:
                    dve.wait_ge(s_evac, gi + 1)
                    if gi == 6:
                        dve.wait_ge(s_v0, 1)
                    n = 4 if gi < 12 else 3
                    dst = rkv[:, 4 * (gi - 6):4 * (gi - 6) + 4, :] if gi < 12 else lora[:, :, :]
                    link(nc.vector.tensor_tensor(dst, ybuf[:, 0:n, 0:T], ybuf[:, 0:n, 1:T + 1], ALU.subtract))
                    for i in range(n):
                        last = nc.vector.scalar_tensor_tensor(dst[:, i, :], dst[:, i, :], v1(V_MU + 4 * (gi - 6) + i),
                                                              ybuf[:, i, 1:T + 1], ALU.mult, ALU.add)
                    last.then_inc(s_shift if gi < 12 else s_lora, 1)

            def attn_mask(h):
                dve.wait_ge(s_score, h + 1)
                if h:
                    dve.wait_ge(s_pt, h)
                link(nc.vector.scalar_tensor_tensor(prob[:], ps[4][:, 0:3 * P].rearrange("p (k t) -> p k t", k=3),
                                                    HD ** -0.5, ck(C_LC, 3 * P).rearrange("p (k t) -> p k t", k=3),
                                                    ALU.mult, ALU.add))
                nc.vector.tensor_reduce(stat[:, 6:7], prob[:, 0, :], axis=AX, op=ALU.max, negate=True)
                nc.vector.tensor_reduce(stat[:, 7:8], prob[:, 1:3, :].rearrange("p k t -> p (k t)"), axis=AX,
                                        op=ALU.max, negate=True).then_inc(s_masked, 1)

            def attn_norm(h):
                dve.wait_ge(s_exp, h + 1)
                link(nc.vector.reciprocal(stat[:, 8:10], stat[:, 8:10]))
                nc.vector.tensor_scalar(prob[:, 0, :], prob[:, 0, :], stat[:, 8:9], None, ALU.mult)
                nc.vector.tensor_scalar(prob[:, 1:3, :], prob[:, 1:3, :], stat[:, 9:10], None, ALU.mult).then_inc(s_prob, 1)

            def attn_rest(hp):
                dve.wait_ge(s_ohi, hp + 1)
                nc.vector.tensor_tensor(mixa_lo[:, hp, :], ps[7][:, 0:T], mixa_hi[:, hp, :].bitcast(F32),
                                        ALU.subtract).then_inc(s_mixa, 1)

            def attn_slot(i):
                if 2 <= i < HEADS + 2 and i % 2 == 1:
                    attn_rest((i - 3) // 2)
                if i < HEADS:
                    attn_mask(i)

            ada_next = [INIT_ADA]

            def ada_step(limit):
                if ada_next[0] < limit:
                    u = ada_next[0]
                    ada_unit(u)
                    ada_next[0] += 1

            for gi in range(WIN_G):
                for ku in range(UPG):
                    n = gi * UPG + ku
                    if n >= RING:
                        rest_unit(n, LORA_W if gi == WIN_G - 1 else CW)
                    if gi and ku == 4:
                        win_epilogue(gi - 1)
                    u = n - 6 * UPG - 4 - LAG
                    if u >= 0 and u % 2 == 0 and u // 2 < HEADS + 2:
                        attn_slot(u // 2)
                    if u >= 0 and u % 2 == 1 and u // 2 < HEADS:
                        attn_norm(u // 2)
                    if n % 2 == 1:
                        ada_step(END_ADA1)
                        if ada_next[0] % UPG == 2 and n > 2 * UPG:
                            ada_cols(ada_next[0] // UPG - 1)
            win_epilogue(WIN_G - 1)

            for hp in range(PAIRS):
                nc.vector.tensor_scalar(kk[:, hp, :], rkv[:, 8 + hp, :], v1(V_KK + hp), None, ALU.mult).then_inc(s_kkr, 1)
            for sd in sides:
                nc.vector.memset(sd.br[:], 0.0)
                nc.vector.memset(sd.kr[:], 0.0)
                ins = nc.vector.tensor_copy(sd.y1[:].rearrange("p l m t -> p (l m) t"),
                                            ident.unsqueeze(1).broadcast_to([P, 4 * LEVELS, P]))
            link(ins)
            for hp in range(PAIRS):
                sd = sides[hp % 2]
                dve.wait_ge(s_sigs, hp + 1)
                nc.vector.tensor_scalar(lw[:, hp, :], lw[:, hp, :], -SQ, None, ALU.mult)
                link(nc.vector.tensor_scalar(sd.cen[:, 0, :], ab[:, hp, :], 1.0, v1(V_KA + hp), ALU.subtract, ALU.mult))
                ins = nc.vector.scalar_tensor_tensor(rkv[:, 8 + hp, :], sd.cen[:, 0, :], 1.0, rkv[:, 8 + hp, :], ALU.add,
                                                     ALU.mult)
            link(ins)

            def decays(w, i):
                sd, hp = sides[i], 2 * w + i
                cen, refc = sd.cen, sd.refc[:, w % 2, :]
                if w:
                    dve.wait_ge(sd.s_e3, w)
                link(nc.vector.tensor_tensor_scan(cen[:, 0, :], ck(C_RES, T), lw[:, hp, :], 0.0, ALU.mult, ALU.add))
                c4 = cen[:, 0, :].rearrange("p (c b t) -> p c b t", c=2, b=2)
                link(nc.vector.tensor_copy(refc[:, 0:2], c4[:, :, 0, 63]))
                for c in range(2):
                    x = cen[:, 0, 128 * c:128 * c + 64]
                    ins = nc.vector.tensor_scalar(x, x, refc[:, c:c + 1], None, ALU.subtract)
                link(ins)
                nc.vector.tensor_tensor(refc[:, 2:3], refc[:, 1:2], cen[:, 0, 127:128], ALU.add)
                nc.vector.tensor_tensor(cen[:, 1, :], cen[:, 0, :], lw[:, hp, :], ALU.subtract).then_inc(sd.s_cen, 1)

            for i in range(2):
                decays(0, i)
            dve.wait_ge(s_rns, 1)
            link(nc.vector.tensor_scalar(rnc[:], rnc[:], 1e-12, None, ALU.max))
            nc.vector.reciprocal(rnc[:], rnc[:]).then_inc(s_rnc, 1)
            for hp in range(PAIRS):
                dve.wait_ge(s_rnb, hp // 2 + 1)
                link(nc.vector.tensor_tensor(kk[:, hp, :], kk[:, hp, :], ps[hp // 2][:, T * (hp % 2):T * (hp % 2) + T], ALU.mult))
                last = nc.vector.tensor_tensor(ab[:, hp, :], ab[:, hp, :], kk[:, hp, :], ALU.mult)
            last.then_inc(s_pre, 1)
            dve.wait_ge(s_pre, 1)

            def operands(w, i):
                sd, hp = sides[i], 2 * w + i
                op, e3 = sd.op, sd.e3
                dve.wait_ge(sd.s_e3, w + 1)
                if w:
                    dve.wait_ge(sd.s_ot, w)
                nc.vector.scalar_tensor_tensor(op[:, 0, :], kk[:, hp, :], -1.0, e3[:, 2, :], ALU.mult, ALU.mult)
                nc.vector.tensor_tensor(op[:, 1, :], rkv[:, hp, :], e3[:, 0, :], ALU.mult)
                nc.vector.tensor_tensor(op[:, 2, :], ab[:, hp, :], e3[:, 1, :], ALU.mult)
                nc.vector.tensor_tensor(op[:, 3, :], rkv[:, 8 + hp, :], e3[:, 1, :], ALU.mult).then_inc(sd.s_op, 1)

            strict_incl = ck(C_SI, T).bitcast(I32).unsqueeze(1).broadcast_to([P, 2, T])
            m0 = ck(C_M0).bitcast(I32).unsqueeze(1).broadcast_to([P, 2, P])
            m0t = ck(C_M0T).bitcast(I32).unsqueeze(1).broadcast_to([P, 2, P])

            def first_grams(w, i):
                sd = sides[i]
                dve.wait_ge(sd.s_gram, w + 1)
                dve.wait_ge(sd.s_eye, w + 1)
                for e in range(2):
                    nc.vector.copy_predicated(sd.br[:, 2 * e:2 * e + 2, :], strict_incl,
                                              ps[sd.bank[e]][:, :].rearrange("p (c s) -> p c s", c=2))
                for e in range(2):
                    bank, c0 = (sd.bank[2], 0) if e == 0 else ((7, FIN)[i], T)
                    ins = nc.vector.copy_predicated(sd.xm[:, 2 * e:2 * e + 2, :], m0,
                                                    ps[bank][:, c0:c0 + T].rearrange("p (c s) -> p c s", c=2))
                ins.then_inc(sd.s_gramc, 1)
                for e in range(2):
                    ins = nc.vector.copy_predicated(sd.xt[:, 2 * e:2 * e + 2, :], m0t,
                                                    ps[sd.bank[e]][:, :].rearrange("p (c s) -> p c s", c=2)[:, :, 0:P])
                ins.then_inc(sd.s_gramc, 1)

            def key_grams(w, i):
                sd = sides[i]
                dve.wait_ge(sd.s_krg, w + 1)
                for e in range(2):
                    ins = nc.vector.copy_predicated(sd.kr[:, 2 * e:2 * e + 2, :], strict_incl,
                                                    ps[(sd.bank[2], 7)[e]][:, :].rearrange("p (c s) -> p c s", c=2))
                ins.then_inc(sd.s_krc, 1)

            def level(w, i, lev):
                sd, b = sides[i], 2 << lev
                dve.wait_ge(sd.s_y, w * LEVELS + lev + 1)
                mask = ck(C_LEV + P * lev).bitcast(I32).rearrange("p (n two b) -> p n two b", two=2, b=b)[:, :, 0, :]
                nc.vector.copy_predicated(blocks(sd.y1[:, lev], b, 0), mask.unsqueeze(1).broadcast_to([P, 4, HD // b, b]),
                                          blocks(four(sd.bank[0]), b, 0)).then_inc(sd.s_y1, 1)

            for i in range(2):
                operands(0, i)
            last_slot = -1
            for slot, w, i, step, nth in turns_of:
                sd, hp = sides[i], 2 * w + i
                if slot != last_slot:
                    last_slot = slot
                    if slot % 3 == 0:
                        ada_step(RWKV_ADA_END)
                    if slot - 2 in FIN_SLOT:
                        ada_cols(14 + FIN_SLOT.index(slot - 2))
                if step == "gram":
                    first_grams(w, i)
                elif step == "y":
                    level(w, i, nth)
                elif step == "keys":
                    key_grams(w, i)
                elif step == "u" and nth == 0:
                    if w + 1 < WAVES:
                        decays(w + 1, i)
                    nc.vector.scalar_tensor_tensor(rkv[:, hp, :], rkv[:, hp, :], v1(V_RK + hp), rkv[:, 8 + hp, :],
                                                   ALU.mult, ALU.mult).then_inc(sd.s_bon, 1)
                elif step == "mean":
                    dve.wait_ge(sd.s_mean, w + 1)
                    nc.vector.scalar_tensor_tensor(lw[:, hp, :], ps[sd.bank[2]][:, 0:T], -1.0 / HD, sd.o_t[:], ALU.mult,
                                                   ALU.add).then_inc(sd.s_dev, 1)
                    if w + 1 < WAVES:
                        operands(w + 1, i)
                elif step == "var":
                    dve.wait_ge(sd.s_var, w + 1)
                    nc.vector.tensor_scalar(varc[:, 4 * hp:4 * hp + 4], ps[sd.bank[0]][:, 0:4], 1.0 / HD, GN_EPS,
                                            ALU.mult, ALU.add)
                    nc.vector.tensor_tensor(rkv[:, hp, :], ps[sd.bank[1]][:, 0:T], rkv[:, 16 + hp, :],
                                            ALU.mult).then_inc(sd.s_bonus, 1)
            dve.wait_ge(s_sd, 1)
            nc.vector.reciprocal(varc[:], varc[:]).then_inc(s_rstd, 1)
            for sd in sides:
                dve.wait_ge(sd.s_bonus, WAVES)
            for hp in range(PAIRS):
                dve.wait_ge(s_g, hp + 1)
                y = lw[:, hp, :]
                pb = (0, 1, 2, 3)[hp % 4]
                link(nc.vector.scalar_tensor_tensor(y, ps[pb][:, 0:T], v1(V_GG + hp), y, ALU.mult, ALU.mult))
                link(nc.vector.scalar_tensor_tensor(y, y, v1(V_GB + hp), rkv[:, hp, :], ALU.add, ALU.add))
                nc.vector.tensor_tensor(y, y, ps[pb][:, T:2 * T], ALU.mult).then_inc(s_mixf, 1)
            for hp in range(PAIRS):
                dve.wait_ge(s_mrhi, hp + 1)
                nc.vector.tensor_tensor(mixr_lo[:, hp, :], lw[:, hp, :], mixr_hi[:, hp, :].bitcast(F32),
                                        ALU.subtract).then_inc(s_mixr, 1)

            def gate_diag(i, dst):
                c = (8 if i < 4 else 20) * 4 + 4 * (i % 4)
                if i:
                    dve.wait_ge(s_gt, i)
                nc.vector.tensor_tensor(dst[:].rearrange("p (k t) -> p k t", k=4), over4(ident),
                                        ada_t[:, c:c + 4].unsqueeze(2).broadcast_to([P, 4, P]), ALU.mult).then_inc(s_diag, 1)

            def residual(i, gate, tmp, banks):
                ct = i % 4
                dve.wait_ge(s_gtb, i + 1)
                dve.wait_ge(s_used, N_OUT0 + UPG * (i + 1) if i < 4 else N_DOWN0 + DOWN_U * (i - 3))
                for t in range(NT):
                    if i or t:
                        dve.wait_ge(s_x1, 2 * i + t)
                    link(nc.vector.tensor_tensor(tmp[:], ps[banks + t][:, :], gate[:], ALU.mult))
                    x = x1[:, t, ct * CW:(ct + 1) * CW]
                    nc.vector.tensor_tensor(x, x, tmp[:], ALU.add).then_inc(s_x1, 1)

            def row_rms(i):
                dve.wait_ge(s_ssp, 8 * (i + 1))
                link(nc.vector.tensor_reduce(stat[:, 2:4], stat[:, 10:18].rearrange("p (t c) -> p t c", t=2), axis=AX, op=ALU.add))
                nc.vector.tensor_scalar(stat[:, 2:4], stat[:, 2:4], 1.0 / D, RMS_EPS, ALU.mult, ALU.add).then_inc(s_ms2, 1)
                dve.wait_ge(s_rt2, i + 1)
                link(nc.vector.reciprocal(stat[:, 4:6], stat[:, 4:6]))

            dve.wait_ge(s_x1in, 16)
            for g in range(OUT_G):
                for ku in range(UPG):
                    n_out = g * UPG + ku
                    rest_unit(N_OUT0 + n_out)
                    ada_step(END_ADA1)
                    if ku == 1:
                        gate_diag(g, diag)
                    if g and ku == 4:
                        residual(g - 1, gtb, upd, 2 * ((g - 1) % 2))
                    if n_out == 8:
                        ada_cols(18)
                    if n_out == 18:
                        ada_cols(19)
            link(nc.vector.scalar_tensor_tensor(scale2[:], ada_t[:, 64:80], 1.0, vec[:, V_N2:V_N2 + KT], ALU.add, ALU.mult))
            residual(OUT_G - 1, gtb, upd, 2)
            row_rms(0)
            for t in range(NT):
                nc.vector.tensor_scalar(xn2[:, t, :], x1[:, t, :], stat[:, 4 + t:5 + t], None, ALU.mult).then_inc(s_xn2, 1)
            for n in range(RING):
                rest_unit(N_GU0 + n)
            for j in range(4):
                if j >= 2:
                    dve.wait_ge(s_h2lo, j - 1)
                for b in range(2):
                    dve.wait_ge(s_x2t, 2 * j + b + 1)
                    for kx in range(2):
                        k = 4 * j + 2 * b + kx
                        last = nc.vector.tensor_scalar(h2f[:, j % 2, 2 * b + kx, :], ps[(2 * j + b) % 4][:, kx * T:(kx + 1) * T],
                                                       scale2[:, k:k + 1], ada_t[:, 48 + k:49 + k], ALU.mult, ALU.add)
                last.then_inc(s_h2f, 1)
                dve.wait_ge(s_h2hi, j + 1)
                nc.vector.tensor_tensor(h_lo[:, 4 * j:4 * j + 4, :], h2f[:, j % 2], h_hi[:, 4 * j:4 * j + 4, :].bitcast(F32),
                                        ALU.subtract).then_inc(s_h2lo, 1)

            def ffn_product(gn, parity):
                dve.wait_ge(s_silu, gn + 1)
                for b in range(2):
                    x = sg[:, parity, 2 * b:2 * b + 2, :]
                    last = nc.vector.tensor_tensor(x, x, ps[4 * parity + 2 + b][:, :].rearrange("p (k t) -> p k t", k=2), ALU.mult)
                last.then_inc(s_prod, 1)

            def ffn_lo(gn, parity):
                dve.wait_ge(s_ahi, gn + 1)
                nc.vector.tensor_tensor(act_lo[:, bass.ds(gn * 4, 4), :], sg[:, parity],
                                        act_hi[:, bass.ds(gn * 4, 4), :].bitcast(F32), ALU.subtract).then_inc(s_alo, 1)

            def rest_gu(it, j):
                dve.wait_ge(s_hi, it * (2 * UPG) + (N_GU0 + j + 1))
                nc.vector.tensor_tensor(w_lo[:, j % RING], raw[:, j % RING], w_hi[:, j % RING].bitcast(F32),
                                        ALU.subtract).then_inc(s_lo, 1)

            for j in range(RING, 2 * UPG):
                rest_gu(0, j)
            with dve.Fori(0, (GU_G - 1) // 2) as it:
                for half in range(2):
                    for j in range(2 * UPG):
                        rest_gu(it * 2, 2 * UPG * (1 + half) + j)
                        if j == 3:
                            ffn_product(it * 2 + half, half)
                        if j == 7:
                            ffn_lo(it * 2 + half, half)
            ffn_product(GU_G - 1, 0)
            for n in range(N_DOWN0, N_DOWN0 + 2):
                rest_unit(n)
            ffn_lo(GU_G - 1, 0)
            for g in range(OUT_G):
                for ku in range(DOWN_U):
                    n = N_DOWN0 + g * DOWN_U + ku
                    if n >= N_DOWN0 + 2:
                        rest_unit(n)
                    if ku % 2 == 0 and ku < 2 * UPG:
                        ada_unit(END_ADA1 + g * UPG + ku // 2)
                    if ku == DOWN_U - 3:
                        ada_cols(20 + g)
                        gate_diag(OUT_G + g, diag2)
                    if g and ku == 4:
                        residual(OUT_G + g - 1, gtb2, upd2, 2 * ((g - 1) % 2))
            residual(2 * OUT_G - 1, gtb2, upd2, 2)
            row_rms(1)
            dve.wait_ge(s_nf, 16)
            for t in range(NT):
                nc.vector.scalar_tensor_tensor(x1[:, t, :], x1[:, t, :], stat[:, 4 + t:5 + t], nf_b[:], ALU.mult,
                                               ALU.mult).then_inc(s_fs, 1)

        @block.tensor
        def _(pe):
            mm = nc.tensor.matmul

            def three_pass(out, sh, sl, mh, ml, first, last, shared=False):
                mm(out, sh, mh, start=first, stop=False, skip_group_check=shared)
                mm(out, sh, ml, start=False, stop=False, skip_group_check=shared)
                return mm(out, sl, mh, start=False, stop=last, skip_group_check=shared)

            def unit_channels(n, ku, pb, hi, lo, blocks):
                pe.wait_ge(s_lo, n + 1)
                for i, c0 in enumerate(blocks):
                    for kx in range(UK):
                        k = UK * ku + kx
                        out = ps[pb + i // 2][:, (i % 2) * T:(i % 2 + 1) * T]
                        w = slice(c0, c0 + P)
                        last = three_pass(out, w_hi[:, n % RING, kx, w] if isinstance(n, int) else None,
                                          w_lo[:, n % RING, kx, w], hi[:, k, :], lo[:, k, :],
                                          first=(k == 0 and i % 2 == 0), last=(k == KT - 1), shared=True)
                last.then_inc(s_used, 1)

            def unit_tokens(n, k0, kmax, pb, hi, lo):
                pe.wait_ge(s_lo, n + 1)
                for t in range(NT):
                    for kx in range(UK):
                        k = k0 + kx
                        hk, lk, kk_ = (hi, lo, k) if not isinstance(hi, tuple) else (hi[k // 8], lo[k // 8], k % 8)
                        tok = slice(t * P, (t + 1) * P)
                        last = three_pass(ps[pb + t][:, :], hk[:, kk_, tok], lk[:, kk_, tok], w_hi[:, slot_of(n), kx, :],
                                          w_lo[:, slot_of(n), kx, :], first=(k == 0), last=(k == kmax - 1))
                last.then_inc(s_used, 1)

            def ada_fin(g):
                pe.wait_ge(s_adaused, UPG * (g + 1))
                if g:
                    pe.wait_ge(s_col, g)
                for j in range(4):
                    last = mm(ps[FIN][:, j:j + 1], acc[:, g % 2, j * P:(j + 1) * P], ones[:, 0:1], start=True, stop=True)
                last.then_inc(s_fin, 1)

            pe.wait_ge(s_cst, 16)
            pe.wait_ge(s_rows, 16 * 13)
            for i, (rows, col) in enumerate(((104, 0), (96, V_B), (27, V_MU))):
                last = nc.tensor.transpose(ps[4][:, col:col + rows], vrows[0:rows, i, :], ident[0:rows, 0:rows])
            last.then_inc(s_vt, 1)
            pe.wait_ge(s_xn, NT)
            pe.wait_ge(s_vec, 1)
            for b in range(8):
                for kx in range(2):
                    for t in range(NT):
                        k = 2 * b + kx
                        last = nc.tensor.transpose(ps[b][:, kx * T + t * P:kx * T + (t + 1) * P],
                                                   x_in[:, t, k * P:(k + 1) * P], ident)
                last.then_inc(s_xt, 1)
            pe.wait_ge(s_xnt, FIN + 1)
            for g in range(8):
                ada_fin(g)

            def rope_perm(gi):
                pe.wait_ge(s_evac, gi + 1)
                if gi == 0:
                    pe.wait_ge(s_small, 80)
                    pe.wait_ge(s_xnt, 8)
                else:
                    pe.wait_ge(s_rope, 2 * gi)
                for b in range(2):
                    mm(ps[6 + b][:, :], ck(C_PERM), qraw[:, 2 * b:2 * b + 2, :].rearrange("p k t -> p (k t)"),
                       start=True, stop=True).then_inc(s_perm, 1)

            def attn_slot(i):
                if 2 <= i < HEADS + 2:
                    h = i - 2
                    hp, e = h // 2, h % 2
                    pe.wait_ge(s_ptc, h + 1)
                    if e == 0 and hp:
                        pe.wait_ge(s_mixa, hp)
                    rows = slice(64 * e, 64 * e + 64)
                    vs = slice(HD * h, HD * h + HD)
                    mm(ps[7][rows, 0:P], v_tok[:, 0, vs], prob_t[:, 0, :], start=True, stop=True)
                    mm(ps[7][rows, P:T], v_tok[:, 0, vs], prob_t[:, 1, :], start=True, stop=False)
                    mm(ps[7][rows, P:T], v_tok[:, 1, vs], prob_t[:, 2, :], start=False, stop=True).then_inc(s_o, 1)
                if 1 <= i < HEADS + 1:
                    h = i - 1
                    pe.wait_ge(s_prob, h + 1)
                    if h:
                        pe.wait_ge(s_ptc, h)
                    for j in range(3):
                        last = nc.tensor.transpose(ps[6][:, j * P:(j + 1) * P], prob[:, j, :], ident)
                    last.then_inc(s_pt, 1)
                if i < HEADS:
                    h = i
                    if h == 0:
                        pe.wait_ge(s_rope, 8)
                        pe.wait_ge(s_evac, 6)
                    else:
                        pe.wait_ge(s_masked, h)
                    rows = slice(64 * (h % 2), 64 * (h % 2) + 64)
                    q, k = qk[rows, h // 2, :], qk[rows, 8 + h // 2, :]
                    mm(ps[4][:, 0:P], q[:, 0:P], k[:, 0:P], start=True, stop=True)
                    mm(ps[4][:, P:3 * P], q[:, P:T], k, start=True, stop=True).then_inc(s_score, 1)

            full = (0, P, 2 * P, 3 * P)
            fins = [8]
            pe.wait_ge(s_xnt, 8)
            for gi in range(WIN_G):
                for ku in range(UPG):
                    n = gi * UPG + ku
                    if gi == 0 and ku % 2 == 0:
                        pe.wait_ge(s_hlo, ku // 2 + 1)
                    if gi >= 2 and ku == 0:
                        pe.wait_ge(s_evac, gi - 1)
                    pb = 2 * (gi % 2)
                    if gi in (4, 5):
                        unit_tokens(n, UK * ku, KT, pb, h_hi, h_lo)
                    else:
                        unit_channels(n, ku, pb, h_hi, h_lo, full if gi < WIN_G - 1 else (0, P, LORA_W - P))
                    if 1 <= gi <= 4 and ku == 1:
                        rope_perm(gi - 1)
                    u = n - 6 * UPG - 4
                    if u >= 0 and u % 2 == 0 and u // 2 < HEADS + 2:
                        attn_slot(u // 2)
                    if n % 2 == 1 and (INIT_ADA + n // 2 + 1) % UPG == 1 and n > 2 * UPG:
                        ada_fin(fins[0])
                        fins[0] += 1

            pe.wait_ge(s_lora, 2)
            pe.wait_ge(s_mixa, PAIRS)
            half = [slice(0, 64), slice(64, 128)]
            chunk = [slice(0, P), slice(P, T)]
            head_ones = ck(C_BLK)[:, 0:P:HD]
            for hp in range(PAIRS):
                cols = slice(hp * P, (hp + 1) * P)
                if hp >= 2:
                    pe.wait_ge(s_sigs, hp - 1)
                zb, ab_b = (4, 6) if hp % 2 == 0 else (2, 3)
                mm(ps[zb][:, 0:T], w_di[0:64, cols], lora[0:64, 0, :], start=True, stop=True)
                mm(ps[ab_b][:, 0:T], w_di[64:128, cols], lora[64:128, 0, :], start=True, stop=True).then_inc(s_zw, 1)
                pe.wait_ge(s_sqk, hp + 1)
                for c in range(2):
                    last = mm(ps[7][:, 4 * hp + 2 * c:4 * hp + 2 * c + 2], sides[hp % 2].sq[:, c * P:(c + 1) * P], head_ones,
                              start=True, stop=True)
                last.then_inc(s_ssq, 1)

            def spread(bank, c0, table, hp):
                for e in range(2):
                    for c in range(2):
                        col = table[:, 4 * hp + 2 * c + e:4 * hp + 2 * c + e + 1].broadcast_to([P, HD])
                        last = mm(ps[bank][half[e], c0 + c * P:c0 + (c + 1) * P], col, ident, start=True, stop=True)
                return last

            pe.wait_ge(s_sigs, PAIRS)
            pe.wait_ge(s_rnc, 1)
            for hp in range(PAIRS):
                last = spread(hp // 2, T * (hp % 2), rnc, hp)
                if hp % 2:
                    last.then_inc(s_rnb, 1)

            def first_grams(w, i):
                sd = sides[i]
                op, bank = sd.op, sd.bank
                pe.wait_ge(sd.s_op, w + 1)
                if w:
                    pe.wait_ge(sd.s_bonus, w)
                for e in range(2):
                    for c in range(2):
                        mm(ps[bank[e]][:, 2 * c * P:2 * (c + 1) * P], op[half[e], 2, chunk[c]],
                           op[half[e], 0:2, chunk[c]], start=True, stop=True)
                if i:
                    pe.wait_ge(s_col, 14 + w)
                elif w:
                    pe.wait_ge(sides[1].s_tvc, w)
                for e in range(2):
                    gb, c0 = (bank[2], 0) if e == 0 else ((7, FIN)[i], T)
                    for c in range(2):
                        last = mm(ps[gb][:, c0 + c * P:c0 + (c + 1) * P], op[half[e], 0, chunk[c]],
                                  op[half[e], 2, chunk[c]], start=True, stop=True)
                last.then_inc(sd.s_gram, 1)

            def key_grams(w, i):
                sd = sides[i]
                pe.wait_ge(sd.s_gramc, 2 * w + 1)
                if i:
                    pe.wait_ge(sides[0].s_tvc, w + 1)
                for e in range(2):
                    for c in range(2):
                        last = mm(ps[(sd.bank[2], 7)[e]][:, 2 * c * P:2 * (c + 1) * P], sd.op[half[e], 3, chunk[c]],
                                  sd.op[half[e], 0:2, chunk[c]], start=True, stop=True)
                last.then_inc(sd.s_krg, 1)

            def level_y(w, i, lev):
                sd = sides[i]
                if lev:
                    pe.wait_ge(sd.s_xm, w * (LEVELS - 1) + lev)
                else:
                    pe.wait_ge(sd.s_gramc, 2 * w + 2)
                for m in range(4):
                    last = mm(ps[sd.bank[0]][:, m * P:(m + 1) * P], sd.br[:, m, 0:P], sd.xm[:, m, :], start=True, stop=True)
                last.then_inc(sd.s_y, 1)

            def level_x(w, i, lev):
                sd, n = sides[i], w * LEVELS + lev
                pe.wait_ge(sd.s_y1, n + 1)
                if lev:
                    pe.wait_ge(sd.s_xt, n)
                else:
                    pe.wait_ge(sd.s_krc, w + 1)
                if lev < LEVELS - 1:
                    for m in range(4):
                        mm(ps[sd.bank[1]][:, m * P:(m + 1) * P], sd.xt[:, m, :], sd.y1[:, lev, m, :], start=True, stop=True)
                for m in range(4):
                    last = mm(ps[sd.bank[2]][:, m * P:(m + 1) * P], sd.y1[:, lev, m, :], sd.xt[:, m, :], start=True, stop=True)
                last.then_inc(sd.s_xx, 1)

            def to_tokens(w, i):
                sd, hp = sides[i], 2 * w + i
                pe.wait_ge(sd.s_krc, w + 1)
                for j, src in enumerate((sd.op[:, 2, 0:P], sd.op[:, 3, 0:P], rkv[:, 16 + hp, 0:P], rkv[:, 16 + hp, P:T])):
                    last = nc.tensor.transpose(ps[7][:, j * P:(j + 1) * P], src, ident)
                last.then_inc(sd.s_tv, 1)

            def right_sides(w, i, c):
                sd = sides[i]
                if c == 0:
                    pe.wait_ge(sd.s_tvc, w + 1)
                    pe.wait_ge(sd.s_xt, (w + 1) * LEVELS)
                else:
                    pe.wait_ge(sd.s_stc, w + 1)
                for e in range(2):
                    hd = slice(HD * e, HD * (e + 1))
                    last = mm(ps[sd.bank[e]][:, 0:HD], sd.kr[:, 2 * e + c, 0:P], sd.tv[:, 2 + c, hd], start=True, stop=(c == 0))
                    if c:
                        last = mm(ps[sd.bank[e]][:, 0:HD], sd.op[half[e], 0, chunk[1]], sd.s0[half[e], :], start=False,
                                  stop=True)
                last.then_inc(sd.s_u, 1)

            def solve(w, i, c):
                sd = sides[i]
                pe.wait_ge(sd.s_uc, 2 * w + c + 1)
                for e in range(2):
                    last = mm(ps[sd.bank[2]][:, e * HD:(e + 1) * HD], sd.xt[:, 2 * e + c, :], sd.us[:, e, :],
                              start=True, stop=True)
                last.then_inc(sd.s_sa, 1)

            def state(w, i):
                sd = sides[i]
                pe.wait_ge(sd.s_sac, 2 * w + 1)
                for e in range(2):
                    hd = slice(HD * e, HD * (e + 1))
                    out = ps[sd.bank[2]][half[e], 2 * HD:3 * HD]
                    mm(out, sd.tv[:, 0, hd], sd.sa[:, 0, e, :], start=True, stop=False)
                    last = mm(out, sd.tv[:, 1, hd], sd.tv[:, 2, hd], start=False, stop=True)
                last.then_inc(sd.s_st, 1)

            def outputs(w, i):
                sd = sides[i]
                pe.wait_ge(sd.s_sac, 2 * w + 2)
                for e in range(2):
                    hd = slice(HD * e, HD * (e + 1))
                    for c in range(2):
                        m = 2 * e + c
                        out = ps[sd.bank[e]][half[e], c * P:(c + 1) * P]
                        mm(out, sd.sa[:, c, e, :], sd.br[:, m, P:2 * P], start=True, stop=False)
                        last = mm(out, sd.tv[:, 2 + c, hd], sd.kr[:, m, P:2 * P], start=False, stop=(c == 0))
                        if c:
                            last = mm(out, sd.s0[half[e], :], sd.op[half[e], 1, chunk[1]], start=False, stop=True)
                last.then_inc(sd.s_ot, 1)

            def means(w, i):
                sd = sides[i]
                pe.wait_ge(sd.s_otc, w + 1)
                mm(ps[sd.bank[2]][:, 0:T], ck(C_BLK), sd.o_t[:], start=True, stop=True).then_inc(sd.s_mean, 1)

            def variances(w, i):
                sd, hp = sides[i], 2 * w + i
                pe.wait_ge(sd.s_bon, w + 1)
                mm(ps[sd.bank[1]][:, 0:T], ck(C_BLK), rkv[:, hp, :], start=True, stop=True)
                pe.wait_ge(sd.s_dsq, w + 1)
                for c in range(2):
                    last = mm(ps[sd.bank[0]][:, 2 * c:2 * c + 2], sd.sq[:, chunk[c]], head_ones, start=True, stop=True)
                last.then_inc(sd.s_var, 1)

            pe.wait_ge(s_pre, 1)
            for slot, w, i, step, nth in turns_of:
                if step == "gram":
                    first_grams(w, i)
                elif step == "y":
                    level_y(w, i, nth)
                elif step == "x":
                    level_x(w, i, nth)
                elif step == "keys":
                    key_grams(w, i)
                elif step == "tokens":
                    to_tokens(w, i)
                elif step == "u":
                    right_sides(w, i, nth)
                elif step == "solve":
                    solve(w, i, nth)
                elif step == "state":
                    state(w, i)
                elif step == "out":
                    outputs(w, i)
                elif step == "mean":
                    means(w, i)
                elif step == "var":
                    variances(w, i)
                if slot in FIN_SLOT and i == 1:
                    fw = FIN_SLOT.index(slot)
                    pe.wait_ge(sides[1].s_gramc, 2 * fw + 2)
                    ada_fin(14 + fw)
            pe.wait_ge(s_rstd, 1)
            for hp in range(PAIRS):
                cols = slice(hp * P, (hp + 1) * P)
                b = hp % 4
                if hp >= 4:
                    pe.wait_ge(s_mixf, hp - 3)
                spread(b, 0, varc, hp)
                mm(ps[b][:, T:2 * T], w_g[:, cols], lora[:, 1, :], start=True, stop=False)
                mm(ps[b][:, T:2 * T], w_g2[96:128, cols], lora[96:128, 2, :], start=False, stop=True).then_inc(s_g, 1)

            def gate_rows(i, src):
                pe.wait_ge(s_diag, i + 1)
                if i:
                    pe.wait_ge(s_gtb, i)
                mm(ps[4][:, :], ones, src[:], start=True, stop=True).then_inc(s_gt, 1)

            pe.wait_ge(s_mixr, PAIRS)
            for g in range(OUT_G):
                for ku in range(UPG):
                    n = N_OUT0 + g * UPG + ku
                    if g >= 2 and ku == 0:
                        pe.wait_ge(s_x1, 2 * (g - 1))
                    unit_tokens(n, UK * ku, KT, 2 * (g % 2), (mixa_hi, mixr_hi), (mixa_lo, mixr_lo))
                    if ku == 3:
                        gate_rows(g, diag)
                    if g * UPG + ku == 5:
                        ada_fin(18)
                    if g * UPG + ku == 15:
                        ada_fin(19)
            pe.wait_ge(s_xn2, NT)
            for b in range(8):
                if b >= 4:
                    pe.wait_ge(s_h2f, (b - 4) // 2 + 1)
                for kx in range(2):
                    for t in range(NT):
                        k = 2 * b + kx
                        last = nc.tensor.transpose(ps[b % 4][:, kx * T + t * P:kx * T + (t + 1) * P],
                                                   xn2[:, t, k * P:(k + 1) * P], ident)
                last.then_inc(s_x2t, 1)

            def gu_group(g, parity, j0, first):
                if not first:
                    pe.wait_ge(s_prod, g - 1)
                for m in range(2):
                    for ku in range(UPG):
                        pe.wait_ge(s_lo, g * (2 * UPG) + (N_GU0 + m * UPG + ku + 1))
                        for i in range(4):
                            for kx in range(UK):
                                k = UK * ku + kx
                                out = ps[4 * parity + 2 * m + i // 2][:, (i % 2) * T:(i % 2 + 1) * T]
                                w = slice(i * P, (i + 1) * P)
                                last = three_pass(out, w_hi[:, ku % RING, kx, w], w_lo[:, ku % RING, kx, w],
                                                  h_hi[:, k, :], h_lo[:, k, :], first=(k == 0 and i % 2 == 0),
                                                  last=(k == KT - 1), shared=True)
                        last.then_inc(s_used, 1)

            pe.wait_ge(s_h2lo, 4)
            pe.wait_ge(s_gtb, OUT_G)
            pe.wait_ge(s_col, END_ADA1 // UPG)
            gu_group(0, 0, 0, True)
            gu_group(1, 1, 0, True)
            gu_group(2, 0, 0, False)
            with pe.Fori(1, (GU_G - 1) // 2) as it:
                gu_group(it * 2 + 1, 1, 0, False)
                gu_group(it * 2 + 2, 0, 0, False)

            pe.wait_ge(s_prod, GU_G)
            for g in range(OUT_G):
                for ku in range(DOWN_U):
                    n = N_DOWN0 + g * DOWN_U + ku
                    if g >= 2 and ku == 0:
                        pe.wait_ge(s_x1, 2 * OUT_G + 2 * (g - 1))
                    if g == 0 and ku % 2 == 0:
                        pe.wait_ge(s_alo, ku // 2 + 1)
                    unit_tokens(n, UK * ku, FK, 2 * (g % 2), act_hi, act_lo)
                    if ku == DOWN_U - 5:
                        ada_fin(20 + g)
                    if ku == DOWN_U - 1:
                        gate_rows(OUT_G + g, diag2)


_INS = ["x", "c", "positions", "w_ada", "b_ada", "norm1_g", "norm2_g", "normf_g", "w_in", "w_out", "mu_shift", "w0",
        "w_decay_up", "a0", "w_iclr_up", "w_gate_up", "k_k", "k_a", "r_k", "gn_g", "gn_b", "w_ffn_gate", "w_ffn_up",
        "w_ffn_down"]


def kernel(**inputs):
    import concourse.bacc as bacc
    from concourse.bass_utils import run_bass_kernel_spmd as run

    nc = bacc.Bacc("TRN2", target_bir_lowering=False, num_devices=1)
    arrays, aps = {}, {}
    for name in _INS:
        x = np.ascontiguousarray(inputs[name])
        arrays[f"in_{name}"] = x
        aps[name] = nc.dram_tensor(f"in_{name}", x.shape, mybir.dt.from_np(x.dtype), kind="ExternalInput").ap()
    arrays["in_const"] = constants()
    aps["const"] = nc.dram_tensor("in_const", (P, NCONST), F32, kind="ExternalInput").ap()
    aps["out"] = nc.dram_tensor("out_0", (1, T, D), F32, kind="ExternalOutput").ap()
    build(nc, aps)
    r = run(nc, [arrays], core_ids=[0])
    return r.results[0]["out_0"]
```

```python
import math
from contextlib import ExitStack

import numpy as np

import concourse.bass as bass
from concourse import mybir

F32 = mybir.dt.float32
F32R = mybir.dt.float32r
I32 = mybir.dt.int32
ALU = mybir.AluOpType
ACT = mybir.ActivationFunctionType
AX = mybir.AxisListType.X

P = 128
T = 256
NT = T // P
D = 2048
KT = D // P
HD = 64
HEADS = 16
PAIRS = HEADS // 2
AW = 1024
IN_COLS = 3 * AW + 3 * AW + 288
FFN = 5632
FK = FFN // P
CW = 512
UK = 2
RING = 4
LAG = 3
UPG = KT // UK
WIN_G = 13
WIN_ORDER = (0, 1, 2, 3, 4, 5, 12, 8, 9, 6, 7, 10, 11)
N_OUT0 = WIN_G * UPG
OUT_G = D // CW
N_GU0 = N_OUT0 + OUT_G * UPG
GU_G = FFN // CW
N_DOWN0 = N_GU0 + 2 * GU_G * UPG
DOWN_U = FK // UK
N_UNITS = N_DOWN0 + OUT_G * DOWN_U
LORA_W = 288
RMS_EPS = 1e-6
GN_EPS = HD * 1e-5
WAVES = PAIRS // 2
LEVELS = 6
SQ = math.exp(-0.5)

V_C, V_N1, V_N2, V_W0, V_A0, V_KK, V_KA, V_RK, V_GG, V_GB = 0, 16, 32, 48, 56, 64, 72, 80, 88, 96
V_B = 104
V_MU = 200
NVEC = 227

C_ID, C_ONE, C_BLK, C_PERM, C_LC, C_LEV, C_SI, C_M0, C_M0T, C_RES, C_INV = (
    0, 128, 256, 384, 512, 896, 896 + 768, 1920, 2048, 2176, 2432)
NCONST = 2433


def constants():
    c = np.zeros((P, NCONST), np.float32)
    i = np.arange(P)
    c[:, C_ID:C_ID + P] = np.eye(P)
    c[:, C_ONE:C_ONE + P] = 1.0
    c[:, C_BLK:C_BLK + P] = (i[:, None] // HD == i[None, :] // HD)
    for h in (0, HD):
        for d in range(8):
            c[h + d + 8, C_PERM + h + d] = -1.0
            c[h + d, C_PERM + h + d + 8] = 1.0
    t = np.arange(T)[:, None]
    j = np.arange(T)[None, :]
    count = (((t - j) >= 0) & ((t - j) <= 128)).astype(np.float64)
    for dil in (4, 16):
        count += (j <= t) & ((t - j) % dil == 0) & ((t - j) <= 128 * dil)
    lc = np.where(count > 0, np.log(np.maximum(count, 1)), -1e30).astype(np.float32)
    c[:, C_LC:C_LC + P] = lc[:P, :P]
    c[:, C_LC + P:C_LC + 3 * P] = lc[P:, :]
    s, u = i[:, None], i[None, :]
    for lev in range(1, LEVELS + 1):
        b = 2 ** lev
        c[:, C_LEV + P * (lev - 1):C_LEV + P * lev] = (s // b == u // b + 1) & (u // b % 2 == 0)
    c[:, C_SI:C_SI + P] = s < u
    c[:, C_SI + P:C_SI + 2 * P] = s <= u
    c[:, C_M0:C_M0 + P] = (s == u + 1) & (u % 2 == 0)
    c[:, C_M0T:C_M0T + P] = (u == s + 1) & (s % 2 == 0)
    c[:, C_RES:C_RES + T] = (np.arange(T) % 64 != 0)
    rot = 16
    inv = (np.float32(500000.0) ** (-np.arange(0, rot, 2, dtype=np.float32) / np.float32(rot))).astype(np.float32)
    for h in (0, HD):
        for d in range(rot):
            c[h + d, C_INV] = inv[d % 8]
    return c


def slot_of(n):
    return n % RING


def build(nc, a):
    ctx = ExitStack()
    with ctx:
        def sem(name):
            return ctx.enter_context(nc.semaphore(name))

        top = [nc.sbuf_base + 31 - (nc.sbuf_base + 31) % 32]

        def fixed(name, shape, dt=F32):
            size = 4 * int(np.prod(shape[1:]))
            t = nc.alloc_sbuf_tensor_at(name, shape, dt, offset=top[0])
            top[0] += -(-size // 32) * 32
            return t

        raw = fixed("raw", [P, RING, UK, CW])
        split_off = top[0]
        w_hi = fixed("w_hi", [P, RING, UK, CW], F32R)
        w_lo = fixed("w_lo", [P, RING, UK, CW], F32R)
        idone = fixed("idone", [P, 2 * P])
        vec = fixed("vec", [P, NVEC])
        ada_t = fixed("ada_t", [P, 96])
        scale1 = fixed("scale1", [P, KT])
        scale2 = fixed("scale2", [P, KT])
        silu_c = fixed("silu_c", [P, KT])
        sig_c = fixed("sig_c", [P, KT])
        acc = fixed("acc", [P, 2, CW])
        stat = fixed("stat", [P, 32])
        rnc = fixed("rnc", [P, 4 * PAIRS])
        varc = fixed("varc", [P, 4 * PAIRS])
        refcs = [fixed(f"refc{i}", [P, 2, 4]) for i in range(2)]
        base = top[0]
        end = nc.sbuf_usable_end

        def at(name, offset, shape, dt=F32):
            size = 4 * int(np.prod(shape[1:]))
            assert base + offset + size <= end, (name, base, offset, size, end)
            return nc.alloc_sbuf_tensor_at(name, shape, dt, offset=base + offset)

        ident = idone[:, 0:P]
        ones = idone[:, P:2 * P]

        KB = 1024
        h_hi = at("h_hi", 0, [P, KT, T], F32R)
        h_lo = at("h_lo", 16 * KB, [P, KT, T], F32R)
        o = 32 * KB
        cst = at("cst", o, [P, NCONST - 256]); o += 4 * NCONST - 1024 + 28
        o = -(-o // 32) * 32
        cosT = at("cosT", o, [P, T]); o += KB
        sinT = at("sinT", o, [P, T]); o += KB
        ada_raw = at("ada_raw", o, [P, RING, UK, CW]); o += 16 * KB
        w_di = at("w_di", o, [P, AW]); o += 4 * KB
        w_g = at("w_g", o, [P, AW]); o += 4 * KB
        w_g2 = at("w_g2", o, [P, AW]); o += 4 * KB
        rkv_off = o
        rkv = at("rkv", o, [P, 24, T]); o += 24 * KB
        lora = at("lora", o, [P, 3, T]); o += 3 * KB
        mixa_hi = at("mixa_hi", o, [P, 8, T], F32R); o += 8 * KB
        mixa_lo = at("mixa_lo", o, [P, 8, T], F32R); o += 8 * KB
        qkv_off = o
        qk = at("qk", o, [P, 16, T]); o += 16 * KB
        v_tok = at("v_tok", o, [P, NT, AW]); o += 8 * KB
        tmp_off = o
        ybuf = at("ybuf", o, [P, 4, T + 1]); o += 4 * 4 * (T + 1)
        o = -(-o // 32) * 32
        qraw = at("qraw", o, [P, 4, T])
        t1 = at("t1", o + 4 * KB, [P, 2, T])
        prob = at("prob", o, [P, 3, P]); o += 1536
        prob_t = at("prob_t", o, [P, 3, P]); o += 1536
        sq1 = at("sq1", tmp_off + 4128, [P, 2, T])
        ka1 = at("ka1", tmp_off + 4128 + 2 * KB, [P, 2, T])
        x_in = at("x_in", rkv_off, [P, NT, D])
        xn_t = at("xn_t", qkv_off, [P, KT, T])
        vrows = at("vrows", tmp_off, [P, 3, P])
        pos_i = at("pos_i", rkv_off + 16 * KB, [P, T], I32)
        ang = at("ang", rkv_off + 17 * KB, [P, T])
        turns = at("turns", rkv_off + 18 * KB, [P, T])

        class Side:
            pass

        sides = []
        for i, start in enumerate((base, split_off)):
            sd = Side()
            put = [start]

            def room(name, shape):
                t = nc.alloc_sbuf_tensor_at(f"{name}_{i}", shape, F32, offset=put[0])
                put[0] += 4 * int(np.prod(shape[1:]))
                return t

            sd.op = room("op", [P, 4, T])
            sd.br = room("br", [P, 4, 2 * P])
            sd.kr = room("kr", [P, 4, 2 * P])
            sd.xm = room("xm", [P, 4, P])
            sd.xt = room("xt", [P, 4, P])
            sd.y1 = room("y1", [P, LEVELS, 4, P])
            sd.tv = room("tv", [P, 4, P])
            sd.us = room("us", [P, 2, HD])
            sd.s0 = room("s0", [P, HD])
            sd.sa = room("sa", [P, 2, 2, HD])
            sd.refc = refcs[i]
            assert put[0] <= start + 32 * KB
            put[0] = base + qkv_off + (31 - 7 * i) * KB
            sd.e3 = room("e3", [P, 3, T])
            sd.cen = room("cen", [P, 2, T])
            sd.o_t = room("o_t", [P, T])
            sd.sq = room("sq", [P, T])
            assert put[0] <= end
            sd.bank = (0, 1, 2) if i == 0 else (3, 4, 6)
            sides.append(sd)
        lw = at("lw", qkv_off, [P, PAIRS, T])
        ab = at("ab", qkv_off + 8 * KB, [P, PAIRS, T])
        kk = at("kk", qkv_off + 16 * KB, [P, PAIRS, T])
        mixr_hi = at("mixr_hi", 0, [P, 8, T], F32R)
        mixr_lo = at("mixr_lo", 8 * KB, [P, 8, T], F32R)

        act_hi = at("act_hi", 32 * KB, [P, FK, T], F32R)
        act_lo = at("act_lo", 32 * KB + 44 * KB, [P, FK, T], F32R)
        x1 = at("x1", 120 * KB, [P, NT, D])
        sg = at("sg", 136 * KB, [P, 2, 4, T])
        gtb = at("gtb", 136 * KB, [P, CW])
        diag = at("diag", 138 * KB, [P, CW])
        upd = at("upd", 140 * KB, [P, CW])
        h2f = at("h2f", 136 * KB, [P, 2, 4, T])
        rsd = at("rsd", 144 * KB, [P, NT, P])
        ada_raw2 = at("ada_raw2", 0, [P, RING, UK, CW])
        nf_b = at("nf_b", 16 * KB, [P, D])
        gtb2 = at("gtb2", 24 * KB, [P, CW])
        diag2 = at("diag2", 26 * KB, [P, CW])
        upd2 = at("upd2", 28 * KB, [P, CW])
        sqj = at("sqj", 30 * KB, [P, CW])
        sqj1 = at("sqj1", 142 * KB, [P, CW])

        ps = [ctx.enter_context(nc.psum_tensor(f"bank{b}", [P, 512], F32)) for b in range(8)]
        FIN = 5

        def ck(col, n=P):
            return cst[:, col - 256:col - 256 + n]

        def v1(col):
            return vec[:, col:col + 1]

        def four(bank):
            return ps[bank][:, :].rearrange("p (m t) -> p m t", m=4)

        def blocks(x, b, odd):
            return x.rearrange("p m (n two b) -> p m n two b", two=2, b=b)[:, :, :, odd, :]

        def over4(x):
            return x.unsqueeze(1).broadcast_to([P, 4, x.shape[1]])

        s_cst, s_rows, s_x, s_pos, s_small, s_v0, s_cst2 = map(sem, ("s_cst", "s_rows", "s_x", "s_pos", "s_small", "s_v0", "s_cst2"))
        s_raw = [sem(f"s_raw{i}") for i in range(RING)]
        s_hi, s_lo, s_used = sem("s_hi"), sem("s_lo"), sem("s_used")
        s_ada = [sem(f"s_ada{i}") for i in range(RING)]
        s_adaused, s_fin, s_col = map(sem, ("s_adaused", "s_fin", "s_col"))
        s_vt, s_vec, s_sigc, s_siluc = map(sem, ("s_vt", "s_vec", "s_sigc", "s_siluc"))
        s_ss, s_ms, s_rt, s_xn, s_xt, s_xnt = map(sem, ("s_ss", "s_ms", "s_rt", "s_xn", "s_xt", "s_xnt"))
        s_sc1, s_hf, s_hhi, s_hlo, s_rms = map(sem, ("s_sc1", "s_hf", "s_hhi", "s_hlo", "s_rms"))
        s_trig, s_sin = sem("s_trig"), sem("s_sin")
        s_evac, s_perm, s_rope = sem("s_evac"), sem("s_perm"), sem("s_rope")
        s_shift, s_lora = sem("s_shift"), sem("s_lora")
        s_score, s_masked, s_exp, s_prob, s_pt, s_ptc, s_o, s_ohi, s_mixa = map(
            sem, ("s_score", "s_masked", "s_exp", "s_prob", "s_pt", "s_ptc", "s_o", "s_ohi", "s_mixa"))
        s_zw, s_sigs, s_kkr, s_sqk, s_ssq, s_rns, s_rnc, s_rnb, s_pre = map(
            sem, ("s_zw", "s_sigs", "s_kkr", "s_sqk", "s_ssq", "s_rns", "s_rnc", "s_rnb", "s_pre"))
        for i, sd in enumerate(sides):
            (sd.s_cen, sd.s_e3, sd.s_op, sd.s_gram, sd.s_gramc, sd.s_krg, sd.s_krc, sd.s_y, sd.s_y1, sd.s_xx, sd.s_xxt, sd.s_xm,
             sd.s_xt, sd.s_tv, sd.s_tvc, sd.s_eye, sd.s_u, sd.s_uc, sd.s_sa, sd.s_sac, sd.s_st, sd.s_stc, sd.s_ot,
             sd.s_otc, sd.s_mean, sd.s_dev, sd.s_dsq, sd.s_bon, sd.s_var, sd.s_bonus) = [sem(f"s_{name}_{i}") for name in (
                 "cen", "e3", "op", "gram", "gramc", "krg", "krc", "y", "y1", "xx", "xxt", "xm", "xt", "tv", "tvc", "eye", "u",
                 "uc", "sa", "sac", "st", "stc", "ot", "otc", "mean", "dev", "dsq", "bon", "var", "bonus")]
            sd.s_blank, sd.s_y1blank = sem(f"s_blank_{i}"), sem(f"s_y1blank_{i}")
        s_sd, s_rstd, s_g, s_mixf, s_mrhi, s_mixr = map(
            sem, ("s_sd", "s_rstd", "s_g", "s_mixf", "s_mrhi", "s_mixr"))
        s_x1in, s_diag, s_gt, s_gtb, s_x1, s_ssp, s_ms2, s_rt2, s_xn2, s_x2t, s_h2f, s_h2hi, s_h2lo = map(
            sem, ("s_x1in", "s_diag", "s_gt", "s_gtb", "s_x1", "s_ssp", "s_ms2", "s_rt2", "s_xn2", "s_x2t",
                  "s_h2f", "s_h2hi", "s_h2lo"))
        s_silu, s_prod, s_ahi, s_alo, s_nf, s_fs, s_out = map(
            sem, ("s_silu", "s_prod", "s_ahi", "s_alo", "s_nf", "s_fs", "s_out"))
        s_dch = sem("s_dch")

        w_in = a["w_in"].rearrange("l (k p) n -> p (l k) n", p=P)
        w_out = a["w_out"].rearrange("l (k p) n -> p (l k) n", p=P)
        w_gate = a["w_ffn_gate"].rearrange("l (k p) n -> p (l k) n", p=P)
        w_up = a["w_ffn_up"].rearrange("l (k p) n -> p (l k) n", p=P)
        w_down = a["w_ffn_down"].rearrange("l (k p) n -> p (l k) n", p=P)
        w_ada = a["w_ada"].rearrange("l (k p) n -> p (l k) n", p=P)
        x_dram = a["x"].rearrange("b (t p) d -> p (b t) d", p=P)
        out_dram = a["out"].rearrange("b (t p) d -> p (b t) d", p=P)

        INIT_ADA = 8 * UPG
        END_ADA1 = 20 * UPG
        FIRST = 2 * UPG

        ANGLES = 24
        X_STATS = 3

        def first_unit(n):
            return n % 4 // 2, 2 * (n // 4) + n % 2

        def ada_due(n):
            return n >= FIRST and (n % 2 == 1 or n >= 88)

        def ada_done(n):
            return INIT_ADA + sum(ada_due(m) for m in range(n + 1))

        FIN_AT = {g: 1 + min(n for n in range(WIN_G * UPG) if ada_done(n) >= UPG * (g + 1)) for g in range(8, 14)}
        EVAC_AT = {0: FIRST, 1: FIRST + 6}
        ROPE_AT = {0: FIRST + 1, 1: FIRST + 5}
        EPI_AT = {0: FIRST + 4, 1: FIRST + 8}
        for pos in range(2, WIN_G - 1):
            EVAC_AT[pos], EPI_AT[pos] = UPG * (pos + 1) + 2, UPG * (pos + 1) + 4
            if pos < 4:
                ROPE_AT[pos] = UPG * (pos + 1) + 1

        def at_unit(table, n):
            return [key for key, unit in table.items() if unit == n]

        STEPS = (["gram", "keys", "y", "x", "tokens"] + ["y", "x"] * (LEVELS - 1)
                 + ["u", "solve", "state", "u", "solve", "out", "mean", "var"])
        turns_of = []
        BEHIND = 11
        for slot in range(WAVES * len(STEPS) + BEHIND):
            for i in range(2):
                at_step = slot - BEHIND * i
                if 0 <= at_step < WAVES * len(STEPS):
                    w, j = divmod(at_step, len(STEPS))
                    turns_of.append((slot, w, i, STEPS[j], STEPS[:j].count(STEPS[j])))
        X2T_BANKS = (4, 5, 6, 7, 2, 3, 4, 5)
        SIDE0_END = WAVES * len(STEPS)
        FINISH_BANKS = (0, 1, 2, 0, 1, 2, 0, 6)
        RN_BANKS = (7, 4, 6, 3)
        S1_AT = 91
        FIN_SLOT = [15 + len(STEPS) * w for w in range(WAVES)]
        RWKV_ADA_END = ada_done(WIN_G * UPG - 1) + 8 * WAVES

        ada_order = [g for j in range(4) for g in (j, 4 + j)] + list(range(8, 24))

        block = ctx.enter_context(nc.Block())

        @block.sync
        def _(sp):
            sp.dma_start(idone[:], a["const"][:, 0:256]).then_inc(s_cst, 16)
            rows = 0
            for name, n in (("c", 16), ("norm1_g", 16), ("norm2_g", 16), ("w0", 8), ("a0", 8), ("k_k", 8),
                            ("k_a", 8), ("r_k", 8), ("gn_g", 8), ("gn_b", 8)):
                flat = a[name].rearrange("a b c -> (a b c)") if name == "r_k" else a[name].rearrange("a b -> (a b)")
                sp.dma_start(vrows[rows:rows + n, 0, :], flat.rearrange("(r q) -> r q", q=P)).then_inc(s_rows, 16)
                rows += n
            sp.dma_start(vrows[0:96, 1, :], a["b_ada"].rearrange("l (r q) -> (l r) q", q=P)).then_inc(s_rows, 16)
            mu = a["mu_shift"].rearrange("a b -> (a b)")
            sp.dma_start(vrows[0:26, 2, :], mu[0:26 * P].rearrange("(r q) -> r q", q=P)).then_inc(s_rows, 16)
            sp.dma_start(vrows[26:27, 2, :], mu[3232:3360].rearrange("(r q) -> r q", q=P)).then_inc(s_rows, 16)
            for t in range(NT):
                sp.dma_start(x_in[:, t, :], x_dram[:, t, :]).then_inc(s_x, 16)
            sp.dma_start(pos_i[:], a["positions"].partition_broadcast(P).rearrange("p a b -> p (a b)")).then_inc(s_pos, 16)
            sp.dma_start(cst[:], a["const"][:, 256:NCONST]).then_inc(s_cst2, 16)

            for n in range(FIRST):
                g, ku = first_unit(n)
                if n == UPG:
                    sp.dma_start(w_di[0:64, :], a["w_decay_up"][0]).then_inc(s_small, 16)
                    sp.dma_start(w_di[64:128, :], a["w_iclr_up"][0]).then_inc(s_small, 16)
                    sp.dma_start(w_g[:], a["w_gate_up"][0, 0:128, :]).then_inc(s_small, 16)
                    sp.dma_start(w_g2[96:128, :], a["w_gate_up"][0, 128:160, :]).then_inc(s_small, 16)
                if n >= RING:
                    sp.wait_ge(s_lo, n - RING + 1)
                sp.dma_start(raw[:, slot_of(n)],
                             w_in[:, UK * ku:UK * ku + UK, g * CW:(g + 1) * CW]).then_inc(s_raw[slot_of(n)], 16)

            def w_in_group(g, shift):
                for ku in range(UPG):
                    sp.wait_ge(s_lo, g * UPG + (shift * UPG + ku - RING + 1))
                    sp.dma_start(raw[:, slot_of(ku)],
                                 w_in[:, UK * ku:UK * ku + UK, bass.ds(g * CW, CW)]).then_inc(s_raw[slot_of(ku)], 16)

            with sp.Fori(2, 6) as g:
                w_in_group(g, 0)
            for ku in range(UPG):
                sp.wait_ge(s_lo, 6 * UPG + ku - RING + 1)
                sp.dma_start(raw[:, slot_of(ku), :, 0:LORA_W],
                             w_in[:, UK * ku:UK * ku + UK, 6 * AW:6 * AW + LORA_W]).then_inc(s_raw[slot_of(ku)], 16)
            with sp.Fori(8, 10) as g:
                w_in_group(g, -1)
            with sp.Fori(6, 8) as g:
                w_in_group(g, 3)
            with sp.Fori(10, 12) as g:
                w_in_group(g, 1)
            with sp.Fori(0, OUT_G) as g:
                for ku in range(UPG):
                    sp.wait_ge(s_lo, g * UPG + (N_OUT0 + ku - RING + 1))
                    sp.dma_start(raw[:, slot_of(ku)],
                                 w_out[:, UK * ku:UK * ku + UK, bass.ts(g, CW)]).then_inc(s_raw[slot_of(ku)], 16)
            with sp.Fori(0, GU_G) as g:
                for m, w in enumerate((w_gate, w_up)):
                    for ku in range(UPG):
                        sp.wait_ge(s_lo, g * (2 * UPG) + (N_GU0 + m * UPG + ku - RING + 1))
                        sp.dma_start(raw[:, slot_of(ku)],
                                     w[:, UK * ku:UK * ku + UK, bass.ts(g, CW)]).then_inc(s_raw[slot_of(ku)], 16)
            with sp.Fori(0, OUT_G // 2) as g:
                for m in range(2):
                    for ku in range(DOWN_U):
                        j = m * DOWN_U + ku
                        sp.wait_ge(s_lo, g * (2 * DOWN_U) + (N_DOWN0 + j - RING + 1))
                        sp.dma_start(raw[:, slot_of(j)],
                                     w_down[:, UK * ku:UK * ku + UK, bass.ds(g * (2 * CW) + m * CW, CW)]
                                     ).then_inc(s_raw[slot_of(j)], 16)
            for t in range(NT):
                for half, cols in enumerate((slice(0, D // 2), slice(D // 2, D))):
                    sp.wait_ge(s_fs, 2 * t + half + 1)
                    sp.dma_start(out_dram[:, t, cols], x1[:, t, cols]).then_inc(s_out, 16)
            sp.wait_ge(s_out, 32 * NT)

        @block.gpsimd
        def _(pool):
            for u in range(INIT_ADA):
                g, ku = ada_order[u // UPG], u % UPG
                if u >= RING:
                    pool.wait_ge(s_adaused, u - RING + 1)
                pool.dma_start(ada_raw[:, u % RING],
                               w_ada[:, UK * ku:UK * ku + UK, g * CW:(g + 1) * CW]).then_inc(s_ada[u % RING], 16)
            def ada_group(g):
                for ku in range(UPG):
                    pool.wait_ge(s_adaused, g * UPG + (ku - RING + 1))
                    pool.dma_start(ada_raw[:, ku % RING],
                                   w_ada[:, UK * ku:UK * ku + UK, bass.ds(g * CW, CW)]
                                   ).then_inc(s_ada[ku % RING], 16)

            with pool.Fori(8, 15) as g:
                ada_group(g)
            pool.wait_ge(s_used, N_OUT0)
            for sd in sides:
                nc.gpsimd.memset(sd.br[:], 0.0)
                nc.gpsimd.memset(sd.kr[:], 0.0).then_inc(sd.s_blank, 1)
            nc.gpsimd.tensor_copy(sides[1].y1[:].rearrange("p l m t -> p (l m) t"),
                                  ident.unsqueeze(1).broadcast_to([P, 4 * LEVELS, P])).then_inc(sides[1].s_y1blank, 1)
            with pool.Fori(15, 20) as g:
                ada_group(g)
            pool.wait_ge(s_used, N_DOWN0)
            with pool.Fori(0, 4) as g:
                for ku in range(UPG):
                    pool.wait_ge(s_adaused, g * UPG + (END_ADA1 + ku - RING + 1))
                    pool.dma_start(ada_raw2[:, ku % RING],
                                   w_ada[:, UK * ku:UK * ku + UK, bass.ds(g * CW + 20 * CW, CW)]
                                   ).then_inc(s_ada[ku % RING], 16)
            pool.dma_start(nf_b[:], a["normf_g"].partition_broadcast(P)).then_inc(s_nf, 16)

        @block.scalar
        def _(act):
            def round_unit(n, width=CW):
                act.wait_ge(s_raw[slot_of(n)], 16 * (n // RING + 1))
                if n >= RING:
                    act.wait_ge(s_used, n - RING + 1)
                nc.scalar.activation(w_hi[:, slot_of(n), :, 0:width], raw[:, slot_of(n), :, 0:width],
                                     ACT.Copy).then_inc(s_hi, 1)

            act.wait_ge(s_vt, 1)
            nc.scalar.activation(vec[:], ps[4][:, 0:NVEC], ACT.Copy).then_inc(s_vec, 1)
            act.wait_ge(s_vec, 1)
            nc.scalar.activation(sig_c[:], vec[:, V_C:V_C + KT], ACT.Sigmoid).then_inc(s_sigc, 1)
            for t in range(NT):
                act.wait_ge(s_x, 16 * NT)
                nc.scalar.activation(xn_t[:, 8 * t:8 * t + 8, :].rearrange("p k t -> p (k t)"), x_in[:, t, :], ACT.Square,
                                     accum_out=stat[:, t:t + 1]).then_inc(s_ss, 1)
            act.wait_ge(s_ms, 1)
            nc.scalar.activation(stat[:, 4:6], stat[:, 2:4], ACT.Sqrt).then_inc(s_rt, 1)
            act.wait_ge(s_rms, 1)
            for t in range(NT):
                nc.scalar.activation(x_in[:, t, :], x_in[:, t, :], ACT.Copy, scale=stat[:, 4 + t:5 + t]).then_inc(s_xn, 1)
            for b in range(8):
                act.wait_ge(s_xt, b + 1)
                nc.scalar.activation(xn_t[:, 2 * b:2 * b + 2, :], ps[b][:, :].rearrange("p (k t) -> p k t", k=2),
                                     ACT.Copy).then_inc(s_xnt, 1)
            for j in range(4):
                if j == 2:
                    act.wait_ge(s_trig, 1)
                    nc.scalar.activation(sinT[:], ang[:], ACT.Sin)
                    nc.scalar.activation(cosT[:], turns[:], ACT.Sin).then_inc(s_sin, 1)
                for n in range(4 * j, 4 * j + 4):
                    round_unit(n)
                act.wait_ge(s_sc1, j + 1)
                for k in range(4 * j, 4 * j + 4):
                    last = nc.scalar.activation(xn_t[:, k, :], xn_t[:, k, :], ACT.Identity, bias=ada_t[:, k:k + 1],
                                                scale=scale1[:, k:k + 1])
                last.then_inc(s_hf, 1)
                act.wait_ge(s_hf, j + 1)
                nc.scalar.activation(h_hi[:, 4 * j:4 * j + 4, :], xn_t[:, 4 * j:4 * j + 4, :], ACT.Copy).then_inc(s_hhi, 1)

            def win_epilogue(pos):
                pb, gi = 2 * (pos % 2), WIN_ORDER[pos]
                act.wait_ge(s_used, FIRST - 2 if pos == 0 else UPG * (pos + 1))
                if gi < 4:
                    if gi:
                        act.wait_ge(s_rope, 2 * gi)
                    for b in range(2):
                        last = nc.scalar.activation(qraw[:, 2 * b:2 * b + 2, :],
                                                    ps[pb + b][:, :].rearrange("p (k t) -> p k t", k=2), ACT.Copy)
                elif gi < 6:
                    for t in range(NT):
                        last = nc.scalar.activation(v_tok[:, t, CW * (gi - 4):CW * (gi - 3)], ps[pb + t][:, :], ACT.Copy)
                else:
                    if pos == 6:
                        act.wait_ge(s_v0, 1)
                    elif pos == 7:
                        act.wait_ge(s_lora, 1)
                    else:
                        act.wait_ge(s_shift, pos - 7)
                    for b in range(2 if gi < 12 else 1):
                        last = nc.scalar.activation(ybuf[:, 2 * b:2 * b + 2, 1:T + 1],
                                                    ps[pb + b][:, :].rearrange("p (k t) -> p k t", k=2), ACT.Copy)
                    if gi == 12:
                        last = nc.scalar.activation(ybuf[:, 2, 1:T + 1], ps[pb + 1][:, 0:T], ACT.Copy)
                last.then_inc(s_evac, 1)

            def attn_exp(h):
                act.wait_ge(s_masked, h + 1)
                nc.scalar.activation(prob[:, 0, :], prob[:, 0, :], ACT.Exp, bias=stat[:, 6:7],
                                     accum_out=stat[:, 8:9])
                nc.scalar.activation(prob[:, 1:3, :], prob[:, 1:3, :], ACT.Exp, bias=stat[:, 7:8],
                                     accum_out=stat[:, 9:10]).then_inc(s_exp, 1)

            def attn_copy_pt(h):
                act.wait_ge(s_pt, h + 1)
                if h:
                    act.wait_ge(s_o, h)
                nc.scalar.activation(prob_t[:], ps[6][:, 0:3 * P].rearrange("p (k t) -> p k t", k=3),
                                     ACT.Copy).then_inc(s_ptc, 1)

            def attn_out(hp):
                act.wait_ge(s_o, 2 * hp + 2)
                nc.scalar.activation(mixa_hi[:, hp, :], ps[7][:, 0:T], ACT.Copy).then_inc(s_ohi, 1)

            def attn_slot(i):
                if 2 <= i < HEADS + 2 and i % 2 == 1:
                    attn_out((i - 3) // 2)
                if 1 <= i < HEADS + 1:
                    attn_copy_pt(i - 1)
                if i < HEADS:
                    attn_exp(i)

            def s1_inputs():
                act.wait_ge(s_lora, 1)
                nc.scalar.activation(lora[0:64, 0, :], lora[0:64, 0, :], ACT.Tanh)
                nc.scalar.activation(lora[:, 1, :], lora[:, 1, :], ACT.Sigmoid)
                nc.scalar.activation(lora[96:128, 2, :], lora[96:128, 2, :], ACT.Sigmoid).then_inc(s_lora, 1)

            def s1_squares(hp):
                act.wait_ge(s_kkr, hp + 1)
                if hp >= 2:
                    act.wait_ge(s_ssq, hp - 1)
                nc.scalar.activation(sq1[:, hp % 2, :], kk[:, hp, :], ACT.Square).then_inc(s_sqk, 1)

            def s1_rates(hp):
                act.wait_ge(s_zw, hp + 1)
                nc.scalar.activation(lw[:, hp, :], ps[4][:, 0:T], ACT.Sigmoid, bias=v1(V_W0 + hp))
                nc.scalar.activation(ab[:, hp, :], ps[6][:, 0:T], ACT.Sigmoid, bias=v1(V_A0 + hp)).then_inc(s_sigs, 1)

            for pos in range(WIN_G):
                for ku in range(UPG):
                    n = pos * UPG + ku
                    if n < FIRST:
                        continue
                    round_unit(n, LORA_W if pos == 6 else CW)
                    for done in at_unit(EVAC_AT, n):
                        win_epilogue(done)
                    u = n - 6 * UPG - 4 - LAG
                    if u >= 0 and u % 2 == 0 and u // 2 < HEADS + 2:
                        attn_slot(u // 2)
                    if n == S1_AT:
                        s1_inputs()
                    if 0 <= n - S1_AT - LAG < PAIRS:
                        s1_rates(n - S1_AT - LAG)
                    if 0 <= n - S1_AT < PAIRS:
                        s1_squares(n - S1_AT)
                    if n == S1_AT + PAIRS + LAG:
                        act.wait_ge(s_ssq, PAIRS)
                        nc.scalar.activation(rnc[:], ps[7][:, 0:4 * PAIRS], ACT.Sqrt).then_inc(s_rns, 1)
            def pair_exps(w, sd):
                act.wait_ge(sd.s_cen, w + 1)
                if w:
                    act.wait_ge(sd.s_op, w)
                nc.scalar.activation(sd.e3[:, 0, :], sd.cen[:, 0, :], ACT.Exp)
                nc.scalar.activation(sd.e3[:, 1, :], sd.cen[:, 0, :], ACT.Exp, scale=-1.0)
                nc.scalar.activation(sd.e3[:, 2, :], sd.cen[:, 1, :], ACT.Exp)
                nc.scalar.activation(sd.refc[:, w % 2, 3:4], sd.refc[:, w % 2, 2:3], ACT.Exp).then_inc(sd.s_e3, 1)

            def set_identity(sd):
                nc.scalar.activation(sd.xm[:], over4(ident), ACT.Copy)
                nc.scalar.activation(sd.xt[:], over4(ident), ACT.Copy).then_inc(sd.s_eye, 1)

            pair_exps(0, sides[0])
            win_epilogue(WIN_G - 1)
            set_identity(sides[0])
            nc.scalar.activation(sides[0].y1[:].rearrange("p l m t -> p (l m) t"),
                                 ident.unsqueeze(1).broadcast_to([P, 4 * LEVELS, P]), ACT.Copy).then_inc(sides[0].s_y1blank, 1)
            pair_exps(0, sides[1])
            set_identity(sides[1])

            def finish(hp):
                act.wait_ge(s_mixf, hp + 1)
                nc.scalar.activation(mixr_hi[:, hp, :], lw[:, hp, :], ACT.Copy).then_inc(s_mrhi, 1)

            for slot, w, i, step, nth in turns_of:
                sd, hp = sides[i], 2 * w + i
                if slot == SIDE0_END:
                    act.wait_ge(sides[0].s_bonus, WAVES)
                    nc.scalar.activation(varc[:, 0:28], varc[:, 0:28], ACT.Sqrt).then_inc(s_sd, 1)
                if 0 < slot - SIDE0_END < PAIRS:
                    finish(slot - SIDE0_END - 1)
                if step == "x":
                    lev, b = nth, 2 << nth
                    if lev < LEVELS - 1:
                        act.wait_ge(sd.s_xx, w * (LEVELS - 1) + lev + 1)
                        nc.scalar.activation(blocks(sd.xm[:], b, 0), blocks(four(sd.bank[1]), b, 0), ACT.Copy).then_inc(sd.s_xm, 1)
                    act.wait_ge(sd.s_xxt, w * LEVELS + lev + 1)
                    nc.scalar.activation(blocks(sd.xt[:], b, 1), blocks(four(sd.bank[2]), b, 1), ACT.Copy).then_inc(sd.s_xt, 1)
                elif step == "tokens":
                    act.wait_ge(sd.s_tv, w + 1)
                    nc.scalar.activation(sd.tv[:], four(7), ACT.Copy).then_inc(sd.s_tvc, 1)
                elif step == "u":
                    act.wait_ge(sd.s_u, 2 * w + nth + 1)
                    nc.scalar.activation(sd.us[:, 0, :], ps[sd.bank[0]][:, 0:HD], ACT.Copy)
                    nc.scalar.activation(sd.us[:, 1, :], ps[sd.bank[1]][:, 0:HD], ACT.Copy).then_inc(sd.s_uc, 1)
                elif step == "solve":
                    act.wait_ge(sd.s_sa, 2 * w + nth + 1)
                    nc.scalar.activation(sd.sa[:, nth], ps[sd.bank[2]][:, 0:2 * HD].rearrange("p (e d) -> p e d", e=2),
                                         ACT.Copy).then_inc(sd.s_sac, 1)
                elif step == "state":
                    act.wait_ge(sd.s_st, w + 1)
                    nc.scalar.activation(sd.s0[:], ps[sd.bank[2]][:, 2 * HD:3 * HD], ACT.Copy,
                                         scale=sd.refc[:, w % 2, 3:4]).then_inc(sd.s_stc, 1)
                    if w + 1 < WAVES:
                        pair_exps(w + 1, sd)
                elif step == "out":
                    act.wait_ge(sd.s_ot, w + 1)
                    nc.scalar.activation(sd.o_t[0:64, :], ps[sd.bank[0]][0:64, 0:T], ACT.Copy)
                    nc.scalar.activation(sd.o_t[64:128, :], ps[sd.bank[1]][64:128, 0:T], ACT.Copy).then_inc(sd.s_otc, 1)
                    if w + 1 < WAVES:
                        set_identity(sd)
                elif step == "mean":
                    act.wait_ge(sd.s_dev, w + 1)
                    nc.scalar.activation(sd.sq[:], lw[:, hp, :], ACT.Square).then_inc(sd.s_dsq, 1)
            act.wait_ge(sides[1].s_bonus, WAVES)
            nc.scalar.activation(varc[:, 28:32], varc[:, 28:32], ACT.Sqrt).then_inc(s_sd, 1)
            round_unit(N_OUT0)
            finish(PAIRS - 1)

            def gate_copy(i, dst):
                act.wait_ge(s_gt, i + 1)
                if i:
                    act.wait_ge(s_x1, 2 * i)
                nc.scalar.activation(dst[:], ps[4][:, :], ACT.Copy).then_inc(s_gtb, 1)

            def square_sums(i, junk):
                ct = i % 4
                for t in range(NT):
                    act.wait_ge(s_x1, 2 * i + t + 1)
                    if i or t:
                        act.wait_ge(s_ssp, 2 * i + t)
                    ins = nc.scalar.activation(junk[:], x1[:, t, ct * CW:(ct + 1) * CW], ACT.Square,
                                               accum_out=stat[:, 10 + 4 * t + ct:11 + 4 * t + ct])
                    ins.then_inc(s_ssp, 1)

            for g in range(OUT_G):
                for ku in range(UPG):
                    if g or ku:
                        round_unit(N_OUT0 + g * UPG + ku)
                    if g == 0 and ku == 3:
                        act.wait_ge(s_mixr, PAIRS)
                        act.dma_start(x1[:], x_dram).then_inc(s_x1in, 16)
                    if g and ku == 2:
                        gate_copy(g - 1, gtb)
                    if g and ku == 4:
                        square_sums(g - 1, sqj1)
                    if g == OUT_G - 1 and ku == UPG - 1:
                        gate_copy(g, gtb)
            for n in range(RING - 1):
                round_unit(N_GU0 + n)
            square_sums(OUT_G - 1, sqj1)
            act.wait_ge(s_ms2, 1)
            nc.scalar.activation(stat[:, 4:6], stat[:, 2:4], ACT.Sqrt).then_inc(s_rt2, 1)
            round_unit(N_GU0 + RING - 1)
            for j in range(4):
                if j >= 2:
                    act.wait_ge(s_h2lo, j - 1)
                for b in range(2):
                    act.wait_ge(s_x2t, 2 * j + b + 1)
                    for kx in range(2):
                        k = 4 * j + 2 * b + kx
                        last = nc.scalar.activation(h2f[:, j % 2, 2 * b + kx, :],
                                                    ps[X2T_BANKS[2 * j + b]][:, kx * T:(kx + 1) * T], ACT.Identity,
                                                    bias=ada_t[:, 48 + k:49 + k], scale=scale2[:, k:k + 1])
                last.then_inc(s_h2f, 1)
                act.wait_ge(s_h2f, j + 1)
                nc.scalar.activation(h_hi[:, 4 * j:4 * j + 4, :], h2f[:, j % 2], ACT.Copy).then_inc(s_h2hi, 1)

            def ffn_silu(gn, parity):
                act.wait_ge(s_used, gn * (2 * UPG) + (N_GU0 + 2 * UPG))
                for b in range(2):
                    last = nc.scalar.activation(sg[:, parity, 2 * b:2 * b + 2, :],
                                                ps[4 * parity + b][:, :].rearrange("p (k t) -> p k t", k=2), ACT.Silu)
                last.then_inc(s_silu, 1)

            def ffn_hi(gn, parity):
                act.wait_ge(s_prod, gn + 1)
                nc.scalar.activation(act_hi[:, bass.ds(gn * 4, 4), :], sg[:, parity], ACT.Copy).then_inc(s_ahi, 1)

            def round_gu(it, j):
                act.wait_ge(s_raw[j % RING], it * (2 * UPG // RING * 16) + 16 * ((N_GU0 + j) // RING + 1))
                act.wait_ge(s_used, it * (2 * UPG) + (N_GU0 + j - RING + 1))
                nc.scalar.activation(w_hi[:, j % RING], raw[:, j % RING], ACT.Copy).then_inc(s_hi, 1)

            for j in range(RING, 2 * UPG):
                round_gu(0, j)
            with act.Fori(0, (GU_G - 1) // 2) as it:
                for half in range(2):
                    for j in range(2 * UPG):
                        round_gu(it * 2, 2 * UPG * (1 + half) + j)
                        if j == 2:
                            ffn_silu(it * 2 + half, half)
                        if j == 5:
                            ffn_hi(it * 2 + half, half)
            ffn_silu(GU_G - 1, 0)
            for n in range(N_DOWN0, N_DOWN0 + 2):
                round_unit(n)
            ffn_hi(GU_G - 1, 0)
            for g in range(OUT_G):
                for ku in range(DOWN_U):
                    n = N_DOWN0 + g * DOWN_U + ku
                    if n >= N_DOWN0 + 2:
                        round_unit(n)
                    if g and ku == 2:
                        gate_copy(OUT_G + g - 1, gtb2)
                    if g and ku == 4:
                        square_sums(OUT_G + g - 1, sqj)
            gate_copy(2 * OUT_G - 1, gtb2)
            nc.scalar.activation(stat[:, 6:8], stat[:, 2:4], ACT.Sqrt)
            square_sums(2 * OUT_G - 1, sqj)
            act.wait_ge(s_ms2, 2)
            nc.scalar.activation(stat[:, 4:6], stat[:, 2:4], ACT.Sqrt).then_inc(s_rt2, 1)

        @block.vector
        def _(dve):
            links = [0]

            def link(ins):
                links[0] += 1
                ins.then_inc(s_dch, 1)
                dve.wait_ge(s_dch, links[0])

            def rest_unit(n, width=CW):
                dve.wait_ge(s_hi, n + 1)
                nc.vector.tensor_tensor(w_lo[:, slot_of(n), :, 0:width], raw[:, slot_of(n), :, 0:width],
                                        w_hi[:, slot_of(n), :, 0:width].bitcast(F32), ALU.subtract).then_inc(s_lo, 1)

            def ada_unit(u):
                g, ku = u // UPG, u % UPG
                buf = ada_raw2 if u >= END_ADA1 else ada_raw
                dve.wait_ge(s_ada[u % RING], 16 * (u // RING + 1))
                if ku == 0 and g >= 2:
                    dve.wait_ge(s_fin, g - 1)
                dst = acc[:, g % 2, :]
                for kx in range(UK):
                    k = UK * ku + kx
                    if k == 0:
                        link(nc.vector.tensor_scalar(dst, buf[:, u % RING, kx, :], silu_c[:, k:k + 1], None, ALU.mult))
                    elif kx == 0:
                        link(nc.vector.scalar_tensor_tensor(dst, buf[:, u % RING, kx, :], silu_c[:, k:k + 1], dst,
                                                            ALU.mult, ALU.add))
                    else:
                        nc.vector.scalar_tensor_tensor(dst, buf[:, u % RING, kx, :], silu_c[:, k:k + 1], dst,
                                                       ALU.mult, ALU.add).then_inc(s_adaused, 1)
                dve.wait_ge(s_adaused, u + 1)

            def ada_cols(g):
                c = 4 * ada_order[g]
                dve.wait_ge(s_fin, g + 1)
                nc.vector.tensor_tensor(ada_t[:, c:c + 4], ps[FIN][:, 0:4], vec[:, V_B + c:V_B + c + 4],
                                        ALU.add).then_inc(s_col, 1)
                dve.wait_ge(s_col, g + 1)

            def first_h(j):
                nc.vector.scalar_tensor_tensor(scale1[:, 4 * j:4 * j + 4], ada_t[:, 16 + 4 * j:20 + 4 * j], 1.0,
                                               vec[:, V_N1 + 4 * j:V_N1 + 4 * j + 4], ALU.add, ALU.mult).then_inc(s_sc1, 1)
                dve.wait_ge(s_hhi, j + 1)
                nc.vector.tensor_tensor(h_lo[:, 4 * j:4 * j + 4, :], xn_t[:, 4 * j:4 * j + 4, :],
                                        h_hi[:, 4 * j:4 * j + 4, :].bitcast(F32), ALU.subtract).then_inc(s_hlo, 1)

            def angles():
                dve.wait_ge(s_pos, 16)
                dve.wait_ge(s_cst2, 16)
                link(nc.vector.tensor_copy(ang[:], pos_i[:]))
                link(nc.vector.tensor_scalar(ang[:], ang[:], ck(C_INV, 1), None, ALU.mult))
                magic = 12582912.0
                link(nc.vector.tensor_scalar(turns[:], ang[:], 1.0 / (2 * math.pi), magic, ALU.mult, ALU.add))
                link(nc.vector.tensor_scalar(turns[:], turns[:], magic, None, ALU.subtract))
                for part in (6.28125, 0.0019340515136718750, 1.2556659146019e-06):
                    link(nc.vector.scalar_tensor_tensor(ang[:], turns[:], -part, ang[:], ALU.mult, ALU.add))
                link(nc.vector.tensor_scalar(ang[:], ang[:], 3.1415925, -3.1415925, ALU.min, ALU.max))
                link(nc.vector.tensor_scalar(turns[:], ang[:], -1.0, None, ALU.mult))
                link(nc.vector.tensor_tensor(turns[:], turns[:], ang[:], ALU.max))
                nc.vector.tensor_scalar(turns[:], turns[:], -1.0, math.pi / 2, ALU.mult, ALU.add).then_inc(s_trig, 1)

            dve.wait_ge(s_sigc, 1)
            nc.vector.tensor_tensor(silu_c[:], vec[:, V_C:V_C + KT], sig_c[:], ALU.mult).then_inc(s_siluc, 1)
            dve.wait_ge(s_siluc, 1)
            for u in range(INIT_ADA):
                ada_unit(u)
                if u == X_STATS:
                    dve.wait_ge(s_ss, NT)
                    nc.vector.tensor_scalar(stat[:, 2:4], stat[:, 0:2], 1.0 / D, RMS_EPS, ALU.mult, ALU.add).then_inc(s_ms, 1)
                if u == X_STATS + 1:
                    dve.wait_ge(s_rt, 1)
                    nc.vector.reciprocal(stat[:, 4:6], stat[:, 4:6]).then_inc(s_rms, 1)
                if u == ANGLES:
                    angles()
                j, i = u // (2 * UPG) - 1, u % (2 * UPG)
                if i == 11:
                    ada_cols(2 * (u // (2 * UPG)))
                if j >= 0 and i == 2:
                    ada_cols(2 * j + 1)
                    first_h(j)
                if j >= 0 and i in (3, 4, 5, 6):
                    rest_unit(4 * j + i - 3)
            ada_cols(7)
            first_h(3)
            for n in range(12, 16):
                rest_unit(n)
            nc.vector.memset(ybuf[:, :, 0:1], 0.0).then_inc(s_v0, 1)

            def win_epilogue(pos):
                gi = WIN_ORDER[pos]
                if gi < 4:
                    dve.wait_ge(s_sin, 1)
                    for b in range(2):
                        i = 2 * gi + b
                        dve.wait_ge(s_perm, i + 1)
                        dst = qk[:, 4 * gi + 2 * b:4 * gi + 2 * b + 2, :]
                        cos2 = cosT[:].unsqueeze(1).broadcast_to([P, 2, T])
                        sin2 = sinT[:].unsqueeze(1).broadcast_to([P, 2, T])
                        if i:
                            dve.wait_ge(s_rope, i)
                        nc.vector.tensor_tensor(t1[:], ps[6 + b][:, :].rearrange("p (k t) -> p k t", k=2), sin2, ALU.mult)
                        link(nc.vector.tensor_tensor(dst, qraw[:, 2 * b:2 * b + 2, :], cos2, ALU.mult))
                        nc.vector.tensor_tensor(dst, dst, t1[:], ALU.add).then_inc(s_rope, 1)
                elif gi >= 6:
                    dve.wait_ge(s_evac, pos + 1)
                    if pos == 6:
                        dve.wait_ge(s_v0, 1)
                    n = 4 if gi < 12 else 3
                    dst = rkv[:, 4 * (gi - 6):4 * (gi - 6) + 4, :] if gi < 12 else lora[:, :, :]
                    link(nc.vector.tensor_tensor(dst, ybuf[:, 0:n, 0:T], ybuf[:, 0:n, 1:T + 1], ALU.subtract))
                    for i in range(n):
                        last = nc.vector.scalar_tensor_tensor(dst[:, i, :], dst[:, i, :], v1(V_MU + 4 * (gi - 6) + i),
                                                              ybuf[:, i, 1:T + 1], ALU.mult, ALU.add)
                    last.then_inc(s_shift if gi < 12 else s_lora, 1)

            def attn_mask(h):
                dve.wait_ge(s_score, h + 1)
                if h:
                    dve.wait_ge(s_pt, h)
                link(nc.vector.scalar_tensor_tensor(prob[:], ps[4][:, 0:3 * P].rearrange("p (k t) -> p k t", k=3),
                                                    HD ** -0.5, ck(C_LC, 3 * P).rearrange("p (k t) -> p k t", k=3),
                                                    ALU.mult, ALU.add))
                nc.vector.tensor_reduce(stat[:, 6:7], prob[:, 0, :], axis=AX, op=ALU.max, negate=True)
                nc.vector.tensor_reduce(stat[:, 7:8], prob[:, 1:3, :].rearrange("p k t -> p (k t)"), axis=AX,
                                        op=ALU.max, negate=True).then_inc(s_masked, 1)

            def attn_norm(h):
                dve.wait_ge(s_exp, h + 1)
                link(nc.vector.reciprocal(stat[:, 8:10], stat[:, 8:10]))
                nc.vector.tensor_scalar(prob[:, 0, :], prob[:, 0, :], stat[:, 8:9], None, ALU.mult)
                nc.vector.tensor_scalar(prob[:, 1:3, :], prob[:, 1:3, :], stat[:, 9:10], None, ALU.mult).then_inc(s_prob, 1)

            def attn_rest(hp):
                dve.wait_ge(s_ohi, hp + 1)
                nc.vector.tensor_tensor(mixa_lo[:, hp, :], ps[7][:, 0:T], mixa_hi[:, hp, :].bitcast(F32),
                                        ALU.subtract).then_inc(s_mixa, 1)

            def attn_slot(i):
                if 2 <= i < HEADS + 2 and i % 2 == 1:
                    attn_rest((i - 3) // 2)
                if i < HEADS:
                    attn_mask(i)

            ada_next = [INIT_ADA]

            def ada_step(limit):
                if ada_next[0] < limit:
                    u = ada_next[0]
                    ada_unit(u)
                    ada_next[0] += 1

            def s1_keys(hp):
                nc.vector.tensor_scalar(kk[:, hp, :], rkv[:, 8 + hp, :], v1(V_KK + hp), None, ALU.mult).then_inc(s_kkr, 1)

            def s1_update(hp):
                dve.wait_ge(s_sigs, hp + 1)
                link(nc.vector.tensor_scalar(ka1[:, hp % 2, :], ab[:, hp, :], 1.0, v1(V_KA + hp), ALU.subtract, ALU.mult))
                nc.vector.tensor_scalar(lw[:, hp, :], lw[:, hp, :], -SQ, None, ALU.mult)
                link(nc.vector.scalar_tensor_tensor(rkv[:, 8 + hp, :], ka1[:, hp % 2, :], 1.0, rkv[:, 8 + hp, :], ALU.add,
                                                    ALU.mult))

            for pos in range(WIN_G):
                for ku in range(UPG):
                    n = pos * UPG + ku
                    if n < FIRST:
                        continue
                    rest_unit(n, LORA_W if pos == 6 else CW)
                    for done in at_unit(EPI_AT, n):
                        win_epilogue(done)
                    u = n - 6 * UPG - 4 - LAG
                    if u >= 0 and u % 2 == 0 and u // 2 < HEADS + 2:
                        attn_slot(u // 2)
                    if u >= 0 and u % 2 == 1 and u // 2 < HEADS:
                        attn_norm(u // 2)
                    if ada_due(n):
                        ada_step(END_ADA1)
                    for g in at_unit(FIN_AT, n - LAG):
                        ada_cols(g)
                    if 0 <= n - S1_AT < PAIRS:
                        s1_keys(n - S1_AT)
                    if 0 <= n - S1_AT - LAG - 1 < PAIRS:
                        s1_update(n - S1_AT - LAG - 1)
                    if n == S1_AT + PAIRS + LAG:
                        dve.wait_ge(s_rns, 1)
                        link(nc.vector.tensor_scalar(rnc[:], rnc[:], 1e-12, None, ALU.max))
                        nc.vector.reciprocal(rnc[:], rnc[:]).then_inc(s_rnc, 1)
            def decays(w, i):
                sd, hp = sides[i], 2 * w + i
                cen, refc = sd.cen, sd.refc[:, w % 2, :]
                if w:
                    dve.wait_ge(sd.s_e3, w)
                link(nc.vector.tensor_tensor_scan(cen[:, 0, :], ck(C_RES, T), lw[:, hp, :], 0.0, ALU.mult, ALU.add))
                c4 = cen[:, 0, :].rearrange("p (c b t) -> p c b t", c=2, b=2)
                link(nc.vector.tensor_copy(refc[:, 0:2], c4[:, :, 0, 63]))
                for c in range(2):
                    x = cen[:, 0, 128 * c:128 * c + 64]
                    ins = nc.vector.tensor_scalar(x, x, refc[:, c:c + 1], None, ALU.subtract)
                link(ins)
                nc.vector.tensor_tensor(refc[:, 2:3], refc[:, 1:2], cen[:, 0, 127:128], ALU.add)
                nc.vector.tensor_tensor(cen[:, 1, :], cen[:, 0, :], lw[:, hp, :], ALU.subtract).then_inc(sd.s_cen, 1)

            decays(0, 0)

            def unit_keys(hp):
                dve.wait_ge(s_rnb, hp // 2 + 1)
                link(nc.vector.tensor_tensor(kk[:, hp, :], kk[:, hp, :], ps[RN_BANKS[hp // 2]][:, T * (hp % 2):T * (hp % 2) + T], ALU.mult))
                return nc.vector.tensor_tensor(ab[:, hp, :], ab[:, hp, :], kk[:, hp, :], ALU.mult)

            def operands(w, i):
                sd, hp = sides[i], 2 * w + i
                op, e3 = sd.op, sd.e3
                dve.wait_ge(sd.s_e3, w + 1)
                if w:
                    dve.wait_ge(sd.s_ot, w)
                nc.vector.scalar_tensor_tensor(op[:, 0, :], kk[:, hp, :], -1.0, e3[:, 2, :], ALU.mult, ALU.mult)
                nc.vector.tensor_tensor(op[:, 1, :], rkv[:, hp, :], e3[:, 0, :], ALU.mult)
                nc.vector.tensor_tensor(op[:, 2, :], ab[:, hp, :], e3[:, 1, :], ALU.mult)
                nc.vector.tensor_tensor(op[:, 3, :], rkv[:, 8 + hp, :], e3[:, 1, :], ALU.mult).then_inc(sd.s_op, 1)

            strict_incl = ck(C_SI, T).bitcast(I32).unsqueeze(1).broadcast_to([P, 2, T])
            m0 = ck(C_M0).bitcast(I32).unsqueeze(1).broadcast_to([P, 2, P])
            m0t = ck(C_M0T).bitcast(I32).unsqueeze(1).broadcast_to([P, 2, P])

            def first_grams(w, i):
                sd = sides[i]
                dve.wait_ge(sd.s_gram, w + 1)
                dve.wait_ge(sd.s_eye, w + 1)
                if w == 0:
                    dve.wait_ge(sd.s_blank, 1)
                for e in range(2):
                    bank, c0 = (sd.bank[2], 0) if e == 0 else ((7, FIN)[i], T)
                    ins = nc.vector.copy_predicated(sd.xm[:, 2 * e:2 * e + 2, :], m0,
                                                    ps[bank][:, c0:c0 + T].rearrange("p (c s) -> p c s", c=2))
                ins.then_inc(sd.s_gramc, 1)
                for e in range(2):
                    nc.vector.copy_predicated(sd.br[:, 2 * e:2 * e + 2, :], strict_incl,
                                              ps[sd.bank[e]][:, :].rearrange("p (c s) -> p c s", c=2))
                for e in range(2):
                    ins = nc.vector.copy_predicated(sd.xt[:, 2 * e:2 * e + 2, :], m0t,
                                                    ps[sd.bank[e]][:, :].rearrange("p (c s) -> p c s", c=2)[:, :, 0:P])
                ins.then_inc(sd.s_gramc, 1)

            def key_grams(w, i):
                sd = sides[i]
                dve.wait_ge(sd.s_krg, w + 1)
                for e in range(2):
                    ins = nc.vector.copy_predicated(sd.kr[:, 2 * e:2 * e + 2, :], strict_incl,
                                                    ps[(sd.bank[2], 7)[e]][:, :].rearrange("p (c s) -> p c s", c=2))
                ins.then_inc(sd.s_krc, 1)

            def level(w, i, lev):
                sd, b = sides[i], 2 << lev
                dve.wait_ge(sd.s_y, w * LEVELS + lev + 1)
                if w == 0 and lev == 0:
                    dve.wait_ge(sd.s_y1blank, 1)
                mask = ck(C_LEV + P * lev).bitcast(I32).rearrange("p (n two b) -> p n two b", two=2, b=b)[:, :, 0, :]
                nc.vector.copy_predicated(blocks(sd.y1[:, lev], b, 0), mask.unsqueeze(1).broadcast_to([P, 4, HD // b, b]),
                                          blocks(four(sd.bank[0]), b, 0)).then_inc(sd.s_y1, 1)

            unit_keys(0)
            link(unit_keys(1))
            dve.wait_ge(s_used, N_OUT0)
            operands(0, 0)
            for hp in range(2, PAIRS):
                last = unit_keys(hp)
            last.then_inc(s_pre, 1)
            def finish(hp):
                dve.wait_ge(s_g, hp + 1)
                y = lw[:, hp, :]
                pb = FINISH_BANKS[hp]
                link(nc.vector.scalar_tensor_tensor(y, ps[pb][:, 0:T], v1(V_GG + hp), y, ALU.mult, ALU.mult))
                link(nc.vector.scalar_tensor_tensor(y, y, v1(V_GB + hp), rkv[:, hp, :], ALU.add, ALU.add))
                nc.vector.tensor_tensor(y, y, ps[pb][:, T:2 * T], ALU.mult).then_inc(s_mixf, 1)

            def finish_rest(hp):
                dve.wait_ge(s_mrhi, hp + 1)
                nc.vector.tensor_tensor(mixr_lo[:, hp, :], lw[:, hp, :], mixr_hi[:, hp, :].bitcast(F32),
                                        ALU.subtract).then_inc(s_mixr, 1)

            last_slot = -1
            for slot, w, i, step, nth in turns_of:
                sd, hp = sides[i], 2 * w + i
                if slot != last_slot:
                    last_slot = slot
                    if slot == 1:
                        win_epilogue(WIN_G - 1)
                    elif slot == 2:
                        dve.wait_ge(s_shift, 6)
                        decays(0, 1)
                    elif slot == 4:
                        dve.wait_ge(s_pre, 1)
                        operands(0, 1)
                    if slot % 3 == 2:
                        ada_step(RWKV_ADA_END)
                    if slot - 2 in FIN_SLOT:
                        ada_cols(14 + FIN_SLOT.index(slot - 2))
                    if slot == SIDE0_END:
                        dve.wait_ge(s_sd, 1)
                        nc.vector.reciprocal(varc[:, 0:28], varc[:, 0:28]).then_inc(s_rstd, 1)
                    if 0 < slot - SIDE0_END < PAIRS:
                        finish(slot - SIDE0_END - 1)
                    if 1 < slot - SIDE0_END <= PAIRS:
                        finish_rest(slot - SIDE0_END - 2)
                if step == "gram":
                    first_grams(w, i)
                elif step == "y":
                    level(w, i, nth)
                elif step == "keys":
                    key_grams(w, i)
                elif step == "u" and nth == 0:
                    if w + 1 < WAVES:
                        decays(w + 1, i)
                    nc.vector.scalar_tensor_tensor(rkv[:, hp, :], rkv[:, hp, :], v1(V_RK + hp), rkv[:, 8 + hp, :],
                                                   ALU.mult, ALU.mult).then_inc(sd.s_bon, 1)
                elif step == "mean":
                    dve.wait_ge(sd.s_mean, w + 1)
                    nc.vector.scalar_tensor_tensor(lw[:, hp, :], ps[sd.bank[2]][:, 0:T], -1.0 / HD, sd.o_t[:], ALU.mult,
                                                   ALU.add).then_inc(sd.s_dev, 1)
                    if w + 1 < WAVES:
                        operands(w + 1, i)
                elif step == "var":
                    dve.wait_ge(sd.s_var, w + 1)
                    nc.vector.tensor_scalar(varc[:, 4 * hp:4 * hp + 4], ps[sd.bank[0]][:, 0:4], 1.0 / HD, GN_EPS,
                                            ALU.mult, ALU.add)
                    nc.vector.tensor_tensor(rkv[:, hp, :], ps[sd.bank[1]][:, 0:T], rkv[:, 16 + hp, :],
                                            ALU.mult).then_inc(sd.s_bonus, 1)
            dve.wait_ge(s_sd, 2)
            nc.vector.reciprocal(varc[:, 28:32], varc[:, 28:32]).then_inc(s_rstd, 1)
            dve.wait_ge(sides[1].s_bonus, WAVES)
            rest_unit(N_OUT0)
            finish(PAIRS - 1)
            finish_rest(PAIRS - 1)

            def gate_diag(i, dst):
                c = (8 if i < 4 else 20) * 4 + 4 * (i % 4)
                if i:
                    dve.wait_ge(s_gt, i)
                nc.vector.tensor_tensor(dst[:].rearrange("p (k t) -> p k t", k=4), over4(ident),
                                        ada_t[:, c:c + 4].unsqueeze(2).broadcast_to([P, 4, P]), ALU.mult).then_inc(s_diag, 1)

            def residual(i, gate, tmp, banks):
                ct = i % 4
                dve.wait_ge(s_gtb, i + 1)
                if i == 0:
                    dve.wait_ge(s_x1in, 16)
                dve.wait_ge(s_used, N_OUT0 + UPG * (i + 1) if i < 4 else N_DOWN0 + DOWN_U * (i - 3))
                for t in range(NT):
                    if i or t:
                        dve.wait_ge(s_x1, 2 * i + t)
                    link(nc.vector.tensor_tensor(tmp[:], ps[banks + t][:, :], gate[:], ALU.mult))
                    x = x1[:, t, ct * CW:(ct + 1) * CW]
                    nc.vector.tensor_tensor(x, x, tmp[:], ALU.add).then_inc(s_x1, 1)

            def row_rms(i):
                dve.wait_ge(s_ssp, 8 * (i + 1))
                link(nc.vector.tensor_reduce(stat[:, 2:4], stat[:, 10:18].rearrange("p (t c) -> p t c", t=2), axis=AX, op=ALU.add))
                nc.vector.tensor_scalar(stat[:, 2:4], stat[:, 2:4], 1.0 / D, RMS_EPS, ALU.mult, ALU.add).then_inc(s_ms2, 1)
                dve.wait_ge(s_rt2, i + 1)
                link(nc.vector.reciprocal(stat[:, 4:6], stat[:, 4:6]))

            for g in range(OUT_G):
                for ku in range(UPG):
                    n_out = g * UPG + ku
                    if n_out:
                        rest_unit(N_OUT0 + n_out)
                    ada_step(END_ADA1)
                    if ku == 1:
                        gate_diag(g, diag)
                    if g and ku == 4:
                        residual(g - 1, gtb, upd, 2 * ((g - 1) % 2))
                    if n_out == 8:
                        ada_cols(18)
                    if n_out == 18:
                        ada_cols(19)
            link(nc.vector.scalar_tensor_tensor(scale2[:], ada_t[:, 64:80], 1.0, vec[:, V_N2:V_N2 + KT], ALU.add, ALU.mult))
            for n in range(RING - 1):
                rest_unit(N_GU0 + n)
            residual(OUT_G - 1, gtb, upd, 2)
            row_rms(0)
            for t in range(NT):
                nc.vector.tensor_scalar(rsd[:, t, :], ident, stat[:, 4 + t:5 + t], None, ALU.mult).then_inc(s_xn2, 1)
            rest_unit(N_GU0 + RING - 1)
            for j in range(4):
                dve.wait_ge(s_h2hi, j + 1)
                nc.vector.tensor_tensor(h_lo[:, 4 * j:4 * j + 4, :], h2f[:, j % 2], h_hi[:, 4 * j:4 * j + 4, :].bitcast(F32),
                                        ALU.subtract).then_inc(s_h2lo, 1)

            def ffn_product(gn, parity):
                dve.wait_ge(s_silu, gn + 1)
                for b in range(2):
                    x = sg[:, parity, 2 * b:2 * b + 2, :]
                    last = nc.vector.tensor_tensor(x, x, ps[4 * parity + 2 + b][:, :].rearrange("p (k t) -> p k t", k=2), ALU.mult)
                last.then_inc(s_prod, 1)

            def ffn_lo(gn, parity):
                dve.wait_ge(s_ahi, gn + 1)
                nc.vector.tensor_tensor(act_lo[:, bass.ds(gn * 4, 4), :], sg[:, parity],
                                        act_hi[:, bass.ds(gn * 4, 4), :].bitcast(F32), ALU.subtract).then_inc(s_alo, 1)

            def rest_gu(it, j):
                dve.wait_ge(s_hi, it * (2 * UPG) + (N_GU0 + j + 1))
                nc.vector.tensor_tensor(w_lo[:, j % RING], raw[:, j % RING], w_hi[:, j % RING].bitcast(F32),
                                        ALU.subtract).then_inc(s_lo, 1)

            for j in range(RING, 2 * UPG):
                rest_gu(0, j)
            with dve.Fori(0, (GU_G - 1) // 2) as it:
                for half in range(2):
                    for j in range(2 * UPG):
                        rest_gu(it * 2, 2 * UPG * (1 + half) + j)
                        if j == 3:
                            ffn_product(it * 2 + half, half)
                        if j == 7:
                            ffn_lo(it * 2 + half, half)
            ffn_product(GU_G - 1, 0)
            for n in range(N_DOWN0, N_DOWN0 + 2):
                rest_unit(n)
            ffn_lo(GU_G - 1, 0)
            for g in range(OUT_G):
                for ku in range(DOWN_U):
                    n = N_DOWN0 + g * DOWN_U + ku
                    if n >= N_DOWN0 + 2:
                        rest_unit(n)
                    if ku % 2 == 0 and ku < 2 * UPG:
                        ada_unit(END_ADA1 + g * UPG + ku // 2)
                    if ku == DOWN_U - 3:
                        ada_cols(20 + g)
                        gate_diag(OUT_G + g, diag2)
                    if g and ku == 4:
                        residual(OUT_G + g - 1, gtb2, upd2, 2 * ((g - 1) % 2))
            residual(2 * OUT_G - 1, gtb2, upd2, 2)
            row_rms(1)
            dve.wait_ge(s_nf, 16)
            for t in range(NT):
                for cols in (slice(0, D // 2), slice(D // 2, D)):
                    nc.vector.scalar_tensor_tensor(x1[:, t, cols], x1[:, t, cols], stat[:, 4 + t:5 + t], nf_b[:, cols],
                                                   ALU.mult, ALU.mult).then_inc(s_fs, 1)

        @block.tensor
        def _(pe):
            mm = nc.tensor.matmul

            def three_pass(out, sh, sl, mh, ml, first, last, shared=False):
                mm(out, sh, mh, start=first, stop=False, skip_group_check=shared)
                mm(out, sh, ml, start=False, stop=False, skip_group_check=shared)
                return mm(out, sl, mh, start=False, stop=last, skip_group_check=shared)

            def unit_channels(n, ku, pb, hi, lo, blocks):
                pe.wait_ge(s_lo, n + 1)
                for i, c0 in enumerate(blocks):
                    for kx in range(UK):
                        k = UK * ku + kx
                        out = ps[pb + i // 2][:, (i % 2) * T:(i % 2 + 1) * T]
                        w = slice(c0, c0 + P)
                        last = three_pass(out, w_hi[:, n % RING, kx, w], w_lo[:, n % RING, kx, w], hi[:, k, :], lo[:, k, :],
                                          first=(k == 0 and i % 2 == 0), last=(k == KT - 1), shared=True)
                last.then_inc(s_used, 1)

            def unit_tokens(n, k0, kmax, pb, hi, lo):
                pe.wait_ge(s_lo, n + 1)
                for t in range(NT):
                    for kx in range(UK):
                        k = k0 + kx
                        hk, lk, kk_ = (hi, lo, k) if not isinstance(hi, tuple) else (hi[k // 8], lo[k // 8], k % 8)
                        tok = slice(t * P, (t + 1) * P)
                        last = three_pass(ps[pb + t][:, :], hk[:, kk_, tok], lk[:, kk_, tok], w_hi[:, slot_of(n), kx, :],
                                          w_lo[:, slot_of(n), kx, :], first=(k == 0), last=(k == kmax - 1))
                last.then_inc(s_used, 1)

            def ada_fin(g):
                pe.wait_ge(s_adaused, UPG * (g + 1))
                if g:
                    pe.wait_ge(s_col, g)
                for j in range(4):
                    last = mm(ps[FIN][:, j:j + 1], acc[:, g % 2, j * P:(j + 1) * P], ones[:, 0:1], start=True, stop=True)
                last.then_inc(s_fin, 1)

            pe.wait_ge(s_cst, 16)
            pe.wait_ge(s_rows, 16 * 13)
            for i, (rows, col) in enumerate(((104, 0), (96, V_B), (27, V_MU))):
                last = nc.tensor.transpose(ps[4][:, col:col + rows], vrows[0:rows, i, :], ident[0:rows, 0:rows])
            last.then_inc(s_vt, 1)
            pe.wait_ge(s_xn, NT)
            pe.wait_ge(s_vec, 1)
            for b in range(8):
                for kx in range(2):
                    for t in range(NT):
                        k = 2 * b + kx
                        last = nc.tensor.transpose(ps[b][:, kx * T + t * P:kx * T + (t + 1) * P],
                                                   x_in[:, t, k * P:(k + 1) * P], ident)
                last.then_inc(s_xt, 1)
            pe.wait_ge(s_xnt, 8)

            def rope_perm(gi):
                pe.wait_ge(s_evac, gi + 1)
                if gi == 0:
                    pe.wait_ge(s_cst2, 16)
                    pe.wait_ge(s_xnt, 8)
                else:
                    pe.wait_ge(s_rope, 2 * gi)
                for b in range(2):
                    mm(ps[6 + b][:, :], ck(C_PERM), qraw[:, 2 * b:2 * b + 2, :].rearrange("p k t -> p (k t)"),
                       start=True, stop=True).then_inc(s_perm, 1)

            def attn_slot(i):
                if 2 <= i < HEADS + 2:
                    h = i - 2
                    hp, e = h // 2, h % 2
                    pe.wait_ge(s_ptc, h + 1)
                    if e == 0 and hp:
                        pe.wait_ge(s_mixa, hp)
                    rows = slice(64 * e, 64 * e + 64)
                    vs = slice(HD * h, HD * h + HD)
                    mm(ps[7][rows, 0:P], v_tok[:, 0, vs], prob_t[:, 0, :], start=True, stop=True)
                    mm(ps[7][rows, P:T], v_tok[:, 0, vs], prob_t[:, 1, :], start=True, stop=False)
                    mm(ps[7][rows, P:T], v_tok[:, 1, vs], prob_t[:, 2, :], start=False, stop=True).then_inc(s_o, 1)
                if 1 <= i < HEADS + 1:
                    h = i - 1
                    pe.wait_ge(s_prob, h + 1)
                    if h:
                        pe.wait_ge(s_ptc, h)
                    for j in range(3):
                        last = nc.tensor.transpose(ps[6][:, j * P:(j + 1) * P], prob[:, j, :], ident)
                    last.then_inc(s_pt, 1)
                if i < HEADS:
                    h = i
                    if h == 0:
                        pe.wait_ge(s_rope, 8)
                        pe.wait_ge(s_evac, 6)
                    else:
                        pe.wait_ge(s_masked, h)
                    rows = slice(64 * (h % 2), 64 * (h % 2) + 64)
                    q, k = qk[rows, h // 2, :], qk[rows, 8 + h // 2, :]
                    mm(ps[4][:, 0:P], q[:, 0:P], k[:, 0:P], start=True, stop=True)
                    mm(ps[4][:, P:3 * P], q[:, P:T], k, start=True, stop=True).then_inc(s_score, 1)

            full = (0, P, 2 * P, 3 * P)
            for n in range(FIRST):
                g, ku = first_unit(n)
                if n % 4 == 0:
                    ada_fin(n // 2)
                    ada_fin(n // 2 + 1)
                    pe.wait_ge(s_hlo, n // 4 + 1)
                unit_channels(n, ku, 2 * g, h_hi, h_lo, full)
            half = [slice(0, 64), slice(64, 128)]
            chunk = [slice(0, P), slice(P, T)]
            head_ones = ck(C_BLK)[:, 0:P:HD]

            def s1_pair(hp):
                cols = slice(hp * P, (hp + 1) * P)
                if hp:
                    pe.wait_ge(s_sigs, hp)
                mm(ps[4][:, 0:T], w_di[0:64, cols], lora[0:64, 0, :], start=True, stop=True)
                mm(ps[6][:, 0:T], w_di[64:128, cols], lora[64:128, 0, :], start=True, stop=True).then_inc(s_zw, 1)
                pe.wait_ge(s_sqk, hp + 1)
                for c in range(2):
                    last = mm(ps[7][:, 4 * hp + 2 * c:4 * hp + 2 * c + 2], sq1[:, hp % 2, chunk[c]], head_ones,
                              start=True, stop=True)
                last.then_inc(s_ssq, 1)

            def spread(bank, c0, table, hp):
                for e in range(2):
                    for c in range(2):
                        col = table[:, 4 * hp + 2 * c + e:4 * hp + 2 * c + e + 1].broadcast_to([P, HD])
                        last = mm(ps[bank][half[e], c0 + c * P:c0 + (c + 1) * P], col, ident, start=True, stop=True)
                return last

            def s1_norms(j):
                pe.wait_ge(s_rnc, 1)
                for hp in (2 * j, 2 * j + 1):
                    last = spread(RN_BANKS[j], T * (hp % 2), rnc, hp)
                last.then_inc(s_rnb, 1)

            for pos in range(WIN_G):
                for ku in range(UPG):
                    n = pos * UPG + ku
                    if n < FIRST:
                        continue
                    if pos >= 2 and ku == 0:
                        pe.wait_ge(s_evac, pos - 1)
                    pb = 2 * (pos % 2)
                    if pos in (4, 5):
                        unit_tokens(n, UK * ku, KT, pb, h_hi, h_lo)
                    else:
                        unit_channels(n, ku, pb, h_hi, h_lo, full if pos != 6 else (0, P, LORA_W - P))
                    for done in at_unit(ROPE_AT, n):
                        rope_perm(done)
                    u = n - 6 * UPG - 4
                    if u >= 0 and u % 2 == 0 and u // 2 < HEADS + 2:
                        attn_slot(u // 2)
                    for g in at_unit(FIN_AT, n):
                        ada_fin(g)
                    if n == S1_AT:
                        pe.wait_ge(s_small, 64)
                        pe.wait_ge(s_lora, 2)
                        pe.wait_ge(s_mixa, PAIRS)
                    if 0 <= n - S1_AT < PAIRS:
                        s1_pair(n - S1_AT)
                    if n == S1_AT + PAIRS + LAG:
                        pe.wait_ge(s_sigs, PAIRS)
                        pe.wait_ge(s_rns, 1)
                        for j in range(3):
                            s1_norms(j)
                    if n == S1_AT + PAIRS + LAG + 1:
                        pe.wait_ge(s_evac, WIN_G - 1)
                        s1_norms(3)

            def first_grams(w, i):
                sd = sides[i]
                op, bank = sd.op, sd.bank
                pe.wait_ge(sd.s_op, w + 1)
                if w:
                    pe.wait_ge(sd.s_bonus, w)
                for e in range(2):
                    for c in range(2):
                        mm(ps[bank[e]][:, 2 * c * P:2 * (c + 1) * P], op[half[e], 2, chunk[c]],
                           op[half[e], 0:2, chunk[c]], start=True, stop=True)
                if i:
                    pe.wait_ge(s_pre, 1)
                    pe.wait_ge(s_col, 14 + w)
                elif w:
                    pe.wait_ge(sides[1].s_tvc, w)
                for e in range(2):
                    gb, c0 = (bank[2], 0) if e == 0 else ((7, FIN)[i], T)
                    for c in range(2):
                        last = mm(ps[gb][:, c0 + c * P:c0 + (c + 1) * P], op[half[e], 0, chunk[c]],
                                  op[half[e], 2, chunk[c]], start=True, stop=True)
                last.then_inc(sd.s_gram, 1)

            def key_grams(w, i):
                sd = sides[i]
                pe.wait_ge(sd.s_gramc, 2 * w + 1)
                if i:
                    pe.wait_ge(sides[0].s_tvc, w + 1)
                for e in range(2):
                    for c in range(2):
                        last = mm(ps[(sd.bank[2], 7)[e]][:, 2 * c * P:2 * (c + 1) * P], sd.op[half[e], 3, chunk[c]],
                                  sd.op[half[e], 0:2, chunk[c]], start=True, stop=True)
                last.then_inc(sd.s_krg, 1)

            def level_y(w, i, lev):
                sd = sides[i]
                if lev:
                    pe.wait_ge(sd.s_xm, w * (LEVELS - 1) + lev)
                else:
                    pe.wait_ge(sd.s_gramc, 2 * w + 2)
                for m in range(4):
                    last = mm(ps[sd.bank[0]][:, m * P:(m + 1) * P], sd.br[:, m, 0:P], sd.xm[:, m, :], start=True, stop=True)
                last.then_inc(sd.s_y, 1)

            def level_x(w, i, lev):
                sd, n = sides[i], w * LEVELS + lev
                pe.wait_ge(sd.s_y1, n + 1)
                if lev:
                    pe.wait_ge(sd.s_xt, n)
                if lev < LEVELS - 1:
                    for m in range(4):
                        last = mm(ps[sd.bank[1]][:, m * P:(m + 1) * P], sd.xt[:, m, :], sd.y1[:, lev, m, :],
                                  start=True, stop=True)
                    last.then_inc(sd.s_xx, 1)
                if lev == 0:
                    pe.wait_ge(sd.s_krc, w + 1)
                for m in range(4):
                    last = mm(ps[sd.bank[2]][:, m * P:(m + 1) * P], sd.y1[:, lev, m, :], sd.xt[:, m, :], start=True, stop=True)
                last.then_inc(sd.s_xxt, 1)

            def to_tokens(w, i):
                sd, hp = sides[i], 2 * w + i
                pe.wait_ge(sd.s_krc, w + 1)
                if w == 0:
                    pe.wait_ge(s_shift, 6)
                for j, src in enumerate((sd.op[:, 2, 0:P], sd.op[:, 3, 0:P], rkv[:, 16 + hp, 0:P], rkv[:, 16 + hp, P:T])):
                    last = nc.tensor.transpose(ps[7][:, j * P:(j + 1) * P], src, ident)
                last.then_inc(sd.s_tv, 1)

            def right_sides(w, i, c):
                sd = sides[i]
                if c == 0:
                    pe.wait_ge(sd.s_tvc, w + 1)
                    pe.wait_ge(sd.s_xt, (w + 1) * LEVELS)
                else:
                    pe.wait_ge(sd.s_stc, w + 1)
                for e in range(2):
                    hd = slice(HD * e, HD * (e + 1))
                    last = mm(ps[sd.bank[e]][:, 0:HD], sd.kr[:, 2 * e + c, 0:P], sd.tv[:, 2 + c, hd], start=True, stop=(c == 0))
                    if c:
                        last = mm(ps[sd.bank[e]][:, 0:HD], sd.op[half[e], 0, chunk[1]], sd.s0[half[e], :], start=False,
                                  stop=True)
                last.then_inc(sd.s_u, 1)

            def solve(w, i, c):
                sd = sides[i]
                pe.wait_ge(sd.s_uc, 2 * w + c + 1)
                for e in range(2):
                    last = mm(ps[sd.bank[2]][:, e * HD:(e + 1) * HD], sd.xt[:, 2 * e + c, :], sd.us[:, e, :],
                              start=True, stop=True)
                last.then_inc(sd.s_sa, 1)

            def state(w, i):
                sd = sides[i]
                pe.wait_ge(sd.s_sac, 2 * w + 1)
                for e in range(2):
                    hd = slice(HD * e, HD * (e + 1))
                    out = ps[sd.bank[2]][half[e], 2 * HD:3 * HD]
                    mm(out, sd.tv[:, 0, hd], sd.sa[:, 0, e, :], start=True, stop=False)
                    last = mm(out, sd.tv[:, 1, hd], sd.tv[:, 2, hd], start=False, stop=True)
                last.then_inc(sd.s_st, 1)

            def outputs(w, i):
                sd = sides[i]
                pe.wait_ge(sd.s_sac, 2 * w + 2)
                for e in range(2):
                    hd = slice(HD * e, HD * (e + 1))
                    for c in range(2):
                        m = 2 * e + c
                        out = ps[sd.bank[e]][half[e], c * P:(c + 1) * P]
                        mm(out, sd.sa[:, c, e, :], sd.br[:, m, P:2 * P], start=True, stop=False)
                        last = mm(out, sd.tv[:, 2 + c, hd], sd.kr[:, m, P:2 * P], start=False, stop=(c == 0))
                        if c:
                            last = mm(out, sd.s0[half[e], :], sd.op[half[e], 1, chunk[1]], start=False, stop=True)
                last.then_inc(sd.s_ot, 1)

            def means(w, i):
                sd = sides[i]
                pe.wait_ge(sd.s_otc, w + 1)
                mm(ps[sd.bank[2]][:, 0:T], ck(C_BLK), sd.o_t[:], start=True, stop=True).then_inc(sd.s_mean, 1)

            def variances(w, i):
                sd, hp = sides[i], 2 * w + i
                pe.wait_ge(sd.s_bon, w + 1)
                mm(ps[sd.bank[1]][:, 0:T], ck(C_BLK), rkv[:, hp, :], start=True, stop=True)
                pe.wait_ge(sd.s_dsq, w + 1)
                for c in range(2):
                    last = mm(ps[sd.bank[0]][:, 2 * c:2 * c + 2], sd.sq[:, chunk[c]], head_ones, start=True, stop=True)
                last.then_inc(sd.s_var, 1)

            pe.wait_ge(s_evac, WIN_G)
            def finish(hp):
                cols = slice(hp * P, (hp + 1) * P)
                b = FINISH_BANKS[hp]
                if 3 <= hp < PAIRS - 1:
                    pe.wait_ge(s_mixf, hp - 2)
                elif hp == PAIRS - 1:
                    pe.wait_ge(sides[1].s_bonus, WAVES)
                mm(ps[b][:, T:2 * T], w_g[:, cols], lora[:, 1, :], start=True, stop=False)
                mm(ps[b][:, T:2 * T], w_g2[96:128, cols], lora[96:128, 2, :], start=False, stop=True)
                pe.wait_ge(s_rstd, 1 if hp < PAIRS - 1 else 2)
                spread(b, 0, varc, hp).then_inc(s_g, 1)

            for slot, w, i, step, nth in turns_of:
                if slot == SIDE0_END:
                    pe.wait_ge(sides[0].s_bonus, WAVES)
                if 0 < slot - SIDE0_END < PAIRS:
                    finish(slot - SIDE0_END - 1)
                if step == "gram":
                    first_grams(w, i)
                elif step == "y":
                    level_y(w, i, nth)
                elif step == "x":
                    level_x(w, i, nth)
                elif step == "keys":
                    key_grams(w, i)
                elif step == "tokens":
                    to_tokens(w, i)
                elif step == "u":
                    right_sides(w, i, nth)
                elif step == "solve":
                    solve(w, i, nth)
                elif step == "state":
                    state(w, i)
                elif step == "out":
                    outputs(w, i)
                elif step == "mean":
                    means(w, i)
                elif step == "var":
                    variances(w, i)
                if slot in FIN_SLOT and i == 1:
                    fw = FIN_SLOT.index(slot)
                    pe.wait_ge(sides[1].s_gramc, 2 * fw + 2)
                    ada_fin(14 + fw)
            finish(PAIRS - 1)

            def gate_rows(i, src):
                pe.wait_ge(s_diag, i + 1)
                if i:
                    pe.wait_ge(s_gtb, i)
                mm(ps[4][:, :], ones, src[:], start=True, stop=True).then_inc(s_gt, 1)

            for g in range(OUT_G):
                for ku in range(UPG):
                    n = N_OUT0 + g * UPG + ku
                    if g == 0 and ku == 0:
                        pe.wait_ge(s_mixf, PAIRS - 1)
                    if g == 0 and ku == UPG // 2:
                        pe.wait_ge(s_mixr, PAIRS)
                    if g >= 2 and ku == 0:
                        pe.wait_ge(s_x1, 2 * (g - 1))
                    unit_tokens(n, UK * ku, KT, 2 * (g % 2), (mixa_hi, mixr_hi), (mixa_lo, mixr_lo))
                    if ku == 3:
                        gate_rows(g, diag)
                    if g * UPG + ku == 5:
                        ada_fin(18)
                    if g * UPG + ku == 15:
                        ada_fin(19)
            pe.wait_ge(s_xn2, NT)
            pe.wait_ge(s_gtb, OUT_G)
            pe.wait_ge(s_col, END_ADA1 // UPG)
            for b in range(8):
                if b >= 6:
                    pe.wait_ge(s_h2f, (b - 6) // 2 + 1)
                for kx in range(2):
                    for t in range(NT):
                        k = 2 * b + kx
                        last = mm(ps[X2T_BANKS[b]][:, kx * T + t * P:kx * T + (t + 1) * P], x1[:, t, k * P:(k + 1) * P],
                                  rsd[:, t, :], start=True, stop=True)
                last.then_inc(s_x2t, 1)

            def gu_group(g, parity, first=False):
                if not isinstance(g, int) or g >= 2:
                    pe.wait_ge(s_prod, g - 1)
                for m in range(2):
                    for ku in range(UPG):
                        if first and m == 0 and ku % 2 == 0:
                            pe.wait_ge(s_h2lo, ku // 2 + 1)
                        pe.wait_ge(s_lo, g * (2 * UPG) + (N_GU0 + m * UPG + ku + 1))
                        for i in range(4):
                            for kx in range(UK):
                                k = UK * ku + kx
                                out = ps[4 * parity + 2 * m + i // 2][:, (i % 2) * T:(i % 2 + 1) * T]
                                w = slice(i * P, (i + 1) * P)
                                last = three_pass(out, w_hi[:, ku % RING, kx, w], w_lo[:, ku % RING, kx, w],
                                                  h_hi[:, k, :], h_lo[:, k, :], first=(k == 0 and i % 2 == 0),
                                                  last=(k == KT - 1), shared=True)
                        last.then_inc(s_used, 1)

            gu_group(0, 0, first=True)
            gu_group(1, 1)
            gu_group(2, 0)
            with pe.Fori(1, (GU_G - 1) // 2) as it:
                gu_group(it * 2 + 1, 1)
                gu_group(it * 2 + 2, 0)

            pe.wait_ge(s_prod, GU_G)
            for g in range(OUT_G):
                for ku in range(DOWN_U):
                    n = N_DOWN0 + g * DOWN_U + ku
                    if g >= 2 and ku == 0:
                        pe.wait_ge(s_x1, 2 * OUT_G + 2 * (g - 1))
                    if g == 0 and ku % 2 == 0:
                        pe.wait_ge(s_alo, ku // 2 + 1)
                    unit_tokens(n, UK * ku, FK, 2 * (g % 2), act_hi, act_lo)
                    if ku == DOWN_U - 5:
                        ada_fin(20 + g)
                    if ku == DOWN_U - 2:
                        gate_rows(OUT_G + g, diag2)


_INS = ["x", "c", "positions", "w_ada", "b_ada", "norm1_g", "norm2_g", "normf_g", "w_in", "w_out", "mu_shift", "w0",
        "w_decay_up", "a0", "w_iclr_up", "w_gate_up", "k_k", "k_a", "r_k", "gn_g", "gn_b", "w_ffn_gate", "w_ffn_up",
        "w_ffn_down"]


def kernel(**inputs):
    import concourse.bacc as bacc
    from concourse.bass_utils import run_bass_kernel_spmd as run

    nc = bacc.Bacc("TRN2", target_bir_lowering=False, num_devices=1)
    arrays, aps = {}, {}
    for name in _INS:
        x = np.ascontiguousarray(inputs[name])
        arrays[f"in_{name}"] = x
        aps[name] = nc.dram_tensor(f"in_{name}", x.shape, mybir.dt.from_np(x.dtype), kind="ExternalInput").ap()
    arrays["in_const"] = constants()
    aps["const"] = nc.dram_tensor("in_const", (P, NCONST), F32, kind="ExternalInput").ap()
    aps["out"] = nc.dram_tensor("out_0", (1, T, D), F32, kind="ExternalOutput").ap()
    build(nc, aps)
    r = run(nc, [arrays], core_ids=[0])
    return r.results[0]["out_0"]
```
